# Optimizing a Trainium2 kernel written in Bass

```python
import jax, jax.numpy as jnp
from jax import lax
import numpy as np

D_MODEL = 1024
BATCH = 1
SEQ = 2048
DEPTH = 1
DEC_BATCH = 1
DEC_SEQ = 64
PAST_LEN = 128

CHUNK = 64
CONV_CH = 512
CONV_WIDTH = 31
N_HEADS = 8
HEAD_DIM = 64
ATTN_W = N_HEADS * HEAD_DIM
MIX_W = CONV_CH + ATTN_W
IN_COLS = 2 * CONV_CH + 3 * ATTN_W
D_FF = 4 * D_MODEL
Q_BLOCK = 128
EPS = 1e-6

kernel_name = "hymba_conformer_stickbreaking_stream_step"

def _rmsnorm(x, g):
    xf = x.astype(jnp.float32)
    y = xf * lax.rsqrt(jnp.mean(xf * xf, axis=-1, keepdims=True) + EPS)
    return (y * g.astype(jnp.float32)).astype(x.dtype)

def _layernorm(x, g, b):
    xf = x.astype(jnp.float32)
    mu = jnp.mean(xf, axis=-1, keepdims=True)
    xc = xf - mu
    y = xc * lax.rsqrt(jnp.mean(xc * xc, axis=-1, keepdims=True) + EPS)
    return (y * g.astype(jnp.float32) + b.astype(jnp.float32)).astype(x.dtype)

def _causal_dwconv(u_ext, w):
    c = w.shape[-1]
    return lax.conv_general_dilated(
        u_ext, w.reshape(CONV_WIDTH, 1, c).astype(u_ext.dtype),
        window_strides=(1,), padding='VALID',
        dimension_numbers=('NWC', 'WIO', 'NWC'), feature_group_count=c)

def _sb_block(qb, qpos, k, v, kpos):
    scale = HEAD_DIM ** -0.5
    z = jnp.einsum('bqhd,bkhd->bhqk', qb.astype(jnp.float32), k.astype(jnp.float32)) * scale
    mask = kpos[None, :] < qpos[:, None]
    log_1m_beta = jnp.where(mask, jax.nn.log_sigmoid(-z), 0.0)
    between = lax.cumsum(log_1m_beta, axis=3, reverse=True) - log_1m_beta
    a = jnp.where(mask, jnp.exp(jax.nn.log_sigmoid(z) + between), 0.0)
    return jnp.einsum('bhqk,bkhd->bqhd', a, v.astype(jnp.float32)).astype(v.dtype)

def _stick_breaking(q, k, v, q_pos, k_pos):
    b, t, h, d = q.shape
    blk = Q_BLOCK if t % Q_BLOCK == 0 else t
    nblk = t // blk
    qb = q.reshape(b, nblk, blk, h, d).transpose(1, 0, 2, 3, 4)
    pb = q_pos.reshape(nblk, blk)
    out = lax.map(lambda args: _sb_block(args[0], args[1], k, v, k_pos), (qb, pb))
    return out.transpose(1, 0, 2, 3, 4).reshape(b, t, h, d)

def _layer(x, past_conv, past_k, past_v, g_mix, w_in, w_dw, b_dw, g_cn, b_cn, w_pw,
           g_q, g_k, w_out, g_ff, w_ff1, w_ff2):
    b, t, _ = x.shape
    n_past = past_k.shape[1]
    h = _rmsnorm(x, g_mix)
    proj = h @ w_in
    a, gate, q, k, v = jnp.split(
        proj, [CONV_CH, 2 * CONV_CH, 2 * CONV_CH + ATTN_W, 2 * CONV_CH + 2 * ATTN_W], axis=-1)
    u = a * jax.nn.sigmoid(gate)
    u_ext = jnp.concatenate([past_conv.astype(u.dtype), u], axis=1)
    c = _causal_dwconv(u_ext, w_dw) + b_dw
    c = jax.nn.silu(_layernorm(c, g_cn, b_cn)) @ w_pw
    new_conv = u_ext[:, u_ext.shape[1] - (CONV_WIDTH - 1):]
    q = _rmsnorm(q.reshape(b, t, N_HEADS, HEAD_DIM), g_q)
    k = _rmsnorm(k.reshape(b, t, N_HEADS, HEAD_DIM), g_k)
    v = v.reshape(b, t, N_HEADS, HEAD_DIM)
    k_all = jnp.concatenate([past_k.astype(k.dtype), k], axis=1)
    v_all = jnp.concatenate([past_v.astype(v.dtype), v], axis=1)
    k_pos = jnp.arange(n_past + t, dtype=jnp.int32)
    q_pos = n_past + jnp.arange(t, dtype=jnp.int32)
    o = _stick_breaking(q, k_all, v_all, q_pos, k_pos)
    x = x + jnp.concatenate([c, o.reshape(b, t, ATTN_W)], axis=-1) @ w_out
    f = jax.nn.relu(_rmsnorm(x, g_ff) @ w_ff1)
    x = x + (f * f) @ w_ff2
    return x, k, v, new_conv

def setup_inputs(seed: int = 0) -> dict:
    key = jax.random.key(seed)
    ks = jax.random.split(key, 20)
    f32 = jnp.float32

    def nrm(k, shape, scale):
        return jax.random.normal(k, shape, f32) * scale

    return {
        "x_prompt": nrm(ks[0], (BATCH, SEQ, D_MODEL), 1.0),
        "x_sample": nrm(ks[1], (DEC_BATCH, DEC_SEQ, D_MODEL), 1.0),
        "cache_k": nrm(ks[2], (DEPTH, DEC_BATCH, PAST_LEN, N_HEADS, HEAD_DIM), 1.0),
        "cache_v": nrm(ks[3], (DEPTH, DEC_BATCH, PAST_LEN, N_HEADS, HEAD_DIM), 1.0),
        "state_conv": nrm(ks[4], (DEPTH, DEC_BATCH, CONV_WIDTH - 1, CONV_CH), 0.5),
        "g_mix": 1.0 + nrm(ks[5], (DEPTH, D_MODEL), 0.02),
        "w_in": nrm(ks[6], (DEPTH, D_MODEL, IN_COLS), D_MODEL ** -0.5),
        "w_dw": nrm(ks[7], (DEPTH, CONV_WIDTH, CONV_CH), CONV_WIDTH ** -0.5),
        "b_dw": nrm(ks[8], (DEPTH, CONV_CH), 0.02),
        "g_cn": 1.0 + nrm(ks[9], (DEPTH, CONV_CH), 0.02),
        "b_cn": nrm(ks[10], (DEPTH, CONV_CH), 0.02),
        "w_pw": nrm(ks[11], (DEPTH, CONV_CH, CONV_CH), CONV_CH ** -0.5),
        "g_q": 1.0 + nrm(ks[12], (DEPTH, HEAD_DIM), 0.02),
        "g_k": 1.0 + nrm(ks[13], (DEPTH, HEAD_DIM), 0.02),
        "w_out": nrm(ks[14], (DEPTH, MIX_W, D_MODEL), MIX_W ** -0.5),
        "g_ff": 1.0 + nrm(ks[15], (DEPTH, D_MODEL), 0.02),
        "w_ff1": nrm(ks[16], (DEPTH, D_MODEL, D_FF), D_MODEL ** -0.5),
        "w_ff2": nrm(ks[17], (DEPTH, D_FF, D_MODEL), D_FF ** -0.5),
    }

def reference(x_prompt, x_sample, cache_k, cache_v, state_conv, g_mix, w_in, w_dw, b_dw,
              g_cn, b_cn, w_pw, g_q, g_k, w_out, g_ff, w_ff1, w_ff2):
    assert x_sample.shape[1] <= CHUNK
    bp = x_prompt.shape[0]
    hp = x_prompt
    hs = x_sample
    kp, vp, cp, ksl, vsl, csl = [], [], [], [], [], []
    empty_kv = jnp.zeros((bp, 0, N_HEADS, HEAD_DIM), x_prompt.dtype)
    zero_conv = jnp.zeros((bp, CONV_WIDTH - 1, CONV_CH), x_prompt.dtype)
    for l in range(DEPTH):
        w = (g_mix[l], w_in[l], w_dw[l], b_dw[l], g_cn[l], b_cn[l], w_pw[l],
             g_q[l], g_k[l], w_out[l], g_ff[l], w_ff1[l], w_ff2[l])
        hp, k_new, v_new, conv_new = _layer(hp, zero_conv, empty_kv, empty_kv, *w)
        kp.append(k_new); vp.append(v_new); cp.append(conv_new)
        hs, k_new, v_new, conv_new = _layer(hs, state_conv[l], cache_k[l], cache_v[l], *w)
        ksl.append(k_new); vsl.append(v_new); csl.append(conv_new)
    return (hp, hs, jnp.stack(kp), jnp.stack(vp), jnp.stack(cp),
            jnp.stack(ksl), jnp.stack(vsl), jnp.stack(csl))


_drawn_inputs = setup_inputs


def setup_inputs(seed=0):
    import zlib

    import numpy as np

    out = dict(_drawn_inputs(seed))
    spreads = {}
    factors = {'b_dw': 3.84, 'g_cn': 6.157, 'b_cn': 6.816, 'g_q': 37.504, 'g_k': 7.89, 'g_ff': 3.448}
    for name, (base, spread) in spreads.items():
        noise = np.random.default_rng([zlib.crc32(name.encode()), seed]).standard_normal(out[name].shape)
        drawn = base * np.exp(spread * noise) if base else spread * noise
        out[name] = __import__('jax').numpy.asarray(drawn.astype(out[name].dtype))
    for name, factor in factors.items():
        out[name] = (out[name] * factor).astype(out[name].dtype)
    return out
```

```python
import concourse.bass as bass
from concourse import mybir
from contextlib import ExitStack

F32 = mybir.dt.float32
F32R = mybir.dt.float32r
ALU = mybir.AluOpType
ACT = mybir.ActivationFunctionType
AX = mybir.AxisListType

P = 128
D = 1024
KD = D // P
SEQ, DEC, PAST = 2048, 64, 128
NH, HD = 8, 64
AW = NH * HD
CC, CW = 512, 31
CB = CC // P
HIST = CW - 1
FF = 4096
EPS = 1e-6
BANK = 512
CHUNK = 512
NC = SEQ // CHUNK
TMAX = CHUNK + DEC
SLAB = 1024
RAW = 4
RING = 8
GROUPS = 24
G_AG, G_K, G_V, G_Q, G_PW, G_OUT, G_FF = 0, 2, 3, 4, 5, 6, 8
FFE = FF // P // 4
SMP = CHUNK + HIST
CVW = SMP + DEC
ACT_TABLE_LN_EXP = 6


def tiles(c):
    t = [(P * i, P) for i in range(CHUNK // P)]
    return t + [(CHUNK, DEC)] if c == NC - 1 else t


def splits(c):
    return [(0, TMAX // 2), (TMAX // 2, TMAX // 2)] if c == NC - 1 else [(0, CHUNK)]


def conv_pieces(c):
    return [(0, 0, CHUNK)] + ([(SMP, CHUNK, DEC)] if c == NC - 1 else [])


def passes(c):
    prompt = [[(P * i, P, CHUNK * c + P * (i + 1)) for i in (2 * p, 2 * p + 1)] for p in range(2)]
    out = [(0, prompt)]
    if c == NC - 1:
        out.append((1, [[(0, DEC, PAST + DEC)]]))
    return out


def pieces(pairs):
    out = []
    for p, pair in enumerate(pairs):
        for t, (q0, r, n) in enumerate(pair):
            cut = [(SLAB, n)] if n > SLAB else []
            cut.append((0, min(n, SLAB)))
            for k, (a, b) in enumerate(cut):
                out.append((p, t, q0, r, a, b - a, k == 0, k == len(cut) - 1))
    return out


def key_groups(a, n):
    blocks = [((a + x) // P, min(P, n - x)) for x in range(0, n, P)]
    return [blocks[x:x + 4] for x in range(0, len(blocks), 4)]


def build(nc, x_prompt, x_sample, cache_k, cache_v, state_conv, g_mix, w_in, w_dw, b_dw, g_cn, b_cn, w_pw,
          g_q, g_k, w_out, g_ff, w_ff1, w_ff2, y_prompt, y_sample, nk_prompt, nv_prompt, ncv_prompt,
          nk_sample, nv_sample, ncv_sample):
    ctx = ExitStack()
    with ctx:
        base = (nc.sbuf_base + 31) // 32 * 32
        at = [base]

        def place(name, shape, dt=F32, offset=None):
            n = 4
            for s in shape[1:]:
                n *= s
            if offset is None:
                offset = at[0]
                at[0] += (n + 31) // 32 * 32
            return nc.alloc_sbuf_tensor_at(name, shape, dt, offset=offset)

        o_w = at[0]
        half = 2 * 4 * SLAB * 4
        at[0] += 2 * half
        w_hi = [place(f"w_hi{g}", [P, 4, SLAB], F32R, o_w + g * half) for g in range(2)]
        w_lo = [place(f"w_lo{g}", [P, 4, SLAB], F32R, o_w + g * half + half // 2) for g in range(2)]
        w_raw = place("w_raw", [P, RAW, SLAB])
        resid = place("resid", [P, 5, D])
        o_h = at[0]
        hT_hi = place("hT_hi", [P, KD, TMAX], F32R)
        hT_lo = place("hT_lo", [P, KD, TMAX], F32R)
        o_mix = at[0]
        mixT_hi = place("mixT_hi", [P, KD, TMAX], F32R)
        mixT_lo = place("mixT_lo", [P, KD, TMAX], F32R)
        uT = place("uT", [P, CB, SMP + HIST + DEC])
        o_cv = at[0]
        cacc = place("cacc", [P, CB, CVW])
        cT_lo = place("cT_lo", [P, CB, CVW], F32R, o_cv)
        o_ch = at[0]
        cT_hi = place("cT_hi", [P, CB, CVW], F32R)
        g_row = place("g_row", [P, D])
        vecs = place("vecs", [P, CB, CW + 3])
        gq = place("gq", [P, HD])
        gk = place("gk", [P, HD])
        ident = place("ident", [P, P])
        ones = place("ones", [P, P])
        neghalf = place("neghalf", [P, 1])
        ssum = place("ssum", [P, 5])
        rstd = place("rstd", [P, 5])
        hss = place("hss", [P, 2, NH])
        hrs = place("hrs", [P, 2, NH])
        carry = place("carry", [P, 1])
        past = place("past", [P, P])
        xn = place("xn", [P, 2, D], offset=o_cv)
        kqT = place("kqT", [P, NH, TMAX], F32R, o_mix)
        o_t = o_mix + NH * TMAX * 4
        raw_kq = place("raw_kq", [P, 2, AW], offset=o_t)
        sqr = place("sqr", [P, AW], offset=o_t + 4096)
        kn = place("kn", [P, 2, AW], offset=o_t + 6144)
        packed = place("packed", [P, 2, NH, P], F32R, o_t + 10240)
        vout = place("vout", [P, 2, AW], offset=o_ch)
        vpack_o = o_ch + 4096
        vpack = place("vpack", [P, NH, P], F32R, vpack_o)
        sgate = place("sgate", [P, 2, BANK], offset=o_t)
        csq = place("csq", [P, CB, CVW], offset=o_ch)
        lnv = place("lnv", [P, BANK], offset=o_t)
        lnr = place("lnr", [P, BANK], offset=o_t + 2048)
        csig = place("csig", [P, 2, BANK], offset=o_t + 4096)
        cid = place("cid", [P, 2, BANK], offset=o_t + 8192)
        cvout = place("cvout", [HIST, 2, CC], offset=o_t + 12288)
        hid_hi = place("hid_hi", [P, 4, TMAX], F32R, o_cv)
        hid_lo = place("hid_lo", [P, 4, TMAX], F32R, o_cv + 4 * TMAX * 4)
        frel = place("frel", [P, 2, BANK], offset=o_mix)
        fsq = place("fsq", [P, 2, BANK], offset=o_mix + 4096)
        KB, VB, QB = SEQ * 4, (SEQ // P) * P * 4, 2 * CHUNK * 4
        a_k = [place(f"a_k{b}", [P, SEQ], F32R, o_h + b * KB) for b in range(2)]
        a_v = [place(f"a_v{b}", [P, SEQ // P, P], F32R, o_h + 2 * KB + b * VB) for b in range(2)]
        a_q = [place("a_q0", [P, 2, CHUNK], F32R, o_h + 2 * KB + 2 * VB),
               place("a_q1", [P, 2, CHUNK], F32R, o_cv + 3 * SLAB * 4)]
        sc = [place(f"sc{i}", [P, SLAB], F32, o_cv + i * SLAB * 4) for i in range(3)]
        aT_hi = place("aT_hi", [P, SEQ // P, 2 * P], F32R, o_w + half)
        aT_lo = place("aT_lo", [P, SEQ // P, 2 * P], F32R, o_w + half + half // 2)
        osb = place("osb", [P, 2 * P], offset=o_cv + 4 * SLAB * 4)
        of = place("of", [P, 2 * P], offset=o_cv + 4 * SLAB * 4 + 1024)
        crow = place("crow", [CW + 3, CC], offset=o_t)
        srow = place("srow", [HIST, CC], offset=o_t + 2048)

        ps = ctx.enter_context(nc.psum_tensor("ps", [P, 8, BANK], F32))

        k_d = nc.dram_tensor("k_scratch", [NH, P, SEQ], F32).ap()
        v_d = nc.dram_tensor("v_scratch", [NH, P, SEQ // P, P], F32).ap()
        q_d = nc.dram_tensor("q_scratch", [NH, P, SEQ + DEC], F32).ap()
        ks_d = nc.dram_tensor("ks_scratch", [NH, P, PAST + DEC], F32).ap()
        vs_d = nc.dram_tensor("vs_scratch", [NH, P, 2, P], F32).ap()

        def sem(name):
            return ctx.enter_context(nc.semaphore(name))

        raw_in = [sem(f"raw_in{j}") for j in range(RAW)]
        hi_done, lo_done = sem("hi_done"), sem("lo_done")
        consts, rows_in, vec_t, vec_ok, ch_start, gains_in = (sem(n) for n in (
            "consts", "rows_in", "vec_t", "vec_ok", "ch_start", "gains_in"))
        ck_in, cv_in, ck_hi, ck_lo, cv_hi, cv_lo, ckT_ps, ckT_ok, cache_out = (sem(n) for n in (
            "ck_in", "cv_in", "ck_hi", "ck_lo", "cv_hi", "cv_lo", "ckT_ps", "ckT_ok", "cache_out"))
        x_in = [sem(f"x_in{i}") for i in range(5)]
        grow_in, n_ss, n_var, n_rstd, n_xn, n_tp, n_hi, n_lo = (sem(n) for n in (
            "grow_in", "n_ss", "n_var", "n_rstd", "n_xn", "n_tp", "n_hi", "n_lo"))
        ag_ps, ag_sig, ag_u, hist_ok, taps = (sem(n) for n in ("ag_ps", "ag_sig", "ag_u", "hist_ok", "taps"))
        kvq_ps, kvq_cp, kq_sq, kq_ss, kq_var, kq_rs, kq_mul, kq_n, pk_hi, pk_lo, v_lo, kqT_ps, kqT_ok = (sem(n) for n in (
            "kvq_ps", "kvq_cp", "kq_sq", "kq_ss", "kq_var", "kq_rs", "kq_mul", "kq_n", "pk_hi", "pk_lo", "v_lo",
            "kqT_ps", "kqT_ok"))
        kn_out = [sem(f"kn_out{i}") for i in range(2)]
        vo_out = [sem(f"vo_out{i}") for i in range(2)]
        vp_out, kT_out, qT_out = sem("vp_out"), sem("kT_out"), sem("qT_out")
        mean_ps, xc_ok, sq_ok, var_ps, var_ok, lnr_ok, yn_ok, sg_ok, cm_ok, c_hi, c_lo, cvo_ps, cvo_ok, cvo_out = (
            sem(n) for n in ("mean_ps", "xc_ok", "sq_ok", "var_ps", "var_ok", "lnr_ok", "yn_ok", "sg_ok", "cm_ok",
                             "c_hi", "c_lo", "cvo_ps", "cvo_ok", "cvo_out"))
        pw_ps, pw_hi, pw_lo, out_ps, out_add = (sem(n) for n in ("pw_ps", "pw_hi", "pw_lo", "out_ps", "out_add"))
        at_in = [sem(f"at_in{b}") for b in range(2)]
        z_ps, z_msk, z_abs, s_exp, s_ln, s_lnm, s_p, s_fin, s_edge, s_scan, s_a, s_am, t_ps, t_hi, t_lo, o_ps, o_cp, o_sum, o_hi, o_lo = (
            sem(n) for n in ("z_ps", "z_msk", "z_abs", "s_exp", "s_ln", "s_lnm", "s_p", "s_fin", "s_edge", "s_scan", "s_a",
                             "s_am", "t_ps", "t_hi", "t_lo", "o_ps", "o_cp", "o_sum", "o_hi", "o_lo"))
        f1_ps, f_rel, f_sq, f_hi, f_lo, f2_ps, f2_add = (sem(n) for n in (
            "f1_ps", "f_rel", "f_sq", "f_hi", "f_lo", "f2_ps", "f2_add"))
        y_out = [sem(f"y_out{i}") for i in range(5)]

        def norm_base(c, which):
            return 2 * 4 * c + which * len(tiles(c))

        def att_counts(c, kind):
            before = dict(z=0, m=0, x=0, t=0, o=0)
            for cc in range(NC):
                for k, pairs in passes(cc):
                    pc = pieces(pairs) * 2
                    n = dict(z=len(pc), m=sum(p[6] for p in pc), x=sum(not p[7] for p in pc),
                             t=sum(len(key_groups(p[4], p[5])) for p in pc), o=2 * len(pairs))
                    if (cc, k) == (c, kind):
                        return before, n
                    for key in before:
                        before[key] += n[key] * NH // 2
            return before, None

        def att_sequence(pairs):
            seq, m, t = [], 0, 0
            for head in range(2):
                for pc in pieces(pairs):
                    seq.append((head, pc, m, t))
                    m += pc[6]
                    t += len(key_groups(pc[4], pc[5]))
            return seq

        def kvq_events(c):
            nt = len(tiles(c))
            return ([("k", i, i) for i in range(nt)] + [("v", i, None) for i in range(nt)]
                    + [("q", i, nt + i) for i in range(nt)])

        TAPS = CB * CW

        def taps_of(c, e):
            n = len(kvq_events(c))
            return range(TAPS * e // n, TAPS * (e + 1) // n)

        def evacuate(copy, sub, dst, grp, t, r, bank, done):
            w0 = grp[0][1]
            b0, n = grp[0][0], len(grp)
            same = [x for x in grp if x[1] == w0]
            parts = [(b0, len(same), w0, 0)]
            if len(same) < n:
                parts.append((b0 + len(same), 1, grp[-1][1], len(same)))
            for q, (b, m, w, k0) in enumerate(parts):
                o = dst[0:w, b:b + m, t * P:t * P + r]
                i = bank[0:w, k0 * r:(k0 + m) * r].rearrange("p (a b) -> p a b", a=m)
                ins = copy(o, i) if sub is None else copy(o, i, sub[0:w, b:b + m, t * P:t * P + r].bitcast(F32), ALU.subtract)
                if q == len(parts) - 1:
                    ins.then_inc(done, 1)

        def bank(k, r, x0, x1):
            return ps[0:r, 2 * (k % 2):2 * (k % 2) + 2, :].rearrange("p a b -> p (a b)")[:, x0:x1]

        block = ctx.enter_context(nc.Block())

        def att_outputs(c):
            before, n = att_counts(c, passes(c)[-1][0])
            return before["o"] + n["o"] * NH // 2

        @block.sync
        def _(sp):
            def load_slab(slab, src, width=None):
                j = slab % RAW
                if not isinstance(slab, int) or slab >= RAW:
                    sp.wait_ge(lo_done, slab - RAW + 1)
                dst = w_raw[:, j, :] if width is None else w_raw[:, j, 0:width]
                if len(src.shape) == 3:
                    dst = dst.rearrange("p (a b) -> p a b", a=src.shape[1])
                sp.dma_start(dst, src).then_inc(raw_in[j], 16)

            w_in_k = w_in[0].rearrange("(k p) n -> p k n", p=P)
            w_out_k = w_out[0].rearrange("(k p) n -> p k n", p=P)
            w_pw_k = w_pw[0].rearrange("(k p) n -> p k n", p=P)
            w1_k = w_ff1[0].rearrange("(k p) n -> p k n", p=P)
            w2_k = w_ff2[0].rearrange("(k p) n -> p k n", p=P)

            def load_group(c, g):
                if c >= NC:
                    return
                for j in range(4):
                    slab = 4 * (GROUPS * c + g) + j
                    if g < G_K:
                        col = (j % 2) * CC + (2 * g + j // 2) * P
                        src = w_in_k[:, :, col:col + P]
                    elif g <= G_Q:
                        col = 2 * CC + {G_K: 1, G_V: 2, G_Q: 0}[g] * AW
                        src = w_in_k[:, 2 * j:2 * j + 2, col:col + AW]
                    elif g == G_PW:
                        src = w_pw_k[:, j, :]
                    elif g < G_FF:
                        hf = g - G_OUT
                        src = w_out_k[:, 2 * j:2 * j + 2, hf * BANK:(hf + 1) * BANK]
                    load_slab(slab, src, CC if g == G_PW else None)

            def load_ff1(c, e):
                for j in range(4):
                    col = 4 * e + j
                    sl = bass.ts(col, P)
                    n = 4 * (GROUPS * c + G_FF) + 8 * e + j
                    sp.wait_ge(lo_done, n - RAW + 1)
                    sp.dma_start(w_raw[:, j, :].rearrange("p (a b) -> p a b", a=KD),
                                 w1_k[:, :, sl]).then_inc(raw_in[j], 16)

            def load_ff2(c, e):
                for j in range(4):
                    n = 4 * (GROUPS * c + G_FF + 1) + 8 * e + j
                    sp.wait_ge(lo_done, n - RAW + 1)
                    sp.dma_start(w_raw[:, j, :], w2_k[:, 4 * e + j, :]).then_inc(raw_in[j], 16)

            def load_gain(c, which):
                g = (g_mix if which == 0 else g_ff)[0:1, :]
                if c or which:
                    sp.wait_ge(n_xn, norm_base(c, which))
                sp.dma_start(g_row[:], g.partition_broadcast(P)[:, 0, :]).then_inc(grow_in, 16)

            sp.dma_start(crow[0:CW, :], w_dw[0]).then_inc(rows_in, 16)
            sp.dma_start(crow[CW:CW + 1, :], b_dw[0:1, :]).then_inc(rows_in, 16)
            sp.dma_start(crow[CW + 1:CW + 2, :], g_cn[0:1, :]).then_inc(rows_in, 16)
            sp.dma_start(crow[CW + 2:CW + 3, :], b_cn[0:1, :]).then_inc(rows_in, 16)
            sp.dma_start(srow[:], state_conv[0, 0]).then_inc(rows_in, 16)
            sp.dma_start(gq[:], g_q[0:1, :].partition_broadcast(P)[:, 0, :]).then_inc(gains_in, 16)
            sp.dma_start(gk[:], g_k[0:1, :].partition_broadcast(P)[:, 0, :]).then_inc(gains_in, 16)
            sp.dma_start(kn[:, 0, :], cache_k[0, 0].rearrange("t h d -> t (h d)")).then_inc(ck_in, 16)
            sp.dma_start(vout[:, 0, :], cache_v[0, 0].rearrange("t h d -> t (h d)")).then_inc(cv_in, 16)
            for c in range(NC):
                tl = tiles(c)
                nt = len(tl)
                t0 = c * CHUNK
                for i, (q0, r) in enumerate(tl):
                    if c and i < 4:
                        sp.wait_ge(y_out[i], 16 * c)
                    src = x_prompt[0, t0 + q0:t0 + q0 + r, :] if i < 4 else x_sample[0]
                    sp.dma_start(resid[0:r, i, :], src).then_inc(x_in[i], 16)
                load_gain(c, 0)
                if c == 0:
                    load_group(0, 0)
                    load_group(0, 1)
                    sp.wait_ge(ckT_ok, 2)
                    sp.dma_start(ks_d[:, :, 0:PAST].rearrange("h p k -> p h k"),
                                 kqT[:, :, 0:PAST].bitcast(F32)).then_inc(cache_out, 16)
                    sp.wait_ge(cv_lo, 1)
                    sp.dma_start(vs_d[:, :, 0, :].rearrange("h p k -> p h k"), vpack[:].bitcast(F32)).then_inc(cache_out, 16)
                load_group(c, 2)
                load_group(c, 3)
                kq0 = 2 * 4 * c
                for s, (sec, i, m) in enumerate(kvq_events(c)):
                    q0, r = tl[i]
                    if sec == "k":
                        sp.wait_ge(kq_n, kq0 + m + 1)
                        dst = nk_prompt[0, 0, t0 + q0:t0 + q0 + r] if i < 4 else nk_sample[0, 0]
                        sp.dma_start(dst.rearrange("t h d -> t (h d)"), kn[0:r, m % 2, :]).then_inc(kn_out[m % 2], 16)
                        if i == 1:
                            load_group(c, G_Q)
                    elif sec == "v":
                        sp.wait_ge(v_lo, 4 * c + i + 1)
                        dst = nv_prompt[0, 0, t0 + q0:t0 + q0 + r] if i < 4 else nv_sample[0, 0]
                        sp.dma_start(dst.rearrange("t h d -> t (h d)"), vout[0:r, i % 2, :]).then_inc(vo_out[i % 2], 16)
                        dst = (v_d[:, :, 4 * c + i, :] if i < 4 else vs_d[:, 0:r, 1, :]).rearrange("h p k -> p h k")
                        sp.dma_start(dst, vpack[0:r].bitcast(F32)).then_inc(vp_out, 16)
                        if i == 1:
                            sp.wait_ge(kqT_ok, 2 * (kq0 + nt))
                            sp.dma_start(k_d[:, :, t0:t0 + CHUNK].rearrange("h p k -> p h k"),
                                         kqT[:, :, 0:CHUNK].bitcast(F32)).then_inc(kT_out, 16)
                            if c == NC - 1:
                                sp.dma_start(ks_d[:, :, PAST:PAST + DEC].rearrange("h p k -> p h k"),
                                             kqT[:, :, CHUNK:TMAX].bitcast(F32)).then_inc(kT_out, 16)
                        if i == 2:
                            load_group(c, G_PW)
                sp.wait_ge(kqT_ok, 2 * (kq0 + 2 * nt))
                T = tl[-1][0] + tl[-1][1]
                sp.dma_start(q_d[:, :, t0:t0 + T].rearrange("h p k -> p h k"),
                             kqT[:, :, 0:T].bitcast(F32)).then_inc(qT_out, 16)
                load_group(c, G_OUT)
                if c == NC - 1:
                    sp.wait_ge(cvo_ok, 2)
                    sp.dma_start(ncv_prompt[0, 0], cvout[:, 0, :]).then_inc(cvo_out, 16)
                    sp.dma_start(ncv_sample[0, 0], cvout[:, 1, :]).then_inc(cvo_out, 16)
                sp.wait_ge(kT_out, 16 * (c + 1 + (c == NC - 1)))
                sp.wait_ge(vp_out, 16 * (4 * c + nt))
                sp.wait_ge(qT_out, 16 * (c + 1))
                sp.wait_ge(cache_out, 32)
                sp.wait_ge(kvq_ps, 3 * (4 * c + nt))
                sp.wait_ge(pw_lo, CB * (c + len(conv_pieces(c))))
                for kind, pairs in passes(c):
                    before, n = att_counts(c, kind)

                    def load_head(it, b):
                        h = 2 * it + b
                        k_b, v_b, q_b, done = a_k[b], a_v[b], a_q[b], at_in[b]
                        if kind == 0:
                            nk, qs, w = CHUNK * (c + 1), t0, CHUNK
                            sp.dma_start(k_b[:, 0:nk].bitcast(F32), k_d[h, :, 0:nk]).then_inc(done, 16)
                            sp.dma_start(v_b[:, 0:nk // P, :].bitcast(F32), v_d[h, :, 0:nk // P, :]).then_inc(done, 16)
                        else:
                            qs, w = SEQ, DEC
                            sp.dma_start(k_b[:, 0:PAST + DEC].bitcast(F32), ks_d[h]).then_inc(done, 16)
                            sp.dma_start(v_b[:, 0, :].bitcast(F32), vs_d[h, :, 0, :]).then_inc(done, 16)
                            sp.dma_start(v_b[0:DEC, 1, :].bitcast(F32), vs_d[h, 0:DEC, 1, :]).then_inc(done, 16)
                        sp.dma_start(q_b[:, 0, 0:w].bitcast(F32), q_d[h, :, qs:qs + w]).then_inc(done, 16)
                        for p0 in (0, HD):
                            sp.dma_start(q_b[p0:p0 + HD, 1, 0:w].bitcast(F32),
                                         q_d[h, HD - p0:P - p0, qs:qs + w]).then_inc(done, 16)

                    sp.wait_ge(o_lo, before["o"] + 1)
                    for b in range(2):
                        load_head(0, b)
                    with sp.Fori(1, NH // 2) as it:
                        for b in range(2):
                            sp.wait_ge(o_lo, before["o"] + 1 + it * n["o"] - (1 - b) * len(pairs))
                            load_head(it, b)
                load_gain(c, 1)
                load_group(c, G_OUT + 1)
                load_ff1(c, 0)
                with sp.Fori(0, FFE - 1) as e:
                    load_ff2(c, e)
                    load_ff1(c, e + 1)
                load_ff2(c, FFE - 1)
                load_group(c + 1, 0)
                load_group(c + 1, 1)
                for i, (q0, r) in enumerate(tl):
                    sp.wait_ge(f2_add, 2 * (4 * c * FFE + (FFE - 1) * nt + i + 1))
                    dst = y_prompt[0, t0 + q0:t0 + q0 + r, :] if i < 4 else y_sample[0]
                    sp.dma_start(dst, resid[0:r, i, :]).then_inc(y_out[i], 16)
            for i in range(4):
                sp.wait_ge(y_out[i], 16 * NC)
            sp.wait_ge(y_out[4], 16)
            sp.wait_ge(kn_out[0], 16 * (2 * NC + 1))
            sp.wait_ge(kn_out[1], 16 * 2 * NC)
            sp.wait_ge(vo_out[0], 16 * (2 * NC + 1))
            sp.wait_ge(vo_out[1], 16 * 2 * NC)
            sp.wait_ge(cvo_out, 32)

        @block.gpsimd
        def _(pool):
            def split_lo(c, g, j, width=SLAB):
                n = 4 * (GROUPS * c + g) + j
                pool.wait_ge(hi_done, n + 1)
                nc.gpsimd.tensor_tensor(w_lo[g % 2][:, j, 0:width], w_raw[:, j, 0:width],
                                        w_hi[g % 2][:, j, 0:width].bitcast(F32), ALU.subtract).then_inc(lo_done, 1)

            def split_lo_group(c, g):
                if g == GROUPS:
                    c, g = c + 1, 0
                if c < NC:
                    for j in range(4):
                        split_lo(c, g, j, CC if g == G_PW else SLAB)

            def norm(c, which):
                nb = norm_base(c, which)
                for i, (q0, r) in enumerate(tiles(c)):
                    pool.wait_ge(n_ss, nb + i + 1)
                    if i == 0 and nb:
                        pool.wait_ge(n_xn, nb)
                    nc.gpsimd.tensor_scalar(rstd[0:r, i:i + 1], ssum[0:r, i:i + 1], 1.0 / D, EPS,
                                            ALU.mult, ALU.add).then_inc(n_var, 1)
                    pool.wait_ge(n_var, nb + i + 1)
                    nc.gpsimd.tensor_tensor(rstd[0:r, i:i + 1], rstd[0:r, i:i + 1], neghalf[0:r, :],
                                            ALU.pow).then_inc(n_rstd, 1)

            nc.gpsimd.memset(ident[:], 0.0).then_inc(consts, 1)
            nc.gpsimd.memset(ones[:], 1.0).then_inc(consts, 1)
            nc.gpsimd.memset(neghalf[:], -0.5).then_inc(consts, 1)
            pool.wait_ge(consts, 3)
            nc.gpsimd.affine_select(out=ident[:], in_=ident[:], compare_op=ALU.not_equal, fill=1.0, base=0,
                                    pattern=[[-1, P]], channel_multiplier=1).then_inc(consts, 1)
            nc.gpsimd.memset(past[:], 1.0).then_inc(consts, 1)
            pool.wait_ge(consts, 5)
            nc.gpsimd.affine_select(out=past[:], in_=past[:], compare_op=ALU.is_gt, fill=0.0, base=0,
                                    pattern=[[-1, P]], channel_multiplier=1).then_inc(consts, 1)
            for c in range(NC):
                nt = len(tiles(c))
                if c == 0:
                    split_lo_group(0, 0)
                norm(c, 0)
                split_lo_group(c, 1)
                split_lo_group(c, 2)
                kq0 = 8 * c
                for s, (sec, i, m) in enumerate(kvq_events(c)):
                    if m is not None:
                        u = kq0 + m
                        rr = tiles(c)[i][1]
                        pool.wait_ge(kq_ss, u + 1)
                        nc.gpsimd.tensor_scalar(hrs[0:rr, m % 2, :], hss[0:rr, m % 2, :], 1.0 / HD, EPS,
                                                ALU.mult, ALU.add).then_inc(kq_var, 1)
                        pool.wait_ge(kq_var, u + 1)
                        nc.gpsimd.tensor_tensor(hrs[0:rr, m % 2, :], hrs[0:rr, m % 2, :],
                                                neghalf[0:rr, :].to_broadcast([rr, NH]), ALU.pow).then_inc(kq_rs, 1)
                    if i < 4:
                        g = {"k": G_V, "v": G_Q, "q": G_PW}[sec]
                        split_lo(c, g, i, CC if g == G_PW else SLAB)
                lb = c
                for n, (a, q0, w) in enumerate(conv_pieces(c)):
                    pool.wait_ge(var_ok, lb + n + 1)
                    nc.gpsimd.tensor_tensor(lnr[:, 0:w], lnv[:, 0:w], neghalf[:].to_broadcast([P, w]),
                                            ALU.pow).then_inc(lnr_ok, 1)
                split_lo_group(c, G_OUT)
                pool.wait_ge(consts, 6)
                for kind, pairs in passes(c):
                    before, cn = att_counts(c, kind)
                    seq = att_sequence(pairs)
                    with pool.Fori(0, NH // 2) as it:
                        def mask(k, ready):
                            head, (p, t, q0, r, a0, n, diag, last), m, tg = seq[k]
                            if not diag:
                                return
                            pool.wait_ge(ready, before["z"] + it * cn["z"] + k + 1)
                            v = sc[k % 3][0:r, n - r:n]
                            nc.gpsimd.tensor_tensor(v, v, past[0:r, 0:r], ALU.mult).then_inc(
                                s_lnm if ready is s_ln else s_am, 1)
                        for k in range(len(seq) + 1):
                            if k < len(seq):
                                mask(k, s_ln)
                            if k >= 1:
                                mask(k - 1, s_a)
                split_lo_group(c, G_OUT + 1)
                split_lo_group(c, G_FF)
                norm(c, 1)
                with pool.Fori(0, FFE - 1) as e:
                    for g in (G_FF + 1, G_FF + 2):
                        for j in range(4):
                            n = 4 * (GROUPS * c + g) + 8 * e + j
                            pool.wait_ge(hi_done, n + 1)
                            nc.gpsimd.tensor_tensor(w_lo[g % 2][:, j, :], w_raw[:, j, :],
                                                    w_hi[g % 2][:, j, :].bitcast(F32), ALU.subtract).then_inc(lo_done, 1)
                split_lo_group(c, GROUPS - 1)
                split_lo_group(c, GROUPS)

        @block.scalar
        def _(act):
            def split_hi(c, g, j, width=SLAB, e=None):
                act.wait_ge(raw_in[j], 16 * (GROUPS * c + g + 1) + (32 * e if e is not None else 0))
                nc.scalar.copy(w_hi[g % 2][:, j, 0:width], w_raw[:, j, 0:width]).then_inc(hi_done, 1)

            def split_hi_group(c, g):
                if g == GROUPS:
                    c, g = c + 1, 0
                if c < NC:
                    for j in range(4):
                        split_hi(c, g, j, CC if g == G_PW else SLAB)

            def norm(c, which):
                nb = norm_base(c, which)
                tl = tiles(c)
                if c or which:
                    if which:
                        act.wait_ge(out_add, 2 * (4 * c + len(tl)))
                    else:
                        act.wait_ge(f2_add, 2 * FFE * 4 * c)
                for i, (q0, r) in enumerate(tl):
                    if which == 0:
                        act.wait_ge(x_in[i], 16 * ((c if i < 4 else 0) + 1))
                    if i == 0 and nb:
                        act.wait_ge(n_rstd, nb)
                    if i:
                        act.wait_ge(n_ss, nb + i)
                    nc.scalar.activation(ps[0:r, 6:8, :].rearrange("p a b -> p (a b)"), resid[0:r, i, :], ACT.Square,
                                         accum_out=ssum[0:r, i:i + 1]).then_inc(n_ss, 1)
                for i, (q0, r) in enumerate(tl):
                    for hf in range(2):
                        ev = 2 * (nb + i) + hf
                        act.wait_ge(n_tp, ev + 1)
                        nc.scalar.copy(hT_hi[:, 4 * hf:4 * hf + 4, q0:q0 + r],
                                       ps[:, 4 + hf, 0:4 * r].rearrange("p (a b) -> p a b", a=4)).then_inc(n_hi, 1)

            act.wait_ge(consts, 4)
            act.wait_ge(vec_t, 1)
            nc.scalar.copy(vecs[:], ps[:, 0, 0:CB * (CW + 3)].rearrange("p (a b) -> p a b", a=CB)).then_inc(vec_ok, 1)
            act.wait_ge(vec_t, 2)
            nc.scalar.copy(uT[:, :, SMP:SMP + HIST], ps[:, 1, 0:CB * HIST].rearrange("p (a b) -> p a b", a=CB)).then_inc(vec_ok, 1)
            act.wait_ge(ck_in, 16)
            nc.scalar.copy(packed[:, 0, :, 0:HD], kn[:, 0, :].rearrange("p (h d) -> p h d", h=NH)).then_inc(ck_hi, 1)
            act.wait_ge(cv_in, 16)
            nc.scalar.copy(vpack[:, :, 0:HD], vout[:, 0, :].rearrange("p (h d) -> p h d", h=NH)).then_inc(cv_hi, 1)
            for q in range(2):
                act.wait_ge(ckT_ps, q + 1)
                nc.scalar.copy(kqT[:, 4 * q:4 * q + 4, 0:PAST],
                               ps[:, 2 + q, :].rearrange("p (a b) -> p a b", a=4)).then_inc(ckT_ok, 1)
            for c in range(NC):
                tl = tiles(c)
                nt = len(tl)
                sp_ = splits(c)
                ns = len(sp_)
                if c == 0:
                    split_hi_group(0, 0)
                norm(c, 0)
                for g in range(2):
                    split_hi_group(c, g + 1)
                    for pr in range(2):
                        for s, (s0, w) in enumerate(sp_):
                            ev = 8 * c + (4 * g + 2 * pr + 1) * ns + s
                            u = 4 * c + (2 * g + pr) * ns + s
                            act.wait_ge(ag_ps, ev + 1)
                            if u >= 2:
                                act.wait_ge(ag_u, u - 1)
                            if c == 0 and g == 0 and pr == 0 and s == 0:
                                act.wait_ge(vec_ok, 2)
                                act.wait_ge(vec_t, 2)
                            nc.scalar.activation(sgate[:, u % 2, 0:w], ps[:, (ev - 8 * c) % 4, 0:w],
                                                 ACT.Sigmoid).then_inc(ag_sig, 1)
                ev0 = 12 * c
                kq0 = 8 * c
                evs = kvq_events(c)
                act.wait_ge(ag_u, 4 * c + 4 * ns)
                act.wait_ge(cache_out, 32)
                for s in range(len(evs) + 3):
                    if s < len(evs):
                        sec, i, m = evs[s]
                        r = tl[i][1]
                        act.wait_ge(kvq_ps, ev0 + s + 1)
                        src = ps[0:r, 4 + s % 4, :]
                        if sec == "v":
                            k = i % 2
                            n = 2 * c + i // 2
                            if n:
                                act.wait_ge(vo_out[k], 16 * n)
                            if i >= 2:
                                act.wait_ge(v_lo, 4 * c + i - 1)
                            nc.scalar.copy(vout[0:r, k, :], src).then_inc(kvq_cp, 1)
                        else:
                            if m >= 2:
                                act.wait_ge(kq_mul, kq0 + m - 1)
                            nc.scalar.copy(raw_kq[0:r, m % 2, :], src).then_inc(kvq_cp, 1)
                    if 1 <= s <= len(evs):
                        sec, i, m = evs[s - 1]
                        r = tl[i][1]
                        if sec == "v":
                            act.wait_ge(kvq_cp, ev0 + s)
                            if 4 * c + i:
                                act.wait_ge(vp_out, 16 * (4 * c + i))
                            nc.scalar.copy(vpack[0:r, :, 0:HD],
                                           vout[0:r, i % 2, :].rearrange("p (h d) -> p h d", h=NH)).then_inc(cv_hi, 1)
                        else:
                            act.wait_ge(kq_n, kq0 + m + 1)
                            if m >= 2:
                                act.wait_ge(kqT_ps, 2 * (kq0 + m - 1))
                            nc.scalar.copy(packed[0:r, m % 2, :, 0:HD],
                                           kn[0:r, m % 2, :].rearrange("p (h d) -> p h d", h=NH)).then_inc(pk_hi, 1)
                    if s >= 3:
                        sec, i, m = evs[s - 3]
                        q0, r = tl[i]
                        if sec != "v":
                            if sec == "q" and i == 0:
                                act.wait_ge(kT_out, 16 * (c + 1 + (c == NC - 1)))
                            for q in range(2):
                                act.wait_ge(kqT_ps, 2 * (kq0 + m) + q + 1)
                                nc.scalar.copy(kqT[:, 4 * q:4 * q + 4, q0:q0 + r],
                                               ps[:, q, 0:4 * r].rearrange("p (a b) -> p a b", a=4)).then_inc(kqT_ok, 1)
                    if s < len(evs) and evs[s][1] < 4:
                        g = {"k": G_V, "v": G_Q, "q": G_PW}[evs[s][0]]
                        split_hi(c, g, evs[s][1], CC if g == G_PW else SLAB)
                if c == NC - 1:
                    for q in range(2):
                        act.wait_ge(cvo_ps, q + 1)
                        nc.scalar.copy(cvout[:, q, :], ps[0:HIST, 4 + q, :]).then_inc(cvo_ok, 1)
                for n, (a, q0, w) in enumerate(conv_pieces(c)):
                    lb = c + n
                    for k in range(CB):
                        act.wait_ge(xc_ok, CB * lb + k + 1)
                        if k == 0:
                            act.wait_ge(vp_out, 16 * (4 * c + nt))
                            act.wait_ge(vo_out[0], 16 * (2 * c + (nt + 1) // 2))
                            act.wait_ge(vo_out[1], 16 * (2 * c + 2))
                        nc.scalar.activation(csq[:, k, a:a + w], cacc[:, k, a:a + w], ACT.Square).then_inc(sq_ok, 1)
                    act.wait_ge(kn_out[0], 16 * (2 * c + (nt + 1) // 2))
                    act.wait_ge(kn_out[1], 16 * (2 * c + nt // 2))
                    for k in range(CB):
                        act.wait_ge(yn_ok, CB * lb + k + 1)
                        if CB * lb + k >= 2:
                            act.wait_ge(cm_ok, CB * lb + k - 1)
                        nc.scalar.activation(csig[:, k % 2, 0:w], cacc[:, k, a:a + w], ACT.Sigmoid,
                                             bias=vecs[:, k, CW + 2:CW + 3], scale=vecs[:, k, CW + 1:CW + 2]).then_inc(sg_ok, 1)
                        nc.scalar.activation(cid[:, k % 2, 0:w], cacc[:, k, a:a + w], ACT.Identity,
                                             bias=vecs[:, k, CW + 2:CW + 3], scale=vecs[:, k, CW + 1:CW + 2]).then_inc(sg_ok, 1)
                        act.wait_ge(cm_ok, CB * lb + k + 1)
                        if k == 0:
                            act.wait_ge(var_ps, lb + 1)
                        nc.scalar.copy(cT_hi[:, k, a:a + w], cacc[:, k, a:a + w]).then_inc(c_hi, 1)
                split_hi_group(c, G_OUT)
                act.wait_ge(qT_out, 16 * (c + 1))
                for m in range(CB):
                    for n, (a, q0, w) in enumerate(conv_pieces(c)):
                        npc = len(conv_pieces(c))
                        ev = CB * c + npc * m + n
                        act.wait_ge(pw_ps, ev + 1)
                        nc.scalar.copy(mixT_hi[:, m, q0:q0 + w], ps[:, (ev - CB * c) % 4, 0:w]).then_inc(pw_hi, 1)
                act.add_instruction(mybir.InstLoadActFuncSet(name=nc.get_next_instruction_name(), engine=act.engine,
                                                             act_func_set_id=ACT_TABLE_LN_EXP, ins=[], outs=[]))
                if c == NC - 1:
                    act.wait_ge(cvo_out, 32)
                for kind, pairs in passes(c):
                    before, cn = att_counts(c, kind)
                    seq = att_sequence(pairs)
                    npair = len(pairs)
                    with act.Fori(0, NH // 2) as it:
                        def cnt(what, n):
                            return before[what] + it * cn[what] + n

                        for k in range(len(seq) + 3):
                            if k < len(seq):
                                head, (p, t, q0, r, a0, n, diag, last), m, tg = seq[k]
                                v = sc[k % 3][0:r, 0:n]
                                if diag:
                                    act.wait_ge(z_msk, cnt("m", m + 1))
                                else:
                                    act.wait_ge(z_ps, cnt("z", k + 1))
                                if k >= 3:
                                    old = seq[k - 3]
                                    act.wait_ge(t_ps, cnt("t", old[3] + len(key_groups(old[1][4], old[1][5]))))
                                nc.scalar.activation(v, bank(k, r, 0, n), ACT.Abs).then_inc(z_abs, 1)
                                act.wait_ge(z_abs, cnt("z", k + 1))
                                nc.scalar.activation(v, v, ACT.Exp, scale=-1.0).then_inc(s_exp, 1)
                                act.wait_ge(s_exp, cnt("z", k + 1))
                                nc.scalar.activation(v, v, ACT.Ln, bias=1.0).then_inc(s_ln, 1)
                            if 1 <= k <= len(seq):
                                head, (p, t, q0, r, a0, n, diag, last), m, tg = seq[k - 1]
                                v = sc[(k - 1) % 3][0:r, 0:n]
                                act.wait_ge(s_scan, cnt("z", k))
                                nc.scalar.activation(v, v, ACT.Exp).then_inc(s_a, 1)
                            if k >= 3:
                                head, (p, t, q0, r, a0, n, diag, last), m, tg = seq[k - 3]
                                if last and t == len(pairs[p]) - 1:
                                    ob = head * npair + p
                                    w = sum(x[1] for x in pairs[p])
                                    act.wait_ge(o_ps, cnt("o", ob + 1))
                                    act.wait_ge(o_lo, cnt("o", ob) + 1)
                                    mine = head * HD
                                    nc.scalar.copy(osb[mine:mine + HD, 0:w],
                                                   ps[HD - mine:P - mine, 6 + ob % 2, 0:w]).then_inc(o_cp, 1)
                split_hi_group(c, G_OUT + 1)
                act.wait_ge(out_ps, 8 * c + nt)
                split_hi_group(c, G_FF)
                norm(c, 1)
                f1b = 4 * FFE * c
                f2b = 8 * FFE * c + 1

                def hi_of(e, k):
                    j, s = k // ns, k % ns
                    s0, w = sp_[s]
                    act.wait_ge(f_sq, f1b + k + 1 + e * 4 * ns)
                    nc.scalar.copy(hid_hi[:, j, s0:s0 + w], fsq[:, k % 2, 0:w]).then_inc(f_hi, 1)

                def ff1(e):
                    for k in range(4 * ns):
                        w = sp_[k % ns][1]
                        act.wait_ge(f1_ps, f1b + k + 1 + e * 4 * ns)
                        if k >= 2:
                            act.wait_ge(f_sq, f1b + k - 1 + e * 4 * ns)
                        nc.scalar.activation(frel[:, k % 2, 0:w], ps[:, k % 4, 0:w], ACT.Relu).then_inc(f_rel, 1)
                        if k >= 1:
                            hi_of(e, k - 1)
                    hi_of(e, 4 * ns - 1)

                with act.Fori(0, FFE - 1) as e:
                    act.wait_ge(f2_ps, f2b + e * 2 * nt)
                    for j in range(4):
                        split_hi(c, G_FF + 1, j, e=e)
                    ff1(e)
                    for j in range(4):
                        split_hi(c, G_FF + 2, j, e=e)
                act.wait_ge(f2_ps, f2b + (FFE - 1) * 2 * nt)
                split_hi_group(c, GROUPS - 1)
                ff1(FFE - 1)
                split_hi_group(c, GROUPS)

        @block.vector
        def _(dve):
            def norm(c, which):
                nb = norm_base(c, which)
                tl = tiles(c)
                nst = 2 * c + which
                dve.wait_ge(grow_in, 16 * (nst + 1))
                for i in range(len(tl) + 1):
                    if i < len(tl):
                        q0, r = tl[i]
                        dve.wait_ge(n_rstd, nb + i + 1)
                        if i >= 2:
                            dve.wait_ge(n_tp, 2 * (nb + i - 1))
                        nc.vector.scalar_tensor_tensor(out=xn[0:r, i % 2, :], in0=resid[0:r, i, :],
                                                       scalar=rstd[0:r, i:i + 1], in1=g_row[0:r, :],
                                                       op0=ALU.mult, op1=ALU.mult).then_inc(n_xn, 1)
                    if i >= 1:
                        q0, r = tl[i - 1]
                        for hf in range(2):
                            dve.wait_ge(n_hi, 2 * (nb + i - 1) + hf + 1)
                            nc.vector.tensor_tensor(hT_lo[:, 4 * hf:4 * hf + 4, q0:q0 + r],
                                                    ps[:, 4 + hf, 0:4 * r].rearrange("p (a b) -> p a b", a=4),
                                                    hT_hi[:, 4 * hf:4 * hf + 4, q0:q0 + r].bitcast(F32),
                                                    ALU.subtract).then_inc(n_lo, 1)

            dve.wait_ge(gains_in, 32)
            nc.vector.tensor_scalar(gq[:], gq[:], HD ** -0.5, None, ALU.mult).then_inc(hist_ok, 1)
            nc.vector.memset(uT[:, :, 0:HIST], 0.0).then_inc(hist_ok, 1)
            nc.vector.memset(carry[:], 0.0).then_inc(o_lo, 1)
            dve.wait_ge(ck_hi, 1)
            nc.vector.tensor_tensor(packed[:, 0, :, HD:P], kn[:, 0, :].rearrange("p (h d) -> p h d", h=NH),
                                    packed[:, 0, :, 0:HD].bitcast(F32), ALU.subtract).then_inc(ck_lo, 1)
            dve.wait_ge(cv_hi, 1)
            nc.vector.tensor_tensor(vpack[:, :, HD:P], vout[:, 0, :].rearrange("p (h d) -> p h d", h=NH),
                                    vpack[:, :, 0:HD].bitcast(F32), ALU.subtract).then_inc(cv_lo, 1)
            for c in range(NC):
                tl = tiles(c)
                nt = len(tl)
                sp_ = splits(c)
                ns = len(sp_)
                norm(c, 0)
                if c:
                    dve.wait_ge(taps, TAPS * c)
                    nc.vector.tensor_copy(uT[:, :, 0:HIST], uT[:, :, CHUNK:CHUNK + HIST]).then_inc(hist_ok, 1)
                dve.wait_ge(hist_ok, 2 + c)
                for m in range(CB):
                    for s, (s0, w) in enumerate(sp_):
                        u = 4 * c + m * ns + s
                        evv = 2 * m * ns + s
                        dve.wait_ge(ag_sig, u + 1)
                        cut = max(s0, min(s0 + w, CHUNK))
                        for n, (x0, x1) in enumerate([(s0, cut), (cut, s0 + w)]):
                            if x1 > x0:
                                d0 = x0 + HIST + (HIST if x0 >= CHUNK else 0)
                                ins = nc.vector.tensor_tensor(uT[:, m, d0:d0 + x1 - x0], ps[:, evv % 4, x0 - s0:x1 - s0],
                                                              sgate[:, u % 2, x0 - s0:x1 - s0], ALU.mult)
                        ins.then_inc(ag_u, 1)
                evs = kvq_events(c)
                kq0 = 8 * c
                wd = CVW if c == NC - 1 else CHUNK
                dve.wait_ge(vec_ok, 2)
                dve.wait_ge(ag_u, 4 * c + 4 * ns)
                for s in range(len(evs) + 1):
                    if s < len(evs):
                        sec, i, m = evs[s]
                        r = tl[i][1]
                        if m is not None:
                            u = kq0 + m
                            b = m % 2
                            dve.wait_ge(kvq_cp, 12 * c + s + 1)
                            if u:
                                dve.wait_ge(kq_ss, u)
                            nc.vector.tensor_tensor(sqr[0:r, :], raw_kq[0:r, b, :], raw_kq[0:r, b, :], ALU.mult).then_inc(kq_sq, 1)
                            dve.wait_ge(kq_sq, u + 1)
                            nc.vector.tensor_reduce(hss[0:r, b, :], sqr[0:r, :].rearrange("p (h d) -> p h d", h=NH),
                                                    axis=AX.X, op=ALU.add).then_inc(kq_ss, 1)
                    if s >= 1:
                        psec, pi, pm = evs[s - 1]
                        pr = tl[pi][1]
                        if pm is not None:
                            dve.wait_ge(pk_hi, kq0 + pm + 1)
                            nc.vector.tensor_tensor(packed[0:pr, pm % 2, :, HD:P],
                                                    kn[0:pr, pm % 2, :].rearrange("p (h d) -> p h d", h=NH),
                                                    packed[0:pr, pm % 2, :, 0:HD].bitcast(F32), ALU.subtract).then_inc(pk_lo, 1)
                        else:
                            dve.wait_ge(cv_hi, 4 * c + pi + 2)
                            nc.vector.tensor_tensor(vpack[0:pr, :, HD:P],
                                                    vout[0:pr, pi % 2, :].rearrange("p (h d) -> p h d", h=NH),
                                                    vpack[0:pr, :, 0:HD].bitcast(F32), ALU.subtract).then_inc(v_lo, 1)
                    if s < len(evs):
                        for x in taps_of(c, s):
                            tap, k = x // CB, x % CB
                            n = TAPS * c + x
                            if tap == 0:
                                nc.vector.tensor_scalar(cacc[:, k, 0:wd], uT[:, k, 0:wd], vecs[:, k, 0:1],
                                                        vecs[:, k, CW:CW + 1], ALU.mult, ALU.add).then_inc(taps, 1)
                            else:
                                dve.wait_ge(taps, n - CB + 1)
                                nc.vector.scalar_tensor_tensor(out=cacc[:, k, 0:wd], in0=uT[:, k, tap:tap + wd],
                                                               scalar=vecs[:, k, tap:tap + 1], in1=cacc[:, k, 0:wd],
                                                               op0=ALU.mult, op1=ALU.add).then_inc(taps, 1)
                        if m is not None:
                            dve.wait_ge(kq_rs, u + 1)
                            if u >= 2:
                                dve.wait_ge(pk_lo, u - 1)
                            uses = (2 * c + i // 2) if sec == "k" else 2 * c + (nt + 1 - b) // 2
                            if uses:
                                dve.wait_ge(kn_out[b], 16 * uses)
                            dve.wait_ge(ck_lo, 1)
                            nc.vector.tensor_tensor(kn[0:r, b, :].rearrange("p (h d) -> p h d", h=NH),
                                                    raw_kq[0:r, b, :].rearrange("p (h d) -> p h d", h=NH),
                                                    hrs[0:r, b, :].unsqueeze(2).to_broadcast([r, NH, HD]),
                                                    ALU.mult).then_inc(kq_mul, 1)
                            dve.wait_ge(kq_mul, u + 1)
                            gain = gk if sec == "k" else gq
                            nc.vector.tensor_tensor(kn[0:r, b, :].rearrange("p (h d) -> p h d", h=NH),
                                                    kn[0:r, b, :].rearrange("p (h d) -> p h d", h=NH),
                                                    gain[0:r, :].unsqueeze(1).to_broadcast([r, NH, HD]),
                                                    ALU.mult).then_inc(kq_n, 1)
                dve.wait_ge(taps, TAPS * (c + 1))
                for n, (a, q0, w) in enumerate(conv_pieces(c)):
                    lb = c + n
                    dve.wait_ge(mean_ps, lb + 1)
                    for k in range(CB):
                        nc.vector.scalar_tensor_tensor(out=cacc[:, k, a:a + w], in0=ps[:, 2, 0:w], scalar=-1.0 / CC,
                                                       in1=cacc[:, k, a:a + w], op0=ALU.mult, op1=ALU.add).then_inc(xc_ok, 1)
                    dve.wait_ge(var_ps, lb + 1)
                    if n:
                        dve.wait_ge(lnr_ok, lb)
                    nc.vector.tensor_scalar(lnv[:, 0:w], ps[:, 3, 0:w], 1.0 / CC, EPS, ALU.mult, ALU.add).then_inc(var_ok, 1)
                    dve.wait_ge(lnr_ok, lb + 1)
                    dve.wait_ge(xc_ok, CB * (lb + 1))
                    for k in range(CB):
                        nc.vector.tensor_tensor(cacc[:, k, a:a + w], cacc[:, k, a:a + w], lnr[:, 0:w],
                                                ALU.mult).then_inc(yn_ok, 1)
                    for k in range(CB + 1):
                        if k < CB:
                            dve.wait_ge(sg_ok, 2 * (CB * lb + k + 1))
                            nc.vector.tensor_tensor(cacc[:, k, a:a + w], csig[:, k % 2, 0:w], cid[:, k % 2, 0:w],
                                                    ALU.mult).then_inc(cm_ok, 1)
                        if k >= 1:
                            dve.wait_ge(c_hi, CB * lb + k)
                            nc.vector.tensor_tensor(cT_lo[:, k - 1, a:a + w], cacc[:, k - 1, a:a + w],
                                                    cT_hi[:, k - 1, a:a + w].bitcast(F32), ALU.subtract).then_inc(c_lo, 1)
                npc = len(conv_pieces(c))
                for m in range(CB):
                    for n, (a, q0, w) in enumerate(conv_pieces(c)):
                        ev = CB * c + npc * m + n
                        dve.wait_ge(pw_hi, ev + 1)
                        nc.vector.tensor_tensor(mixT_lo[:, m, q0:q0 + w], ps[:, (ev - CB * c) % 4, 0:w],
                                                mixT_hi[:, m, q0:q0 + w].bitcast(F32), ALU.subtract).then_inc(pw_lo, 1)
                dve.wait_ge(consts, 6)
                if c == NC - 1:
                    dve.wait_ge(cvo_out, 32)
                for kind, pairs in passes(c):
                    before, cn = att_counts(c, kind)
                    seq = att_sequence(pairs)
                    npair = len(pairs)
                    with dve.Fori(0, NH // 2) as it:
                        def cnt(what, n):
                            return before[what] + it * cn[what] + n

                        for k in range(len(seq) + 3):
                            if k < len(seq):
                                head, (p, t, q0, r, a0, n, diag, last), m, tg = seq[k]
                                if diag:
                                    dve.wait_ge(z_ps, cnt("z", k + 1))
                                    nc.vector.tensor_tensor(bank(k, r, n - r, n), bank(k, r, n - r, n), past[0:r, 0:r],
                                                            ALU.mult).then_inc(z_msk, 1)
                            if 1 <= k <= len(seq):
                                kk = k - 1
                                head, (p, t, q0, r, a0, n, diag, last), m, tg = seq[kk]
                                v = sc[kk % 3]
                                if diag:
                                    dve.wait_ge(s_lnm, cnt("m", m + 1))
                                else:
                                    dve.wait_ge(s_ln, cnt("z", kk + 1))
                                nc.vector.scalar_tensor_tensor(out=v[0:r, 0:n], in0=bank(kk, r, 0, n), scalar=0.0,
                                                               in1=v[0:r, 0:n], op0=ALU.min, op1=ALU.subtract).then_inc(s_p, 1)
                                dve.wait_ge(s_p, cnt("z", kk + 1))
                                x = sum(not q[1][7] for q in seq[:kk])
                                init = 0.0
                                if not diag:
                                    dve.wait_ge(s_scan, cnt("z", kk))
                                    nc.vector.tensor_tensor(v[0:r, n - 1:n], v[0:r, n - 1:n], carry[0:r, :],
                                                            ALU.add).then_inc(s_edge, 1)
                                    dve.wait_ge(s_edge, cnt("x", x))
                                    init = v[0:r, n - 1:n]
                                ins = nc.vector.tensor_tensor_scan(v[0:r, 0:n - 1][:, ::-1], v[0:r, 0:n - 1][:, ::-1],
                                                                   bank(kk, r, 1, n)[:, ::-1], init, ALU.add, ALU.subtract)
                                if last:
                                    ins.then_inc(s_scan, 1)
                                else:
                                    ins.then_inc(s_fin, 1)
                                    dve.wait_ge(s_fin, cnt("x", x + 1))
                                    nc.vector.tensor_tensor(carry[0:r, :], v[0:r, 0:1], bank(kk, r, 0, 1),
                                                            ALU.subtract).then_inc(s_scan, 1)
                            if 2 <= k <= len(seq) + 1:
                                head, (p, t, q0, r, a0, n, diag, last), m, tg = seq[k - 2]
                                for gi, grp in enumerate(key_groups(a0, n)):
                                    dve.wait_ge(t_ps, cnt("t", tg + gi + 1))
                                    if t == 0 and gi == 0 and diag and (head, p) != (0, 0):
                                        dve.wait_ge(o_ps, cnt("o", head * npair + p))
                                    evacuate(nc.vector.tensor_copy, None, aT_hi, grp, t, r,
                                             ps[:, 4 + (tg + gi) % 2, :], t_hi)
                                    dve.wait_ge(t_hi, cnt("t", tg + gi + 1))
                                    evacuate(nc.vector.tensor_tensor, aT_hi, aT_lo, grp, t, r,
                                             ps[:, 4 + (tg + gi) % 2, :], t_lo)
                            if k >= 3:
                                head, (p, t, q0, r, a0, n, diag, last), m, tg = seq[k - 3]
                                if last and t == len(pairs[p]) - 1:
                                    ob = head * npair + p
                                    w = sum(x[1] for x in pairs[p])
                                    col = pairs[p][0][0] if kind == 0 else CHUNK
                                    mine = head * HD
                                    me = slice(mine, mine + HD)
                                    dve.wait_ge(o_cp, cnt("o", ob + 1))
                                    nc.vector.tensor_tensor(of[me, 0:w], ps[me, 6 + ob % 2, 0:w], osb[me, 0:w], ALU.add).then_inc(o_sum, 1)
                                    dve.wait_ge(o_sum, cnt("o", ob + 1))
                                    dst = mixT_hi[me, CB + it, col:col + w]
                                    nc.vector.tensor_copy(dst, of[me, 0:w]).then_inc(o_hi, 1)
                                    dve.wait_ge(o_hi, cnt("o", ob + 1))
                                    nc.vector.tensor_tensor(mixT_lo[me, CB + it, col:col + w], of[me, 0:w],
                                                            dst.bitcast(F32), ALU.subtract).then_inc(o_lo, 1)
                for hf in range(2):
                    for i, (q0, r) in enumerate(tl):
                        ev = hf * nt + i
                        dve.wait_ge(out_ps, 8 * c + ev + 1)
                        v = resid[0:r, i, hf * BANK:(hf + 1) * BANK]
                        nc.vector.tensor_tensor(v, ps[0:r, 4 + ev % 4, :], v, ALU.add).then_inc(out_add, 1)
                norm(c, 1)
                f1b = 4 * FFE * c
                f2b = 8 * FFE * c

                def round_(e):
                    for k in range(4 * ns + 1):
                        if k < 4 * ns:
                            w = sp_[k % ns][1]
                            dve.wait_ge(f_rel, f1b + k + 1 + e * 4 * ns)
                            if k >= 2:
                                dve.wait_ge(f_lo, f1b + k - 1 + e * 4 * ns)
                            nc.vector.tensor_tensor(fsq[:, k % 2, 0:w], frel[:, k % 2, 0:w], frel[:, k % 2, 0:w],
                                                    ALU.mult).then_inc(f_sq, 1)
                        if k >= 1:
                            j, s = (k - 1) // ns, (k - 1) % ns
                            s0, w = sp_[s]
                            dve.wait_ge(f_hi, f1b + k + e * 4 * ns)
                            nc.vector.tensor_tensor(hid_lo[:, j, s0:s0 + w], fsq[:, (k - 1) % 2, 0:w],
                                                    hid_hi[:, j, s0:s0 + w].bitcast(F32), ALU.subtract).then_inc(f_lo, 1)
                    for ev in range(2 * nt):
                        i, hf = ev // 2, ev % 2
                        r = tl[i][1]
                        dve.wait_ge(f2_ps, f2b + ev + 2 + e * 2 * nt)
                        v = resid[0:r, i, hf * BANK:(hf + 1) * BANK]
                        nc.vector.tensor_tensor(v, ps[0:r, 4 + ev % 4, :], v, ALU.add).then_inc(f2_add, 1)

                with dve.Fori(0, FFE) as e:
                    round_(e)

        @block.tensor
        def _(pe):
            def mm3(out, w, x, start, stop):
                nc.tensor.matmul(out, w[0], x[0], start=start, stop=False)
                nc.tensor.matmul(out, w[0], x[1], start=False, stop=False)
                return nc.tensor.matmul(out, w[1], x[0], start=False, stop=stop)

            def slab(g, j):
                return w_hi[g % 2][:, j, :], w_lo[g % 2][:, j, :]

            def norm(c, which):
                nb = norm_base(c, which)
                for i, (q0, r) in enumerate(tiles(c)):
                    pe.wait_ge(n_xn, nb + i + 1)
                    if i == 0 and which == 0 and c:
                        pe.wait_ge(f2_add, 8 * FFE * c)
                    for hf in range(2):
                        ev = 2 * (nb + i) + hf
                        if i:
                            pe.wait_ge(n_lo, ev - 1)
                        for k in range(4):
                            blk = 4 * hf + k
                            ins = nc.tensor.transpose(ps[:, 4 + hf, k * r:(k + 1) * r], xn[0:r, i % 2, blk * P:(blk + 1) * P],
                                                      ident[0:r, 0:r])
                        ins.then_inc(n_tp, 1)

            pe.wait_ge(consts, 4)
            pe.wait_ge(rows_in, 80)
            for k in range(CB):
                n = CW + 3
                ins = nc.tensor.transpose(ps[:, 0, k * n:(k + 1) * n], crow[:, k * P:(k + 1) * P], ident[0:n, 0:n])
            ins.then_inc(vec_t, 1)
            for k in range(CB):
                ins = nc.tensor.transpose(ps[:, 1, k * HIST:(k + 1) * HIST], srow[:, k * P:(k + 1) * P], ident[0:HIST, 0:HIST])
            ins.then_inc(vec_t, 1)
            pe.wait_ge(ck_lo, 1)
            for q in range(2):
                for k in range(4):
                    ins = nc.tensor.transpose(ps[:, 2 + q, k * P:(k + 1) * P], packed[:, 0, 4 * q + k, :].bitcast(F32), ident[:])
                    if (q, k) == (0, 0):
                        ins.then_inc(f2_ps, 1)
                ins.then_inc(ckT_ps, 1)
            for c in range(NC):
                tl = tiles(c)
                nt = len(tl)
                sp_ = splits(c)
                ns = len(sp_)
                norm(c, 0)
                pe.wait_ge(n_lo, 2 * (norm_base(c, 0) + nt))
                if c == 0:
                    pe.wait_ge(vec_ok, 2)
                    pe.wait_ge(ckT_ok, 2)
                else:
                    pe.wait_ge(f_rel, 4 * FFE * c)
                for g in range(2):
                    for j in range(4):
                        n = 4 * (GROUPS * c + g) + j
                        pe.wait_ge(lo_done, n + 1)
                        wh, wl = slab(g, j)
                        for s, (s0, w) in enumerate(sp_):
                            ev = (4 * g + j) * ns + s
                            old = ev - 4
                            if old >= 0:
                                pe.wait_ge(ag_u, 4 * c + (old // (2 * ns)) * ns + old % ns + 1)
                            for k in range(KD):
                                ins = mm3(ps[:, ev % 4, 0:w], (wh[:, k * P:(k + 1) * P], wl[:, k * P:(k + 1) * P]),
                                          (hT_hi[:, k, s0:s0 + w], hT_lo[:, k, s0:s0 + w]), k == 0, k == KD - 1)
                            ins.then_inc(ag_ps, 1)
                evs = kvq_events(c)
                kq0 = 8 * c
                for s in range(len(evs) + 2):
                    if s < len(evs):
                        sec, i, m = evs[s]
                        g = {"k": G_K, "v": G_V, "q": G_Q}[sec]
                        q0, r = tl[i]
                        if s >= 4:
                            pe.wait_ge(kvq_cp, 12 * c + s - 3)
                        for k in range(KD):
                            if i == 0 and k % 2 == 0:
                                pe.wait_ge(lo_done, 4 * (GROUPS * c + g) + k // 2 + 1)
                            wh, wl = slab(g, k // 2)
                            c0 = (k % 2) * AW
                            nc.tensor.matmul(ps[0:r, 4 + s % 4, :], hT_hi[:, k, q0:q0 + r], wh[:, c0:c0 + AW], start=k == 0, stop=False)
                            nc.tensor.matmul(ps[0:r, 4 + s % 4, :], hT_lo[:, k, q0:q0 + r], wh[:, c0:c0 + AW], start=False, stop=False)
                            ins = nc.tensor.matmul(ps[0:r, 4 + s % 4, :], hT_hi[:, k, q0:q0 + r], wl[:, c0:c0 + AW],
                                                   start=False, stop=k == KD - 1)
                        ins.then_inc(kvq_ps, 1)
                    if s >= 2:
                        sec, i, m = evs[s - 2]
                        r = tl[i][1]
                        if sec != "v":
                            pe.wait_ge(pk_lo, kq0 + m + 1)
                            for q in range(2):
                                if m:
                                    pe.wait_ge(kqT_ok, 2 * (kq0 + m) + q - 1)
                                elif q == 0:
                                    pe.wait_ge(ag_u, 4 * c + 4 * ns)
                                for k in range(4):
                                    ins = nc.tensor.transpose(ps[:, q, k * r:(k + 1) * r],
                                                              packed[0:r, m % 2, 4 * q + k, :].bitcast(F32), ident[0:r, 0:r])
                                ins.then_inc(kqT_ps, 1)
                if c == NC - 1:
                    for q, col in enumerate((CHUNK, SMP + DEC)):
                        pe.wait_ge(kvq_cp, 12 * c + len(evs))
                        for k in range(CB):
                            ins = nc.tensor.transpose(ps[0:HIST, 4 + q, k * P:(k + 1) * P], uT[:, k, col:col + HIST], ident[:])
                        ins.then_inc(cvo_ps, 1)
                for n, (a, q0, w) in enumerate(conv_pieces(c)):
                    lb = c + n
                    pe.wait_ge(taps, TAPS * (c + 1))
                    if n:
                        pe.wait_ge(xc_ok, CB * lb)
                    for k in range(CB):
                        ins = nc.tensor.matmul(ps[:, 2, 0:w], ones[:], cacc[:, k, a:a + w], start=k == 0, stop=k == CB - 1)
                    ins.then_inc(mean_ps, 1)
                    if n:
                        pe.wait_ge(var_ok, lb)
                    for k in range(CB):
                        pe.wait_ge(sq_ok, CB * lb + k + 1)
                        ins = nc.tensor.matmul(ps[:, 3, 0:w], ones[:], csq[:, k, a:a + w], start=k == 0, stop=k == CB - 1)
                    ins.then_inc(var_ps, 1)
                npc = len(conv_pieces(c))
                pe.wait_ge(c_lo, CB * (c + npc))
                pe.wait_ge(kqT_ok, 2 * (kq0 + 2 * nt))
                for m in range(CB):
                    for n, (a, q0, w) in enumerate(conv_pieces(c)):
                        ev = npc * m + n
                        if ev >= 4:
                            pe.wait_ge(pw_lo, CB * c + ev - 3)
                        for k in range(CB):
                            if m == 0 and n == 0:
                                pe.wait_ge(lo_done, 4 * (GROUPS * c + G_PW) + k + 1)
                            wh, wl = slab(G_PW, k)
                            ins = mm3(ps[:, ev % 4, 0:w], (wh[:, m * P:(m + 1) * P], wl[:, m * P:(m + 1) * P]),
                                      (cT_hi[:, k, a:a + w], cT_lo[:, k, a:a + w]), k == 0, k == CB - 1)
                        ins.then_inc(pw_ps, 1)
                pe.wait_ge(pw_lo, CB * (c + npc))
                if c == NC - 1:
                    pe.wait_ge(cvo_ok, 2)
                for kind, pairs in passes(c):
                    before, cn = att_counts(c, kind)
                    seq = att_sequence(pairs)
                    npair = len(pairs)
                    loads = 16 * (5 if kind == 0 else 6)
                    loaded = 16 * 5 * (NH // 2) * (c + kind)

                    def heads(it):
                        def cnt(what, n):
                            return before[what] + it * cn[what] + n

                        def scores(k):
                            head, (p, t, q0, r, a0, n, diag, last), m, tg = seq[k]
                            if k == 0 or seq[k - 1][0] != head:
                                pe.wait_ge(at_in[head], loaded + loads + it * loads)
                            if k >= 2:
                                pe.wait_ge(s_scan, cnt("z", k - 1))
                            for x in range(0, n, BANK):
                                w = min(BANK, n - x)
                                for v in range(2):
                                    ins = nc.tensor.matmul(ps[0:r, 2 * (k % 2) + x // BANK, 0:w], a_q[head][:, v, q0:q0 + r],
                                                           a_k[head][:, a0 + x:a0 + x + w], start=v == 0, stop=v == 1)
                            ins.then_inc(z_ps, 1)

                        def turn(k):
                            head, (p, t, q0, r, a0, n, diag, last), m, tg = seq[k]
                            if diag:
                                pe.wait_ge(s_am, cnt("m", m + 1))
                            else:
                                pe.wait_ge(s_a, cnt("z", k + 1))
                            for gi, grp in enumerate(key_groups(a0, n)):
                                if tg + gi >= 2:
                                    pe.wait_ge(t_lo, cnt("t", tg + gi - 1))
                                for x, (blk, w) in enumerate(grp):
                                    s0 = blk * P - a0
                                    ins = nc.tensor.transpose(ps[0:w, 4 + (tg + gi) % 2, x * r:(x + 1) * r],
                                                              sc[k % 3][0:r, s0:s0 + w], ident[0:r, 0:r])
                                ins.then_inc(t_ps, 1)
                            if last and t == len(pairs[p]) - 1:
                                ob = head * npair + p
                                pe.wait_ge(t_lo, cnt("t", tg + len(key_groups(a0, n))))
                                pe.wait_ge(o_lo, cnt("o", max(ob - 1, 0)) + 1)
                                blocks = [b for g2 in key_groups(0, pairs[p][-1][2]) for b in g2]
                                width = sum(x[1] for x in pairs[p])
                                for blk, w in blocks:
                                    first = 0
                                    while pairs[p][first][2] <= blk * P:
                                        first += 1
                                    c0 = first * P
                                    for v, src in enumerate((aT_hi, aT_lo)):
                                        ins = nc.tensor.matmul(ps[:, 6 + ob % 2, c0:width], a_v[head][0:w, blk, :],
                                                               src[0:w, blk, c0:width], start=blk == 0 and v == 0,
                                                               stop=(blk, w) == blocks[-1] and v == 1)
                                ins.then_inc(o_ps, 1)

                        for k in range(len(seq) + 2):
                            if k < len(seq):
                                scores(k)
                            if k >= 2:
                                turn(k - 2)

                    if kind == 0:
                        with pe.Fori(0, NH // 2) as it:
                            heads(it)
                    else:
                        for it in range(NH // 2):
                            heads(it)
                pe.wait_ge(o_lo, att_outputs(c) + 1)
                for hf in range(2):
                    g = G_OUT + hf
                    for i, (q0, r) in enumerate(tl):
                        ev = hf * nt + i
                        if ev >= 4:
                            pe.wait_ge(out_add, 8 * c + ev - 3)
                        for k in range(KD):
                            if i == 0 and k % 2 == 0:
                                pe.wait_ge(lo_done, 4 * (GROUPS * c + g) + k // 2 + 1)
                            wh, wl = slab(g, k // 2)
                            c0 = (k % 2) * BANK
                            nc.tensor.matmul(ps[0:r, 4 + ev % 4, :], mixT_hi[:, k, q0:q0 + r], wh[:, c0:c0 + BANK], start=k == 0, stop=False)
                            nc.tensor.matmul(ps[0:r, 4 + ev % 4, :], mixT_lo[:, k, q0:q0 + r], wh[:, c0:c0 + BANK], start=False, stop=False)
                            ins = nc.tensor.matmul(ps[0:r, 4 + ev % 4, :], mixT_hi[:, k, q0:q0 + r], wl[:, c0:c0 + BANK],
                                                   start=False, stop=k == KD - 1)
                        ins.then_inc(out_ps, 1)
                norm(c, 1)
                pe.wait_ge(n_lo, 2 * (norm_base(c, 1) + nt))
                with pe.Fori(0, FFE) as e:
                    f1b = 4 * FFE * c
                    f2b = 8 * FFE * c
                    for j in range(4):
                        pe.wait_ge(lo_done, 4 * (GROUPS * c + G_FF) + 8 * e + j + 1)
                        wh, wl = slab(G_FF, j)
                        for s, (s0, w) in enumerate(sp_):
                            ev = j * ns + s
                            if ev >= 4:
                                pe.wait_ge(f_rel, f1b + ev - 3 + e * 4 * ns)
                            for k in range(KD):
                                ins = mm3(ps[:, ev % 4, 0:w], (wh[:, k * P:(k + 1) * P], wl[:, k * P:(k + 1) * P]),
                                          (hT_hi[:, k, s0:s0 + w], hT_lo[:, k, s0:s0 + w]), k == 0, k == KD - 1)
                            ins.then_inc(f1_ps, 1)
                    for ev in range(2 * nt):
                        i, hf = ev // 2, ev % 2
                        q0, r = tl[i]
                        if ev >= 4:
                            pe.wait_ge(f2_add, f2b + ev - 3 + e * 2 * nt)
                        for k in range(4):
                            if ev == 0:
                                pe.wait_ge(f_lo, f1b + (k + 1) * ns + e * 4 * ns)
                                pe.wait_ge(lo_done, 4 * (GROUPS * c + G_FF + 1) + 8 * e + k + 1)
                            wh, wl = slab(G_FF + 1, k)
                            o = ps[0:r, 4 + ev % 4, :]
                            c0 = hf * BANK
                            nc.tensor.matmul(o, hid_hi[:, k, q0:q0 + r], wh[:, c0:c0 + BANK], start=k == 0, stop=False)
                            nc.tensor.matmul(o, hid_lo[:, k, q0:q0 + r], wh[:, c0:c0 + BANK], start=False, stop=False)
                            ins = nc.tensor.matmul(o, hid_hi[:, k, q0:q0 + r], wl[:, c0:c0 + BANK], start=False, stop=k == 3)
                        ins.then_inc(f2_ps, 1)


_INS = ["x_prompt", "x_sample", "cache_k", "cache_v", "state_conv", "g_mix", "w_in", "w_dw", "b_dw", "g_cn", "b_cn",
        "w_pw", "g_q", "g_k", "w_out", "g_ff", "w_ff1", "w_ff2"]
_OUTS = [(1, SEQ, D), (1, DEC, D), (1, 1, SEQ, NH, HD), (1, 1, SEQ, NH, HD), (1, 1, HIST, CC),
         (1, 1, DEC, NH, HD), (1, 1, DEC, NH, HD), (1, 1, HIST, CC)]


def kernel(**inputs):
    import numpy as np
    import concourse.bacc as bacc
    from concourse.bass_utils import run_bass_kernel_spmd

    nc = bacc.Bacc("TRN2", target_bir_lowering=False, num_devices=1)
    arrays, args = {}, []
    for name in _INS:
        a = np.ascontiguousarray(inputs[name])
        arrays[f"in_{name}"] = a
        args.append(nc.dram_tensor(f"in_{name}", a.shape, mybir.dt.from_np(a.dtype), kind="ExternalInput").ap())
    for i, shape in enumerate(_OUTS):
        args.append(nc.dram_tensor(f"out_{i}", shape, F32, kind="ExternalOutput").ap())
    build(nc, *args)
    r = run_bass_kernel_spmd(nc, [arrays], core_ids=[0])
    return tuple(r.results[0][f"out_{i}"] for i in range(len(_OUTS)))
```

```python
import concourse.bass as bass
from concourse import mybir
from collections import namedtuple
from contextlib import ExitStack

F32 = mybir.dt.float32
F32R = mybir.dt.float32r
ALU = mybir.AluOpType
ACT = mybir.ActivationFunctionType
AX = mybir.AxisListType

P = 128
D = 1024
KD = D // P
SEQ, DEC, PAST = 2048, 64, 128
NH, HD = 8, 64
AW = NH * HD
CC, CW = 512, 31
CB = CC // P
HIST = CW - 1
FF = 4096
EPS = 1e-6
BANK = 512
CHUNK = 512
NC = SEQ // CHUNK
TMAX = CHUNK + DEC
SLAB = 1024
RAW = 4
RING = 8
GROUPS = 24
G_AG, G_K, G_V, G_Q, G_PW, G_OUT, G_FF = 0, 2, 3, 4, 5, 6, 8
FFE = FF // P // 4
SMP = CHUNK + HIST
CVW = SMP + DEC
NO_LIMIT, EXCLUDED = 3e38, -1e4


def tiles(c):
    t = [(P * i, P) for i in range(CHUNK // P)]
    return t + [(CHUNK, DEC)] if c == NC - 1 else t


def splits(c):
    return [(0, TMAX // 2), (TMAX // 2, TMAX // 2)] if c == NC - 1 else [(0, CHUNK)]


def conv_pieces(c):
    return [(0, 0, CHUNK)] + ([(SMP, CHUNK, DEC)] if c == NC - 1 else [])


def passes(c):
    prompt = [[(P * i, P, CHUNK * c + P * (i + 1)) for i in (2 * p, 2 * p + 1)] for p in range(2)]
    out = [(0, prompt)]
    if c == NC - 1:
        out.append((1, [[(0, DEC, PAST + DEC)]]))
    return out


Piece = namedtuple("Piece", "head p t q0 r a0 n diag last ends m x tg v ob")


def key_groups(a, n):
    blocks = [((a + x) // P, min(P, n - x)) for x in range(0, n, P)]
    return [blocks[x:x + 4] for x in range(0, len(blocks), 4)]


def round_heads(kind):
    return NH if kind else 2


def att_sequence(kind, pairs):
    seq, m, x, tg, v = [], 0, 0, 0, 0
    for head in range(round_heads(kind)):
        for p, pair in enumerate(pairs):
            parts = [(SLAB, 2 * SLAB), (0, SLAB)] if pair[0][2] > SLAB else [(0, SLAB)]
            for part, (a, b) in enumerate(parts):
                for t, (q0, r, keys) in enumerate(pair):
                    n = min(keys, b) - a
                    diag, last, ends = part == 0, part == len(parts) - 1, t == len(pair) - 1
                    seq.append(Piece(head, p, t, q0, r, a, n, diag, last, ends, m, x, tg, v, head * len(pairs) + p))
                    m += diag
                    x += not last
                    tg += len(key_groups(a, n))
                    v += ends
    return seq


def behind(k, delay, pieces, first):
    j = k - delay
    if j < 0:
        return None if first else (-1, j + pieces)
    return (0, j) if j < pieces else None


def build(nc, x_prompt, x_sample, cache_k, cache_v, state_conv, g_mix, w_in, w_dw, b_dw, g_cn, b_cn, w_pw,
          g_q, g_k, w_out, g_ff, w_ff1, w_ff2, y_prompt, y_sample, nk_prompt, nv_prompt, ncv_prompt,
          nk_sample, nv_sample, ncv_sample):
    ctx = ExitStack()
    with ctx:
        base = (nc.sbuf_base + 31) // 32 * 32
        at = [base]

        def place(name, shape, dt=F32, offset=None):
            n = 4
            for s in shape[1:]:
                n *= s
            if offset is None:
                offset = at[0]
                at[0] += (n + 31) // 32 * 32
            return nc.alloc_sbuf_tensor_at(name, shape, dt, offset=offset)

        o_w = at[0]
        half = 2 * 4 * SLAB * 4
        at[0] += 2 * half
        w_hi = [place(f"w_hi{g}", [P, 4, SLAB], F32R, o_w + g * half) for g in range(2)]
        w_lo = [place(f"w_lo{g}", [P, 4, SLAB], F32R, o_w + g * half + half // 2) for g in range(2)]
        o_raw = at[0]
        w_raw = place("w_raw", [P, RAW, SLAB])
        resid = place("resid", [P, 5, D])
        o_h = at[0]
        hT_hi = place("hT_hi", [P, KD, TMAX], F32R)
        hT_lo = place("hT_lo", [P, KD, TMAX], F32R)
        o_mix = at[0]
        mixT_hi = place("mixT_hi", [P, KD, TMAX], F32R)
        mixT_lo = place("mixT_lo", [P, KD, TMAX], F32R)
        uT = place("uT", [P, CB, SMP + HIST + DEC])
        o_cv = at[0]
        cacc = place("cacc", [P, CB, CVW])
        cT_lo = place("cT_lo", [P, CB, CVW], F32R, o_cv)
        o_ch = at[0]
        cT_hi = place("cT_hi", [P, CB, CVW], F32R)
        o_grow = at[0]
        g_row = place("g_row", [P, D])
        vecs = place("vecs", [P, CB, CW + 3])
        gq = place("gq", [P, HD])
        gk = place("gk", [P, HD])
        ident = place("ident", [P, P])
        ones = place("ones", [P, P])
        neghalf = place("neghalf", [P, 1])
        ssum = place("ssum", [P, 5])
        rstd = place("rstd", [P, 5])
        hss = place("hss", [P, 2, NH])
        hrs = place("hrs", [P, 2, NH])
        limit = place("limit", [P, P])
        xn = place("xn", [P, 2, D], offset=o_cv)
        kqT = place("kqT", [P, NH, TMAX], F32R, o_mix)
        o_t = o_mix + NH * TMAX * 4
        raw_kq = place("raw_kq", [P, 2, AW], offset=o_t)
        sqr = place("sqr", [P, AW], offset=o_t + 4096)
        kn = place("kn", [P, 2, AW], offset=o_t + 6144)
        packed = place("packed", [P, 2, NH, P], F32R, o_t + 10240)
        vout = place("vout", [P, 2, AW], offset=o_ch)
        vpack_o = o_ch + 4096
        vpack = place("vpack", [P, NH, P], F32R, vpack_o)
        sgate = place("sgate", [P, 2, BANK], offset=o_t)
        csq = place("csq", [P, CB, CVW], offset=o_ch)
        lnv = place("lnv", [P, BANK], offset=o_t)
        lnr = place("lnr", [P, BANK], offset=o_t + 2048)
        ntmp = place("ntmp", [P, BANK], offset=o_t + 4096)
        csig = place("csig", [P, 2, BANK], offset=o_t + 4096)
        cid = place("cid", [P, 2, BANK], offset=o_t + 8192)
        cvout = place("cvout", [HIST, 2, CC], offset=o_t + 12288)
        hid_hi = place("hid_hi", [P, 4, TMAX], F32R, o_cv)
        hid_lo = place("hid_lo", [P, 4, TMAX], F32R, o_cv + 4 * TMAX * 4)
        frel = place("frel", [P, 2, BANK], offset=o_mix)
        fsq = place("fsq", [P, 2, BANK], offset=o_mix + 4096)
        KB, VB, QB = SEQ * 4, (SEQ // P) * P * 4, 2 * CHUNK * 4
        a_k = [place(f"a_k{b}", [P, SEQ], F32R, o_h + b * KB) for b in range(2)]
        a_v = [place(f"a_v{b}", [P, SEQ // P, P], F32R, o_h + 2 * KB + b * VB) for b in range(2)]
        a_q = [place("a_q0", [P, 2, CHUNK], F32R, o_h + 2 * KB + 2 * VB),
               place("a_q1", [P, 2, CHUNK], F32R, o_grow)]
        beta = [place(f"beta{i}", [P, SLAB], F32, o_raw + i * SLAB * 4) for i in range(4)]
        stay = [place(f"stay{i}", [P, SLAB], F32, o_cv + i * SLAB * 4) for i in range(4)]
        aT_hi = place("aT_hi", [P, SEQ // P, 2 * P], F32R, o_w + half)
        aT_lo = place("aT_lo", [P, SEQ // P, 2 * P], F32R, o_w + half + half // 2)
        osb = place("osb", [P, 2 * P], offset=o_cv + 4 * SLAB * 4)
        of = place("of", [P, 2 * P], offset=o_cv + 4 * SLAB * 4 + 1024)
        crow = place("crow", [CW + 3, CC], offset=o_t)
        srow = place("srow", [HIST, CC], offset=o_t + 2048)

        ps = ctx.enter_context(nc.psum_tensor("ps", [P, 8, BANK], F32))

        k_d = nc.dram_tensor("k_scratch", [NH, P, SEQ], F32).ap()
        v_d = nc.dram_tensor("v_scratch", [NH, P, SEQ // P, P], F32).ap()
        q_d = nc.dram_tensor("q_scratch", [NH, P, SEQ + DEC], F32).ap()
        ks_d = nc.dram_tensor("ks_scratch", [NH, P, PAST + DEC], F32).ap()
        vs_d = nc.dram_tensor("vs_scratch", [NH, P, 2, P], F32).ap()

        def sem(name):
            return ctx.enter_context(nc.semaphore(name))

        raw_in = [sem(f"raw_in{j}") for j in range(RAW)]
        hi_done, lo_done = sem("hi_done"), sem("lo_done")
        consts, rows_in, vec_t, vec_ok, ch_start, gains_in = (sem(n) for n in (
            "consts", "rows_in", "vec_t", "vec_ok", "ch_start", "gains_in"))
        ck_in, cv_in, ck_hi, ck_lo, cv_hi, cv_lo, ckT_ps, ckT_ok, cache_out = (sem(n) for n in (
            "ck_in", "cv_in", "ck_hi", "ck_lo", "cv_hi", "cv_lo", "ckT_ps", "ckT_ok", "cache_out"))
        x_in = [sem(f"x_in{i}") for i in range(5)]
        grow_in, n_ss, n_var, n_rstd, n_xn, n_tp, n_hi, n_lo = (sem(n) for n in (
            "grow_in", "n_ss", "n_var", "n_rstd", "n_xn", "n_tp", "n_hi", "n_lo"))
        ag_ps, ag_sig, ag_u, hist_ok, taps = (sem(n) for n in ("ag_ps", "ag_sig", "ag_u", "hist_ok", "taps"))
        kvq_ps, kvq_cp, kq_sq, kq_ss, kq_var, kq_rs, kq_mul, kq_n, pk_hi, pk_lo, v_lo, kqT_ps, kqT_ok = (sem(n) for n in (
            "kvq_ps", "kvq_cp", "kq_sq", "kq_ss", "kq_var", "kq_rs", "kq_mul", "kq_n", "pk_hi", "pk_lo", "v_lo",
            "kqT_ps", "kqT_ok"))
        kn_out = [sem(f"kn_out{i}") for i in range(2)]
        vo_out = [sem(f"vo_out{i}") for i in range(2)]
        vp_out, kT_out, qT_out = sem("vp_out"), sem("kT_out"), sem("qT_out")
        sd_ok, nwt = sem("sd_ok"), sem("nwt")
        mean_ps, xc_ok, sq_ok, var_ps, var_ok, lnr_ok, yn_ok, sg_ok, cm_ok, c_hi, c_lo, cvo_ps, cvo_ok, cvo_out = (
            sem(n) for n in ("mean_ps", "xc_ok", "sq_ok", "var_ps", "var_ok", "lnr_ok", "yn_ok", "sg_ok", "cm_ok",
                             "c_hi", "c_lo", "cvo_ps", "cvo_ok", "cvo_out"))
        pw_ps, pw_hi, pw_lo, out_ps, out_add = (sem(n) for n in ("pw_ps", "pw_hi", "pw_lo", "out_ps", "out_add"))
        at_in = [sem(f"at_in{b}") for b in range(2)]
        z_ps, z_msk, s_sg, s_scan, s_a, t_ps, t_hi, t_lo, v_ps, o_cp, o_sum, o_hi, o_lo = (
            sem(n) for n in ("z_ps", "z_msk", "s_sg", "s_scan", "s_a", "t_ps", "t_hi", "t_lo", "v_ps", "o_cp", "o_sum", "o_hi", "o_lo"))
        f1_ps, f_rel, f_sq, f_hi, f_lo, f2_ps, f2_add = (sem(n) for n in (
            "f1_ps", "f_rel", "f_sq", "f_hi", "f_lo", "f2_ps", "f2_add"))
        y_out = [sem(f"y_out{i}") for i in range(5)]

        def norm_base(c, which):
            return 2 * 4 * c + which * len(tiles(c))

        def att_counts(c, kind):
            before = dict(z=0, m=0, x=0, t=0, v=0, o=0)
            for cc in range(NC):
                for k, pairs in passes(cc):
                    seq = att_sequence(k, pairs)
                    n = dict(z=len(seq), m=sum(q.diag for q in seq), 
                             x=sum(not q.last for q in seq), t=sum(len(key_groups(q.a0, q.n)) for q in seq),
                             v=sum(q.ends for q in seq), o=seq[-1].ob + 1)
                    if (cc, k) == (c, kind):
                        return before, n
                    for key in before:
                        before[key] += n[key] * NH // round_heads(k)
            return before, None

        def att_counter(c, kind):
            before, cn = att_counts(c, kind)

            def cnt(what, n, it, rel):
                return it * cn[what] + (before[what] + rel * cn[what] + n)
            return cnt

        def turned(q):
            return q.tg + len(key_groups(q.a0, q.n))

        def aT_blocks(q, grp):
            return [(b - q.a0 // P + KD * (q.v % 2), w) for b, w in grp]

        def kvq_events(c):
            nt = len(tiles(c))
            return ([("k", i, i) for i in range(nt)] + [("v", i, None) for i in range(nt)]
                    + [("q", i, nt + i) for i in range(nt)])

        TAPS = CB * CW

        def taps_of(c, e):
            n = len(kvq_events(c))
            return range(TAPS * e // n, TAPS * (e + 1) // n)

        def evacuate(copy, sub, dst, grp, t, r, bank, done):
            w0 = grp[0][1]
            b0, n = grp[0][0], len(grp)
            same = [x for x in grp if x[1] == w0]
            parts = [(b0, len(same), w0, 0)]
            if len(same) < n:
                parts.append((b0 + len(same), 1, grp[-1][1], len(same)))
            for q, (b, m, w, k0) in enumerate(parts):
                o = dst[0:w, b:b + m, t * P:t * P + r]
                i = bank[0:w, k0 * r:(k0 + m) * r].rearrange("p (a b) -> p a b", a=m)
                ins = copy(o, i) if sub is None else copy(o, i, sub[0:w, b:b + m, t * P:t * P + r].bitcast(F32), ALU.subtract)
                if q == len(parts) - 1:
                    ins.then_inc(done, 1)

        def bank(k, r, x0, x1):
            return ps[0:r, 2 * (k % 2):2 * (k % 2) + 2, :].rearrange("p a b -> p (a b)")[:, x0:x1]

        block = ctx.enter_context(nc.Block())

        def att_outputs(c):
            kind = passes(c)[-1][0]
            before, n = att_counts(c, kind)
            return before["o"] + n["o"] * NH // round_heads(kind)

        @block.sync
        def _(sp):
            def load_slab(slab, src, width=None):
                j = slab % RAW
                if not isinstance(slab, int) or slab >= RAW:
                    sp.wait_ge(lo_done, slab - RAW + 1)
                dst = w_raw[:, j, :] if width is None else w_raw[:, j, 0:width]
                if len(src.shape) == 3:
                    dst = dst.rearrange("p (a b) -> p a b", a=src.shape[1])
                sp.dma_start(dst, src).then_inc(raw_in[j], 16)

            w_in_k = w_in[0].rearrange("(k p) n -> p k n", p=P)
            w_out_k = w_out[0].rearrange("(k p) n -> p k n", p=P)
            w_pw_k = w_pw[0].rearrange("(k p) n -> p k n", p=P)
            w1_k = w_ff1[0].rearrange("(k p) n -> p k n", p=P)
            w2_k = w_ff2[0].rearrange("(k p) n -> p k n", p=P)

            def load_group(c, g):
                if c >= NC:
                    return
                for j in range(4):
                    slab = 4 * (GROUPS * c + g) + j
                    if g < G_K:
                        col = (j % 2) * CC + (2 * g + j // 2) * P
                        src = w_in_k[:, :, col:col + P]
                    elif g <= G_Q:
                        col = 2 * CC + {G_K: 1, G_V: 2, G_Q: 0}[g] * AW
                        src = w_in_k[:, 2 * j:2 * j + 2, col:col + AW]
                    elif g == G_PW:
                        src = w_pw_k[:, j, :]
                    elif g < G_FF:
                        hf = g - G_OUT
                        src = w_out_k[:, 2 * j:2 * j + 2, hf * BANK:(hf + 1) * BANK]
                    load_slab(slab, src, CC if g == G_PW else None)

            def load_ff1(c, e):
                for j in range(4):
                    col = 4 * e + j
                    sl = bass.ts(col, P)
                    n = 4 * (GROUPS * c + G_FF) + 8 * e + j
                    sp.wait_ge(lo_done, n - RAW + 1)
                    sp.dma_start(w_raw[:, j, :].rearrange("p (a b) -> p a b", a=KD),
                                 w1_k[:, :, sl]).then_inc(raw_in[j], 16)

            def load_ff2(c, e):
                for j in range(4):
                    n = 4 * (GROUPS * c + G_FF + 1) + 8 * e + j
                    sp.wait_ge(lo_done, n - RAW + 1)
                    sp.dma_start(w_raw[:, j, :], w2_k[:, 4 * e + j, :]).then_inc(raw_in[j], 16)

            def load_gain(c, which):
                g = (g_mix if which == 0 else g_ff)[0:1, :]
                if c or which:
                    sp.wait_ge(n_xn, norm_base(c, which))
                sp.dma_start(g_row[:], g.partition_broadcast(P)[:, 0, :]).then_inc(grow_in, 16)

            sp.dma_start(crow[0:CW, :], w_dw[0]).then_inc(rows_in, 16)
            sp.dma_start(crow[CW:CW + 1, :], b_dw[0:1, :]).then_inc(rows_in, 16)
            sp.dma_start(crow[CW + 1:CW + 2, :], g_cn[0:1, :]).then_inc(rows_in, 16)
            sp.dma_start(crow[CW + 2:CW + 3, :], b_cn[0:1, :]).then_inc(rows_in, 16)
            sp.dma_start(srow[:], state_conv[0, 0]).then_inc(rows_in, 16)
            sp.dma_start(gq[:], g_q[0:1, :].partition_broadcast(P)[:, 0, :]).then_inc(gains_in, 16)
            sp.dma_start(gk[:], g_k[0:1, :].partition_broadcast(P)[:, 0, :]).then_inc(gains_in, 16)
            sp.dma_start(kn[:, 0, :], cache_k[0, 0].rearrange("t h d -> t (h d)")).then_inc(ck_in, 16)
            sp.dma_start(vout[:, 0, :], cache_v[0, 0].rearrange("t h d -> t (h d)")).then_inc(cv_in, 16)
            for c in range(NC):
                tl = tiles(c)
                nt = len(tl)
                t0 = c * CHUNK
                for i, (q0, r) in enumerate(tl):
                    if c and i < 4:
                        sp.wait_ge(y_out[i], 16 * c)
                    src = x_prompt[0, t0 + q0:t0 + q0 + r, :] if i < 4 else x_sample[0]
                    sp.dma_start(resid[0:r, i, :], src).then_inc(x_in[i], 16)
                load_gain(c, 0)
                if c == 0:
                    load_group(0, 0)
                    load_group(0, 1)
                    sp.wait_ge(ckT_ok, 2)
                    sp.dma_start(ks_d[:, :, 0:PAST].rearrange("h p k -> p h k"),
                                 kqT[:, :, 0:PAST].bitcast(F32)).then_inc(cache_out, 16)
                    sp.wait_ge(cv_lo, 1)
                    sp.dma_start(vs_d[:, :, 0, :].rearrange("h p k -> p h k"), vpack[:].bitcast(F32)).then_inc(cache_out, 16)
                load_group(c, 2)
                load_group(c, 3)
                kq0 = 2 * 4 * c
                for s, (sec, i, m) in enumerate(kvq_events(c)):
                    q0, r = tl[i]
                    if sec == "k":
                        sp.wait_ge(kq_n, kq0 + m + 1)
                        dst = nk_prompt[0, 0, t0 + q0:t0 + q0 + r] if i < 4 else nk_sample[0, 0]
                        sp.dma_start(dst.rearrange("t h d -> t (h d)"), kn[0:r, m % 2, :]).then_inc(kn_out[m % 2], 16)
                        if i == 1:
                            load_group(c, G_Q)
                    elif sec == "v":
                        sp.wait_ge(v_lo, 4 * c + i + 1)
                        dst = nv_prompt[0, 0, t0 + q0:t0 + q0 + r] if i < 4 else nv_sample[0, 0]
                        sp.dma_start(dst.rearrange("t h d -> t (h d)"), vout[0:r, i % 2, :]).then_inc(vo_out[i % 2], 16)
                        dst = (v_d[:, :, 4 * c + i, :] if i < 4 else vs_d[:, 0:r, 1, :]).rearrange("h p k -> p h k")
                        sp.dma_start(dst, vpack[0:r].bitcast(F32)).then_inc(vp_out, 16)
                        if i == 1:
                            sp.wait_ge(kqT_ok, 2 * (kq0 + nt))
                            sp.dma_start(k_d[:, :, t0:t0 + CHUNK].rearrange("h p k -> p h k"),
                                         kqT[:, :, 0:CHUNK].bitcast(F32)).then_inc(kT_out, 16)
                            if c == NC - 1:
                                sp.dma_start(ks_d[:, :, PAST:PAST + DEC].rearrange("h p k -> p h k"),
                                             kqT[:, :, CHUNK:TMAX].bitcast(F32)).then_inc(kT_out, 16)
                        if i == 2:
                            load_group(c, G_PW)
                sp.wait_ge(kqT_ok, 2 * (kq0 + 2 * nt))
                T = tl[-1][0] + tl[-1][1]
                sp.dma_start(q_d[:, :, t0:t0 + T].rearrange("h p k -> p h k"),
                             kqT[:, :, 0:T].bitcast(F32)).then_inc(qT_out, 16)
                load_group(c, G_OUT)
                if c == NC - 1:
                    sp.wait_ge(cvo_ok, 2)
                    sp.dma_start(ncv_prompt[0, 0], cvout[:, 0, :]).then_inc(cvo_out, 16)
                    sp.dma_start(ncv_sample[0, 0], cvout[:, 1, :]).then_inc(cvo_out, 16)
                sp.wait_ge(kT_out, 16 * (c + 1 + (c == NC - 1)))
                sp.wait_ge(vp_out, 16 * (4 * c + nt))
                sp.wait_ge(qT_out, 16 * (c + 1))
                sp.wait_ge(cache_out, 32)
                sp.wait_ge(kvq_ps, 3 * (4 * c + nt))
                sp.wait_ge(pw_lo, CB * (c + len(conv_pieces(c))))
                for kind, pairs in passes(c):
                    cnt = att_counter(c, kind)
                    before, n = att_counts(c, kind)

                    def load_head(it, b):
                        h = 2 * it + b
                        k_b, v_b, q_b, done = a_k[b], a_v[b], a_q[b], at_in[b]
                        nk = CHUNK * (c + 1)
                        sp.dma_start(k_b[:, 0:nk].bitcast(F32), k_d[h, :, 0:nk]).then_inc(done, 16)
                        sp.dma_start(q_b[:, 0, :].bitcast(F32), q_d[h, :, t0:t0 + CHUNK]).then_inc(done, 16)
                        for p0 in (0, HD):
                            sp.dma_start(q_b[p0:p0 + HD, 1, :].bitcast(F32),
                                         q_d[h, HD - p0:P - p0, t0:t0 + CHUNK]).then_inc(done, 16)
                        sp.dma_start(v_b[:, 0:nk // P, :].bitcast(F32), v_d[h, :, 0:nk // P, :]).then_inc(done, 16)

                    def load_running():
                        done = at_in[0]
                        sp.dma_start(a_k[0][:, 0:NH * (PAST + DEC)].bitcast(F32).rearrange("p (h k) -> p h k", h=NH),
                                     ks_d.rearrange("h p k -> p h k")).then_inc(done, 16)
                        qv = [a_q[0][:, v, :].bitcast(F32).rearrange("p (h k) -> p h k", h=NH) for v in range(2)]
                        sp.dma_start(qv[0], q_d[:, :, SEQ:SEQ + DEC].rearrange("h p k -> p h k")).then_inc(done, 16)
                        for p0 in (0, HD):
                            sp.dma_start(qv[1][p0:p0 + HD],
                                         q_d[:, HD - p0:P - p0, SEQ:SEQ + DEC].rearrange("h p k -> p h k")).then_inc(done, 16)
                        for b, rows in ((0, P), (1, DEC)):
                            sp.dma_start(a_v[0][0:rows, b:2 * NH:2, :].bitcast(F32),
                                         vs_d[:, 0:rows, b, :].rearrange("h p k -> p h k")).then_inc(done, 16)

                    if kind == 0:
                        sp.wait_ge(o_lo, before["o"] + 1)
                        for b in range(2):
                            load_head(0, b)
                        with sp.Fori(1, NH // 2) as it:
                            for b in range(2):
                                sp.wait_ge(v_ps, cnt("v", (b + 1) * (n["v"] // 2), it, -1))
                                load_head(it, b)
                        slot0_free = cnt("v", n["v"] // 2, NH // 2 - 1, 0)
                    else:
                        sp.wait_ge(v_ps, slot0_free)
                        load_running()
                sp.wait_ge(o_lo, att_outputs(c) + 1)
                load_group(c, G_OUT + 1)
                load_gain(c, 1)
                load_ff1(c, 0)
                with sp.Fori(0, FFE - 1) as e:
                    load_ff2(c, e)
                    load_ff1(c, e + 1)
                load_ff2(c, FFE - 1)
                load_group(c + 1, 0)
                load_group(c + 1, 1)
                for i, (q0, r) in enumerate(tl):
                    sp.wait_ge(f2_add, 2 * (4 * c * FFE + (FFE - 1) * nt + i + 1))
                    dst = y_prompt[0, t0 + q0:t0 + q0 + r, :] if i < 4 else y_sample[0]
                    sp.dma_start(dst, resid[0:r, i, :]).then_inc(y_out[i], 16)
            for i in range(4):
                sp.wait_ge(y_out[i], 16 * NC)
            sp.wait_ge(y_out[4], 16)
            sp.wait_ge(kn_out[0], 16 * (2 * NC + 1))
            sp.wait_ge(kn_out[1], 16 * 2 * NC)
            sp.wait_ge(vo_out[0], 16 * (2 * NC + 1))
            sp.wait_ge(vo_out[1], 16 * 2 * NC)
            sp.wait_ge(cvo_out, 32)

        @block.gpsimd
        def _(pool):
            def split_lo(c, g, j, width=SLAB):
                n = 4 * (GROUPS * c + g) + j
                pool.wait_ge(hi_done, n + 1)
                nc.gpsimd.tensor_tensor(w_lo[g % 2][:, j, 0:width], w_raw[:, j, 0:width],
                                        w_hi[g % 2][:, j, 0:width].bitcast(F32), ALU.subtract).then_inc(lo_done, 1)

            def split_lo_group(c, g):
                if g == GROUPS:
                    c, g = c + 1, 0
                if c < NC:
                    for j in range(4):
                        split_lo(c, g, j, CC if g == G_PW else SLAB)

            def norm(c, which):
                nb = norm_base(c, which)
                for i, (q0, r) in enumerate(tiles(c)):
                    pool.wait_ge(n_ss, nb + i + 1)
                    if i == 0 and nb:
                        pool.wait_ge(n_xn, nb)
                    nc.gpsimd.tensor_scalar(rstd[0:r, i:i + 1], ssum[0:r, i:i + 1], 1.0 / D, EPS,
                                            ALU.mult, ALU.add).then_inc(n_var, 1)
                    pool.wait_ge(n_var, nb + i + 1)
                    nc.gpsimd.tensor_tensor(rstd[0:r, i:i + 1], rstd[0:r, i:i + 1], neghalf[0:r, :],
                                            ALU.pow).then_inc(n_rstd, 1)

            nc.gpsimd.memset(ident[:], 0.0).then_inc(consts, 1)
            nc.gpsimd.memset(ones[:], 1.0).then_inc(consts, 1)
            nc.gpsimd.memset(neghalf[:], -0.5).then_inc(consts, 1)
            pool.wait_ge(consts, 3)
            nc.gpsimd.affine_select(out=ident[:], in_=ident[:], compare_op=ALU.not_equal, fill=1.0, base=0,
                                    pattern=[[-1, P]], channel_multiplier=1).then_inc(consts, 1)
            nc.gpsimd.memset(limit[:], NO_LIMIT).then_inc(consts, 1)
            pool.wait_ge(consts, 5)
            nc.gpsimd.affine_select(out=limit[:], in_=limit[:], compare_op=ALU.is_gt, fill=EXCLUDED, base=0,
                                    pattern=[[-1, P]], channel_multiplier=1).then_inc(consts, 1)
            for c in range(NC):
                nt = len(tiles(c))
                if c == 0:
                    split_lo_group(0, 0)
                norm(c, 0)
                split_lo_group(c, 1)
                split_lo_group(c, 2)
                kq0 = 8 * c
                for s, (sec, i, m) in enumerate(kvq_events(c)):
                    if m is not None:
                        u = kq0 + m
                        rr = tiles(c)[i][1]
                        pool.wait_ge(kq_ss, u + 1)
                        nc.gpsimd.tensor_scalar(hrs[0:rr, m % 2, :], hss[0:rr, m % 2, :], 1.0 / HD, EPS,
                                                ALU.mult, ALU.add).then_inc(kq_var, 1)
                        pool.wait_ge(kq_var, u + 1)
                        nc.gpsimd.tensor_tensor(hrs[0:rr, m % 2, :], hrs[0:rr, m % 2, :],
                                                neghalf[0:rr, :].to_broadcast([rr, NH]), ALU.pow).then_inc(kq_rs, 1)
                    if i < 4:
                        g = {"k": G_V, "v": G_Q, "q": G_PW}[sec]
                        split_lo(c, g, i, CC if g == G_PW else SLAB)
                split_lo_group(c, G_OUT)
                for kind, pairs in passes(c):
                    cnt = att_counter(c, kind)
                    seq = att_sequence(kind, pairs)
                    L = len(seq)

                    def weights(k, it, rel):
                        q = seq[k]
                        v, n = beta[k % 4], q.n
                        pool.wait_ge(s_scan, cnt("z", k + 1, it, rel))
                        nc.gpsimd.tensor_tensor(v[0:q.r, 0:n - 1], v[0:q.r, 0:n - 1], stay[k % 4][0:q.r, 1:n],
                                                ALU.mult).then_inc(s_a, 1)

                    def steps(it, ks, first=False):
                        for k in ks:
                            if at_ := behind(k, 1, L, first):
                                weights(at_[1], it, at_[0])

                    rounds = NH // round_heads(kind)
                    steps(0, range(L), first=True)
                    if rounds > 1:
                        with pool.Fori(1, rounds) as it:
                            steps(it, range(L))
                    steps(rounds - 1, range(L, L + 1))
                split_lo_group(c, G_OUT + 1)
                split_lo_group(c, G_FF)
                norm(c, 1)
                with pool.Fori(0, FFE - 1) as e:
                    for g in (G_FF + 1, G_FF + 2):
                        for j in range(4):
                            n = 4 * (GROUPS * c + g) + 8 * e + j
                            pool.wait_ge(hi_done, n + 1)
                            nc.gpsimd.tensor_tensor(w_lo[g % 2][:, j, :], w_raw[:, j, :],
                                                    w_hi[g % 2][:, j, :].bitcast(F32), ALU.subtract).then_inc(lo_done, 1)
                split_lo_group(c, GROUPS - 1)
                split_lo_group(c, GROUPS)

        @block.scalar
        def _(act):
            def split_hi(c, g, j, width=SLAB, e=None):
                act.wait_ge(raw_in[j], 16 * (GROUPS * c + g + 1) + (32 * e if e is not None else 0))
                nc.scalar.copy(w_hi[g % 2][:, j, 0:width], w_raw[:, j, 0:width]).then_inc(hi_done, 1)

            def split_hi_group(c, g):
                if g == GROUPS:
                    c, g = c + 1, 0
                if c < NC:
                    for j in range(4):
                        split_hi(c, g, j, CC if g == G_PW else SLAB)

            def norm(c, which):
                nb = norm_base(c, which)
                tl = tiles(c)
                if c or which:
                    if which:
                        act.wait_ge(out_add, 2 * (4 * c + len(tl)))
                    else:
                        act.wait_ge(f2_add, 2 * FFE * 4 * c)
                for i, (q0, r) in enumerate(tl):
                    if which == 0:
                        act.wait_ge(x_in[i], 16 * ((c if i < 4 else 0) + 1))
                    if i == 0 and nb:
                        act.wait_ge(n_rstd, nb)
                    if i:
                        act.wait_ge(n_ss, nb + i)
                    nc.scalar.activation(ps[0:r, 6:8, :].rearrange("p a b -> p (a b)"), resid[0:r, i, :], ACT.Square,
                                         accum_out=ssum[0:r, i:i + 1]).then_inc(n_ss, 1)
                for i, (q0, r) in enumerate(tl):
                    for hf in range(2):
                        ev = 2 * (nb + i) + hf
                        act.wait_ge(n_tp, ev + 1)
                        nc.scalar.copy(hT_hi[:, 4 * hf:4 * hf + 4, q0:q0 + r],
                                       ps[:, 4 + hf, 0:4 * r].rearrange("p (a b) -> p a b", a=4)).then_inc(n_hi, 1)

            act.wait_ge(consts, 4)
            act.wait_ge(vec_t, 1)
            nc.scalar.copy(vecs[:], ps[:, 0, 0:CB * (CW + 3)].rearrange("p (a b) -> p a b", a=CB)).then_inc(vec_ok, 1)
            act.wait_ge(vec_t, 2)
            nc.scalar.copy(uT[:, :, SMP:SMP + HIST], ps[:, 1, 0:CB * HIST].rearrange("p (a b) -> p a b", a=CB)).then_inc(vec_ok, 1)
            act.wait_ge(ck_in, 16)
            nc.scalar.copy(packed[:, 0, :, 0:HD], kn[:, 0, :].rearrange("p (h d) -> p h d", h=NH)).then_inc(ck_hi, 1)
            act.wait_ge(cv_in, 16)
            nc.scalar.copy(vpack[:, :, 0:HD], vout[:, 0, :].rearrange("p (h d) -> p h d", h=NH)).then_inc(cv_hi, 1)
            for q in range(2):
                act.wait_ge(ckT_ps, q + 1)
                nc.scalar.copy(kqT[:, 4 * q:4 * q + 4, 0:PAST],
                               ps[:, 2 + q, :].rearrange("p (a b) -> p a b", a=4)).then_inc(ckT_ok, 1)
            for c in range(NC):
                tl = tiles(c)
                nt = len(tl)
                sp_ = splits(c)
                ns = len(sp_)
                if c == 0:
                    split_hi_group(0, 0)
                norm(c, 0)
                for g in range(2):
                    split_hi_group(c, g + 1)
                    for pr in range(2):
                        for s, (s0, w) in enumerate(sp_):
                            ev = 8 * c + (4 * g + 2 * pr + 1) * ns + s
                            u = 4 * c + (2 * g + pr) * ns + s
                            act.wait_ge(ag_ps, ev + 1)
                            if u >= 2:
                                act.wait_ge(ag_u, u - 1)
                            if c == 0 and g == 0 and pr == 0 and s == 0:
                                act.wait_ge(vec_ok, 2)
                                act.wait_ge(vec_t, 2)
                            nc.scalar.activation(sgate[:, u % 2, 0:w], ps[:, (ev - 8 * c) % 4, 0:w],
                                                 ACT.Sigmoid).then_inc(ag_sig, 1)
                ev0 = 12 * c
                kq0 = 8 * c
                evs = kvq_events(c)
                act.wait_ge(ag_u, 4 * c + 4 * ns)
                act.wait_ge(cache_out, 32)
                for s in range(len(evs) + 3):
                    if s < len(evs):
                        sec, i, m = evs[s]
                        r = tl[i][1]
                        act.wait_ge(kvq_ps, ev0 + s + 1)
                        src = ps[0:r, 4 + s % 4, :]
                        if sec == "v":
                            k = i % 2
                            n = 2 * c + i // 2
                            if n:
                                act.wait_ge(vo_out[k], 16 * n)
                            if i >= 2:
                                act.wait_ge(v_lo, 4 * c + i - 1)
                            nc.scalar.copy(vout[0:r, k, :], src).then_inc(kvq_cp, 1)
                        else:
                            if m >= 2:
                                act.wait_ge(kq_mul, kq0 + m - 1)
                            nc.scalar.copy(raw_kq[0:r, m % 2, :], src).then_inc(kvq_cp, 1)
                    if 1 <= s <= len(evs):
                        sec, i, m = evs[s - 1]
                        r = tl[i][1]
                        if sec == "v":
                            act.wait_ge(kvq_cp, ev0 + s)
                            if 4 * c + i:
                                act.wait_ge(vp_out, 16 * (4 * c + i))
                            nc.scalar.copy(vpack[0:r, :, 0:HD],
                                           vout[0:r, i % 2, :].rearrange("p (h d) -> p h d", h=NH)).then_inc(cv_hi, 1)
                        else:
                            act.wait_ge(kq_n, kq0 + m + 1)
                            if m >= 2:
                                act.wait_ge(kqT_ps, 2 * (kq0 + m - 1))
                            nc.scalar.copy(packed[0:r, m % 2, :, 0:HD],
                                           kn[0:r, m % 2, :].rearrange("p (h d) -> p h d", h=NH)).then_inc(pk_hi, 1)
                    if s >= 3:
                        sec, i, m = evs[s - 3]
                        q0, r = tl[i]
                        if sec != "v":
                            if sec == "q" and i == 0:
                                act.wait_ge(kT_out, 16 * (c + 1 + (c == NC - 1)))
                            for q in range(2):
                                act.wait_ge(kqT_ps, 2 * (kq0 + m) + q + 1)
                                nc.scalar.copy(kqT[:, 4 * q:4 * q + 4, q0:q0 + r],
                                               ps[:, q, 0:4 * r].rearrange("p (a b) -> p a b", a=4)).then_inc(kqT_ok, 1)
                    if s < len(evs) and evs[s][1] < 4:
                        g = {"k": G_V, "v": G_Q, "q": G_PW}[evs[s][0]]
                        split_hi(c, g, evs[s][1], CC if g == G_PW else SLAB)
                if c == NC - 1:
                    for q in range(2):
                        act.wait_ge(cvo_ps, q + 1)
                        nc.scalar.copy(cvout[:, q, :], ps[0:HIST, 4 + q, :]).then_inc(cvo_ok, 1)
                for n, (a, q0, w) in enumerate(conv_pieces(c)):
                    lb = c + n
                    for k in range(CB):
                        act.wait_ge(xc_ok, CB * lb + k + 1)
                        if k == 0:
                            act.wait_ge(vp_out, 16 * (4 * c + nt))
                            act.wait_ge(vo_out[0], 16 * (2 * c + (nt + 1) // 2))
                            act.wait_ge(vo_out[1], 16 * (2 * c + 2))
                        nc.scalar.activation(csq[:, k, a:a + w], cacc[:, k, a:a + w], ACT.Square).then_inc(sq_ok, 1)
                    act.wait_ge(var_ok, lb + 1)
                    nc.scalar.activation(lnr[:, 0:w], lnv[:, 0:w], ACT.Sqrt).then_inc(sd_ok, 1)
                    act.wait_ge(kn_out[0], 16 * (2 * c + (nt + 1) // 2))
                    act.wait_ge(kn_out[1], 16 * (2 * c + nt // 2))
                    for k in range(CB):
                        act.wait_ge(yn_ok, CB * lb + k + 1)
                        if CB * lb + k >= 2:
                            act.wait_ge(cm_ok, CB * lb + k - 1)
                        nc.scalar.activation(csig[:, k % 2, 0:w], cacc[:, k, a:a + w], ACT.Sigmoid,
                                             bias=vecs[:, k, CW + 2:CW + 3], scale=vecs[:, k, CW + 1:CW + 2]).then_inc(sg_ok, 1)
                        nc.scalar.activation(cid[:, k % 2, 0:w], cacc[:, k, a:a + w], ACT.Identity,
                                             bias=vecs[:, k, CW + 2:CW + 3], scale=vecs[:, k, CW + 1:CW + 2]).then_inc(sg_ok, 1)
                        act.wait_ge(cm_ok, CB * lb + k + 1)
                        if k == 0:
                            act.wait_ge(var_ps, lb + 1)
                        nc.scalar.copy(cT_hi[:, k, a:a + w], cacc[:, k, a:a + w]).then_inc(c_hi, 1)
                split_hi_group(c, G_OUT)
                act.wait_ge(qT_out, 16 * (c + 1))
                for m in range(CB):
                    for n, (a, q0, w) in enumerate(conv_pieces(c)):
                        npc = len(conv_pieces(c))
                        ev = CB * c + npc * m + n
                        act.wait_ge(pw_ps, ev + 1)
                        nc.scalar.copy(mixT_hi[:, m, q0:q0 + w], ps[:, (ev - CB * c) % 4, 0:w]).then_inc(pw_hi, 1)
                if c == NC - 1:
                    act.wait_ge(cvo_out, 32)
                for kind, pairs in passes(c):
                    cnt = att_counter(c, kind)
                    seq = att_sequence(kind, pairs)
                    L = len(seq)

                    def sigmoids(k, it, first):
                        q = seq[k]
                        if q.diag:
                            act.wait_ge(z_msk, cnt("m", q.m + 1, it, 0))
                        else:
                            act.wait_ge(z_ps, cnt("z", k + 1, it, 0))
                        if old := behind(k, 4, L, first):
                            act.wait_ge(t_ps, cnt("t", turned(seq[old[1]]), it, old[0]))
                        if old := behind(k, 2, L, first):
                            act.wait_ge(s_scan, cnt("z", old[1] + 1, it, old[0]))
                        z = bank(k, q.r, 0, q.n)
                        nc.scalar.activation(stay[k % 4][0:q.r, 0:q.n], z, ACT.Sigmoid, scale=-1.0)
                        nc.scalar.activation(beta[k % 4][0:q.r, 0:q.n], z, ACT.Sigmoid).then_inc(s_sg, 1)

                    def turned_hi(k, it, rel, first):
                        q = seq[k]
                        for gi, grp in enumerate(key_groups(q.a0, q.n)):
                            act.wait_ge(t_ps, cnt("t", q.tg + gi + 1, it, rel))
                            if q.t == 0 and gi == 0 and not (first and q.v < 2):
                                act.wait_ge(v_ps, cnt("v", q.v - 1, it, rel))
                            evacuate(nc.scalar.copy, None, aT_hi, aT_blocks(q, grp), q.t, q.r,
                                     ps[:, 4 + (q.tg + gi) % 2, :], t_hi)

                    def output(k, it, rel):
                        q = seq[k]
                        if q.last and q.ends:
                            w = sum(x[1] for x in pairs[q.p])
                            act.wait_ge(v_ps, cnt("v", q.v + 1, it, rel))
                            act.wait_ge(o_lo, cnt("o", q.ob + 1, it, rel))
                            mine = q.head % 2 * HD
                            nc.scalar.copy(osb[mine:mine + HD, 0:w],
                                           ps[HD - mine:P - mine, 6 + q.ob % 2, 0:w]).then_inc(o_cp, 1)

                    def steps(it, ks, first=False):
                        for k in ks:
                            if k < L:
                                sigmoids(k, it, first)
                            if at_ := behind(k, 2, L, first):
                                turned_hi(at_[1], it, at_[0], first)
                            if at_ := behind(k, 4, L, first):
                                output(at_[1], it, at_[0])

                    act.wait_ge(lo_done, 4 * (GROUPS * c + G_OUT + 1))
                    rounds = NH // round_heads(kind)
                    steps(0, range(L), first=True)
                    if rounds > 1:
                        with act.Fori(1, rounds) as it:
                            steps(it, range(L))
                    steps(rounds - 1, range(L, L + 4))
                split_hi_group(c, G_OUT + 1)
                act.wait_ge(out_ps, 8 * c + nt)
                split_hi_group(c, G_FF)
                norm(c, 1)
                f1b = 4 * FFE * c
                f2b = 8 * FFE * c + 1

                def hi_of(e, k):
                    j, s = k // ns, k % ns
                    s0, w = sp_[s]
                    act.wait_ge(f_sq, f1b + k + 1 + e * 4 * ns)
                    nc.scalar.copy(hid_hi[:, j, s0:s0 + w], fsq[:, k % 2, 0:w]).then_inc(f_hi, 1)

                def ff1(e):
                    for k in range(4 * ns):
                        w = sp_[k % ns][1]
                        act.wait_ge(f1_ps, f1b + k + 1 + e * 4 * ns)
                        if k >= 2:
                            act.wait_ge(f_sq, f1b + k - 1 + e * 4 * ns)
                        nc.scalar.activation(frel[:, k % 2, 0:w], ps[:, k % 4, 0:w], ACT.Relu).then_inc(f_rel, 1)
                        if k >= 1:
                            hi_of(e, k - 1)
                    hi_of(e, 4 * ns - 1)

                with act.Fori(0, FFE - 1) as e:
                    act.wait_ge(f2_ps, f2b + e * 2 * nt)
                    for j in range(4):
                        split_hi(c, G_FF + 1, j, e=e)
                    ff1(e)
                    for j in range(4):
                        split_hi(c, G_FF + 2, j, e=e)
                act.wait_ge(f2_ps, f2b + (FFE - 1) * 2 * nt)
                split_hi_group(c, GROUPS - 1)
                ff1(FFE - 1)
                split_hi_group(c, GROUPS)

        @block.vector
        def _(dve):
            def norm(c, which):
                nb = norm_base(c, which)
                tl = tiles(c)
                nst = 2 * c + which
                dve.wait_ge(grow_in, 16 * (nst + 1))
                for i in range(len(tl) + 1):
                    if i < len(tl):
                        q0, r = tl[i]
                        dve.wait_ge(n_rstd, nb + i + 1)
                        if i >= 2:
                            dve.wait_ge(n_tp, 2 * (nb + i - 1))
                        nc.vector.scalar_tensor_tensor(out=xn[0:r, i % 2, :], in0=resid[0:r, i, :],
                                                       scalar=rstd[0:r, i:i + 1], in1=g_row[0:r, :],
                                                       op0=ALU.mult, op1=ALU.mult).then_inc(n_xn, 1)
                    if i >= 1:
                        q0, r = tl[i - 1]
                        for hf in range(2):
                            dve.wait_ge(n_hi, 2 * (nb + i - 1) + hf + 1)
                            nc.vector.tensor_tensor(hT_lo[:, 4 * hf:4 * hf + 4, q0:q0 + r],
                                                    ps[:, 4 + hf, 0:4 * r].rearrange("p (a b) -> p a b", a=4),
                                                    hT_hi[:, 4 * hf:4 * hf + 4, q0:q0 + r].bitcast(F32),
                                                    ALU.subtract).then_inc(n_lo, 1)

            dve.wait_ge(gains_in, 32)
            nc.vector.tensor_scalar(gq[:], gq[:], HD ** -0.5, None, ALU.mult).then_inc(hist_ok, 1)
            nc.vector.memset(uT[:, 0, 0:HIST], 0.0).then_inc(o_lo, 1)
            nc.vector.memset(uT[:, 1:CB, 0:HIST], 0.0).then_inc(hist_ok, 1)
            dve.wait_ge(ck_hi, 1)
            nc.vector.tensor_tensor(packed[:, 0, :, HD:P], kn[:, 0, :].rearrange("p (h d) -> p h d", h=NH),
                                    packed[:, 0, :, 0:HD].bitcast(F32), ALU.subtract).then_inc(ck_lo, 1)
            dve.wait_ge(cv_hi, 1)
            nc.vector.tensor_tensor(vpack[:, :, HD:P], vout[:, 0, :].rearrange("p (h d) -> p h d", h=NH),
                                    vpack[:, :, 0:HD].bitcast(F32), ALU.subtract).then_inc(cv_lo, 1)
            for c in range(NC):
                tl = tiles(c)
                nt = len(tl)
                sp_ = splits(c)
                ns = len(sp_)
                norm(c, 0)
                if c:
                    dve.wait_ge(taps, TAPS * c)
                    nc.vector.tensor_copy(uT[:, :, 0:HIST], uT[:, :, CHUNK:CHUNK + HIST]).then_inc(hist_ok, 1)
                dve.wait_ge(hist_ok, 2 + c)
                for m in range(CB):
                    for s, (s0, w) in enumerate(sp_):
                        u = 4 * c + m * ns + s
                        evv = 2 * m * ns + s
                        dve.wait_ge(ag_sig, u + 1)
                        cut = max(s0, min(s0 + w, CHUNK))
                        for n, (x0, x1) in enumerate([(s0, cut), (cut, s0 + w)]):
                            if x1 > x0:
                                d0 = x0 + HIST + (HIST if x0 >= CHUNK else 0)
                                ins = nc.vector.tensor_tensor(uT[:, m, d0:d0 + x1 - x0], ps[:, evv % 4, x0 - s0:x1 - s0],
                                                              sgate[:, u % 2, x0 - s0:x1 - s0], ALU.mult)
                        ins.then_inc(ag_u, 1)
                evs = kvq_events(c)
                kq0 = 8 * c
                wd = CVW if c == NC - 1 else CHUNK
                dve.wait_ge(vec_ok, 2)
                dve.wait_ge(ag_u, 4 * c + 4 * ns)
                for s in range(len(evs) + 1):
                    if s < len(evs):
                        sec, i, m = evs[s]
                        r = tl[i][1]
                        if m is not None:
                            u = kq0 + m
                            b = m % 2
                            dve.wait_ge(kvq_cp, 12 * c + s + 1)
                            if u:
                                dve.wait_ge(kq_ss, u)
                            nc.vector.tensor_tensor(sqr[0:r, :], raw_kq[0:r, b, :], raw_kq[0:r, b, :], ALU.mult).then_inc(kq_sq, 1)
                            dve.wait_ge(kq_sq, u + 1)
                            nc.vector.tensor_reduce(hss[0:r, b, :], sqr[0:r, :].rearrange("p (h d) -> p h d", h=NH),
                                                    axis=AX.X, op=ALU.add).then_inc(kq_ss, 1)
                    if s >= 1:
                        psec, pi, pm = evs[s - 1]
                        pr = tl[pi][1]
                        if pm is not None:
                            dve.wait_ge(pk_hi, kq0 + pm + 1)
                            nc.vector.tensor_tensor(packed[0:pr, pm % 2, :, HD:P],
                                                    kn[0:pr, pm % 2, :].rearrange("p (h d) -> p h d", h=NH),
                                                    packed[0:pr, pm % 2, :, 0:HD].bitcast(F32), ALU.subtract).then_inc(pk_lo, 1)
                        else:
                            dve.wait_ge(cv_hi, 4 * c + pi + 2)
                            nc.vector.tensor_tensor(vpack[0:pr, :, HD:P],
                                                    vout[0:pr, pi % 2, :].rearrange("p (h d) -> p h d", h=NH),
                                                    vpack[0:pr, :, 0:HD].bitcast(F32), ALU.subtract).then_inc(v_lo, 1)
                    if s < len(evs):
                        for x in taps_of(c, s):
                            tap, k = x // CB, x % CB
                            n = TAPS * c + x
                            if tap == 0:
                                nc.vector.tensor_scalar(cacc[:, k, 0:wd], uT[:, k, 0:wd], vecs[:, k, 0:1],
                                                        vecs[:, k, CW:CW + 1], ALU.mult, ALU.add).then_inc(taps, 1)
                            else:
                                dve.wait_ge(taps, n - CB + 1)
                                nc.vector.scalar_tensor_tensor(out=cacc[:, k, 0:wd], in0=uT[:, k, tap:tap + wd],
                                                               scalar=vecs[:, k, tap:tap + 1], in1=cacc[:, k, 0:wd],
                                                               op0=ALU.mult, op1=ALU.add).then_inc(taps, 1)
                        if m is not None:
                            dve.wait_ge(kq_rs, u + 1)
                            if u >= 2:
                                dve.wait_ge(pk_lo, u - 1)
                            uses = (2 * c + i // 2) if sec == "k" else 2 * c + (nt + 1 - b) // 2
                            if uses:
                                dve.wait_ge(kn_out[b], 16 * uses)
                            dve.wait_ge(ck_lo, 1)
                            nc.vector.tensor_tensor(kn[0:r, b, :].rearrange("p (h d) -> p h d", h=NH),
                                                    raw_kq[0:r, b, :].rearrange("p (h d) -> p h d", h=NH),
                                                    hrs[0:r, b, :].unsqueeze(2).to_broadcast([r, NH, HD]),
                                                    ALU.mult).then_inc(kq_mul, 1)
                            dve.wait_ge(kq_mul, u + 1)
                            gain = gk if sec == "k" else gq
                            nc.vector.tensor_tensor(kn[0:r, b, :].rearrange("p (h d) -> p h d", h=NH),
                                                    kn[0:r, b, :].rearrange("p (h d) -> p h d", h=NH),
                                                    gain[0:r, :].unsqueeze(1).to_broadcast([r, NH, HD]),
                                                    ALU.mult).then_inc(kq_n, 1)
                dve.wait_ge(taps, TAPS * (c + 1))
                for n, (a, q0, w) in enumerate(conv_pieces(c)):
                    lb = c + n
                    dve.wait_ge(mean_ps, lb + 1)
                    for k in range(CB):
                        nc.vector.scalar_tensor_tensor(out=cacc[:, k, a:a + w], in0=ps[:, 2, 0:w], scalar=-1.0 / CC,
                                                       in1=cacc[:, k, a:a + w], op0=ALU.mult, op1=ALU.add).then_inc(xc_ok, 1)
                    dve.wait_ge(var_ps, lb + 1)
                    if n:
                        dve.wait_ge(lnr_ok, lb)
                    nc.vector.tensor_scalar(lnv[:, 0:w], ps[:, 3, 0:w], 1.0 / CC, EPS, ALU.mult, ALU.add).then_inc(var_ok, 1)
                    dve.wait_ge(sd_ok, lb + 1)
                    nc.vector.reciprocal(lnr[:, 0:w], lnr[:, 0:w]).then_inc(nwt, 1)
                    dve.wait_ge(nwt, 3 * lb + 1)
                    if n:
                        dve.wait_ge(cm_ok, CB * lb)
                    nc.vector.scalar_tensor_tensor(out=ntmp[:, 0:w], in0=lnr[:, 0:w], scalar=-0.5, in1=lnr[:, 0:w],
                                                   op0=ALU.mult, op1=ALU.mult).then_inc(nwt, 1)
                    dve.wait_ge(nwt, 3 * lb + 2)
                    nc.vector.tensor_tensor(ntmp[:, 0:w], ntmp[:, 0:w], lnv[:, 0:w], ALU.mult).then_inc(nwt, 1)
                    dve.wait_ge(nwt, 3 * lb + 3)
                    nc.vector.scalar_tensor_tensor(out=lnr[:, 0:w], in0=ntmp[:, 0:w], scalar=1.5, in1=lnr[:, 0:w],
                                                   op0=ALU.add, op1=ALU.mult).then_inc(lnr_ok, 1)
                    dve.wait_ge(lnr_ok, lb + 1)
                    dve.wait_ge(xc_ok, CB * (lb + 1))
                    for k in range(CB):
                        nc.vector.tensor_tensor(cacc[:, k, a:a + w], cacc[:, k, a:a + w], lnr[:, 0:w],
                                                ALU.mult).then_inc(yn_ok, 1)
                    for k in range(CB + 1):
                        if k < CB:
                            dve.wait_ge(sg_ok, 2 * (CB * lb + k + 1))
                            nc.vector.tensor_tensor(cacc[:, k, a:a + w], csig[:, k % 2, 0:w], cid[:, k % 2, 0:w],
                                                    ALU.mult).then_inc(cm_ok, 1)
                        if k >= 1:
                            dve.wait_ge(c_hi, CB * lb + k)
                            nc.vector.tensor_tensor(cT_lo[:, k - 1, a:a + w], cacc[:, k - 1, a:a + w],
                                                    cT_hi[:, k - 1, a:a + w].bitcast(F32), ALU.subtract).then_inc(c_lo, 1)
                npc = len(conv_pieces(c))
                for m in range(CB):
                    for n, (a, q0, w) in enumerate(conv_pieces(c)):
                        ev = CB * c + npc * m + n
                        dve.wait_ge(pw_hi, ev + 1)
                        nc.vector.tensor_tensor(mixT_lo[:, m, q0:q0 + w], ps[:, (ev - CB * c) % 4, 0:w],
                                                mixT_hi[:, m, q0:q0 + w].bitcast(F32), ALU.subtract).then_inc(pw_lo, 1)
                dve.wait_ge(consts, 6)
                if c == NC - 1:
                    dve.wait_ge(cvo_out, 32)
                for kind, pairs in passes(c):
                    cnt = att_counter(c, kind)
                    seq = att_sequence(kind, pairs)
                    L = len(seq)

                    def mask(k, it):
                        q = seq[k]
                        if q.diag:
                            dve.wait_ge(z_ps, cnt("z", k + 1, it, 0))
                            v = bank(k, q.r, q.n - q.r, q.n)
                            nc.vector.tensor_tensor(v, v, limit[0:q.r, 0:q.r], ALU.min).then_inc(z_msk, 1)

                    def products(k, it, rel):
                        q = seq[k]
                        v, r, n = stay[k % 4], q.r, q.n
                        dve.wait_ge(s_sg, cnt("z", k + 1, it, rel))
                        init = 1.0
                        if not q.diag:
                            before_ = len(pairs[q.p])
                            dve.wait_ge(s_scan, cnt("z", k - before_ + 1, it, rel))
                            init = stay[(k - before_) % 4][0:r, 0:1]
                            edge = beta[k % 4][0:r, n - 1:n]
                            nc.vector.tensor_tensor(edge, edge, init, ALU.mult)
                        nc.vector.tensor_tensor_scan(v[0:r, 0:n][:, ::-1], v[0:r, 0:n][:, ::-1],
                                                     ones[0:r, 0:1].to_broadcast([r, n]), init,
                                                     ALU.mult, ALU.mult).then_inc(s_scan, 1)

                    def turned_lo(k, it, rel):
                        q = seq[k]
                        for gi, grp in enumerate(key_groups(q.a0, q.n)):
                            dve.wait_ge(t_hi, cnt("t", q.tg + gi + 1, it, rel))
                            evacuate(nc.vector.tensor_tensor, aT_hi, aT_lo, aT_blocks(q, grp), q.t, q.r,
                                     ps[:, 4 + (q.tg + gi) % 2, :], t_lo)

                    def output(k, it, rel):
                        q = seq[k]
                        if q.last and q.ends:
                            w = sum(x[1] for x in pairs[q.p])
                            col = CHUNK if kind else pairs[q.p][0][0]
                            me = slice(q.head % 2 * HD, q.head % 2 * HD + HD)
                            blk = CB + q.head // 2 if kind else it + (CB + rel)
                            dst = mixT_hi[me, blk, col:col + w]
                            o = q.ob + 1
                            dve.wait_ge(o_cp, cnt("o", o, it, rel))
                            nc.vector.tensor_tensor(of[me, 0:w], ps[me, 6 + q.ob % 2, 0:w], osb[me, 0:w], ALU.add).then_inc(o_sum, 1)
                            dve.wait_ge(o_sum, cnt("o", o, it, rel))
                            nc.vector.tensor_copy(dst, of[me, 0:w]).then_inc(o_hi, 1)
                            dve.wait_ge(o_hi, cnt("o", o, it, rel))
                            nc.vector.tensor_tensor(mixT_lo[me, blk, col:col + w], of[me, 0:w], dst.bitcast(F32),
                                                    ALU.subtract).then_inc(o_lo, 1)

                    def steps(it, ks, first=False):
                        for k in ks:
                            if k < L:
                                mask(k, it)
                            if at_ := behind(k, 1, L, first):
                                products(at_[1], it, at_[0])
                            if at_ := behind(k, 2, L, first):
                                turned_lo(at_[1], it, at_[0])
                            if at_ := behind(k, 4, L, first):
                                output(at_[1], it, at_[0])

                    rounds = NH // round_heads(kind)
                    steps(0, range(L), first=True)
                    if rounds > 1:
                        with dve.Fori(1, rounds) as it:
                            steps(it, range(L))
                    steps(rounds - 1, range(L, L + 4))
                for hf in range(2):
                    for i, (q0, r) in enumerate(tl):
                        ev = hf * nt + i
                        dve.wait_ge(out_ps, 8 * c + ev + 1)
                        v = resid[0:r, i, hf * BANK:(hf + 1) * BANK]
                        nc.vector.tensor_tensor(v, ps[0:r, 4 + ev % 4, :], v, ALU.add).then_inc(out_add, 1)
                norm(c, 1)
                f1b = 4 * FFE * c
                f2b = 8 * FFE * c

                def round_(e):
                    for k in range(4 * ns + 1):
                        if k < 4 * ns:
                            w = sp_[k % ns][1]
                            dve.wait_ge(f_rel, f1b + k + 1 + e * 4 * ns)
                            if k >= 2:
                                dve.wait_ge(f_lo, f1b + k - 1 + e * 4 * ns)
                            nc.vector.tensor_tensor(fsq[:, k % 2, 0:w], frel[:, k % 2, 0:w], frel[:, k % 2, 0:w],
                                                    ALU.mult).then_inc(f_sq, 1)
                        if k >= 1:
                            j, s = (k - 1) // ns, (k - 1) % ns
                            s0, w = sp_[s]
                            dve.wait_ge(f_hi, f1b + k + e * 4 * ns)
                            nc.vector.tensor_tensor(hid_lo[:, j, s0:s0 + w], fsq[:, (k - 1) % 2, 0:w],
                                                    hid_hi[:, j, s0:s0 + w].bitcast(F32), ALU.subtract).then_inc(f_lo, 1)
                    for ev in range(2 * nt):
                        i, hf = ev // 2, ev % 2
                        r = tl[i][1]
                        dve.wait_ge(f2_ps, f2b + ev + 2 + e * 2 * nt)
                        v = resid[0:r, i, hf * BANK:(hf + 1) * BANK]
                        nc.vector.tensor_tensor(v, ps[0:r, 4 + ev % 4, :], v, ALU.add).then_inc(f2_add, 1)

                with dve.Fori(0, FFE) as e:
                    round_(e)

        @block.tensor
        def _(pe):
            def mm3(out, w, x, start, stop):
                nc.tensor.matmul(out, w[0], x[0], start=start, stop=False)
                nc.tensor.matmul(out, w[0], x[1], start=False, stop=False)
                return nc.tensor.matmul(out, w[1], x[0], start=False, stop=stop)

            def slab(g, j):
                return w_hi[g % 2][:, j, :], w_lo[g % 2][:, j, :]

            def norm(c, which):
                nb = norm_base(c, which)
                for i, (q0, r) in enumerate(tiles(c)):
                    pe.wait_ge(n_xn, nb + i + 1)
                    if i == 0 and which == 0 and c:
                        pe.wait_ge(f2_add, 8 * FFE * c)
                    for hf in range(2):
                        ev = 2 * (nb + i) + hf
                        if i:
                            pe.wait_ge(n_lo, ev - 1)
                        for k in range(4):
                            blk = 4 * hf + k
                            ins = nc.tensor.transpose(ps[:, 4 + hf, k * r:(k + 1) * r], xn[0:r, i % 2, blk * P:(blk + 1) * P],
                                                      ident[0:r, 0:r])
                        ins.then_inc(n_tp, 1)

            pe.wait_ge(consts, 4)
            pe.wait_ge(rows_in, 80)
            for k in range(CB):
                n = CW + 3
                ins = nc.tensor.transpose(ps[:, 0, k * n:(k + 1) * n], crow[:, k * P:(k + 1) * P], ident[0:n, 0:n])
            ins.then_inc(vec_t, 1)
            for k in range(CB):
                ins = nc.tensor.transpose(ps[:, 1, k * HIST:(k + 1) * HIST], srow[:, k * P:(k + 1) * P], ident[0:HIST, 0:HIST])
            ins.then_inc(vec_t, 1)
            pe.wait_ge(ck_lo, 1)
            for q in range(2):
                for k in range(4):
                    ins = nc.tensor.transpose(ps[:, 2 + q, k * P:(k + 1) * P], packed[:, 0, 4 * q + k, :].bitcast(F32), ident[:])
                    if (q, k) == (0, 0):
                        ins.then_inc(f2_ps, 1)
                ins.then_inc(ckT_ps, 1)
            for c in range(NC):
                tl = tiles(c)
                nt = len(tl)
                sp_ = splits(c)
                ns = len(sp_)
                norm(c, 0)
                pe.wait_ge(n_lo, 2 * (norm_base(c, 0) + nt))
                if c == 0:
                    pe.wait_ge(vec_ok, 2)
                    pe.wait_ge(ckT_ok, 2)
                else:
                    pe.wait_ge(f_rel, 4 * FFE * c)
                for g in range(2):
                    for j in range(4):
                        n = 4 * (GROUPS * c + g) + j
                        pe.wait_ge(lo_done, n + 1)
                        wh, wl = slab(g, j)
                        for s, (s0, w) in enumerate(sp_):
                            ev = (4 * g + j) * ns + s
                            old = ev - 4
                            if old >= 0:
                                pe.wait_ge(ag_u, 4 * c + (old // (2 * ns)) * ns + old % ns + 1)
                            for k in range(KD):
                                ins = mm3(ps[:, ev % 4, 0:w], (wh[:, k * P:(k + 1) * P], wl[:, k * P:(k + 1) * P]),
                                          (hT_hi[:, k, s0:s0 + w], hT_lo[:, k, s0:s0 + w]), k == 0, k == KD - 1)
                            ins.then_inc(ag_ps, 1)
                evs = kvq_events(c)
                kq0 = 8 * c
                for s in range(len(evs) + 2):
                    if s < len(evs):
                        sec, i, m = evs[s]
                        g = {"k": G_K, "v": G_V, "q": G_Q}[sec]
                        q0, r = tl[i]
                        if s >= 4:
                            pe.wait_ge(kvq_cp, 12 * c + s - 3)
                        for k in range(KD):
                            if i == 0 and k % 2 == 0:
                                pe.wait_ge(lo_done, 4 * (GROUPS * c + g) + k // 2 + 1)
                            wh, wl = slab(g, k // 2)
                            c0 = (k % 2) * AW
                            nc.tensor.matmul(ps[0:r, 4 + s % 4, :], hT_hi[:, k, q0:q0 + r], wh[:, c0:c0 + AW], start=k == 0, stop=False)
                            nc.tensor.matmul(ps[0:r, 4 + s % 4, :], hT_lo[:, k, q0:q0 + r], wh[:, c0:c0 + AW], start=False, stop=False)
                            ins = nc.tensor.matmul(ps[0:r, 4 + s % 4, :], hT_hi[:, k, q0:q0 + r], wl[:, c0:c0 + AW],
                                                   start=False, stop=k == KD - 1)
                        ins.then_inc(kvq_ps, 1)
                    if s >= 2:
                        sec, i, m = evs[s - 2]
                        r = tl[i][1]
                        if sec != "v":
                            pe.wait_ge(pk_lo, kq0 + m + 1)
                            for q in range(2):
                                if m:
                                    pe.wait_ge(kqT_ok, 2 * (kq0 + m) + q - 1)
                                elif q == 0:
                                    pe.wait_ge(ag_u, 4 * c + 4 * ns)
                                for k in range(4):
                                    ins = nc.tensor.transpose(ps[:, q, k * r:(k + 1) * r],
                                                              packed[0:r, m % 2, 4 * q + k, :].bitcast(F32), ident[0:r, 0:r])
                                ins.then_inc(kqT_ps, 1)
                if c == NC - 1:
                    for q, col in enumerate((CHUNK, SMP + DEC)):
                        pe.wait_ge(kvq_cp, 12 * c + len(evs))
                        for k in range(CB):
                            ins = nc.tensor.transpose(ps[0:HIST, 4 + q, k * P:(k + 1) * P], uT[:, k, col:col + HIST], ident[:])
                        ins.then_inc(cvo_ps, 1)
                for n, (a, q0, w) in enumerate(conv_pieces(c)):
                    lb = c + n
                    pe.wait_ge(taps, TAPS * (c + 1))
                    if n:
                        pe.wait_ge(xc_ok, CB * lb)
                    for k in range(CB):
                        ins = nc.tensor.matmul(ps[:, 2, 0:w], ones[:], cacc[:, k, a:a + w], start=k == 0, stop=k == CB - 1)
                    ins.then_inc(mean_ps, 1)
                    if n:
                        pe.wait_ge(var_ok, lb)
                    for k in range(CB):
                        pe.wait_ge(sq_ok, CB * lb + k + 1)
                        ins = nc.tensor.matmul(ps[:, 3, 0:w], ones[:], csq[:, k, a:a + w], start=k == 0, stop=k == CB - 1)
                    ins.then_inc(var_ps, 1)
                npc = len(conv_pieces(c))
                pe.wait_ge(c_lo, CB * (c + npc))
                pe.wait_ge(kqT_ok, 2 * (kq0 + 2 * nt))
                for m in range(CB):
                    for n, (a, q0, w) in enumerate(conv_pieces(c)):
                        ev = npc * m + n
                        if ev >= 4:
                            pe.wait_ge(pw_lo, CB * c + ev - 3)
                        for k in range(CB):
                            if m == 0 and n == 0:
                                pe.wait_ge(lo_done, 4 * (GROUPS * c + G_PW) + k + 1)
                            wh, wl = slab(G_PW, k)
                            ins = mm3(ps[:, ev % 4, 0:w], (wh[:, m * P:(m + 1) * P], wl[:, m * P:(m + 1) * P]),
                                      (cT_hi[:, k, a:a + w], cT_lo[:, k, a:a + w]), k == 0, k == CB - 1)
                        ins.then_inc(pw_ps, 1)
                pe.wait_ge(pw_lo, CB * (c + npc))
                if c == NC - 1:
                    pe.wait_ge(cvo_ok, 2)
                for kind, pairs in passes(c):
                    cnt = att_counter(c, kind)
                    seq = att_sequence(kind, pairs)
                    L = len(seq)
                    loads = 16 * 5
                    loaded = loads * (NH // 2) * (c + kind)

                    def scores(k, it, first):
                        q = seq[k]
                        slot, q0, k0 = (0, q.head * DEC, q.head * (PAST + DEC)) if kind else (q.head, q.q0, q.a0)
                        if k == 0 or (not kind and seq[k - 1].head != q.head):
                            pe.wait_ge(at_in[slot], it * loads + loaded + (16 * 6 if kind else loads))
                        if old := behind(k, 2, L, first):
                            pe.wait_ge(s_sg, cnt("z", old[1] + 1, it, old[0]))
                        for x in range(0, q.n, BANK):
                            w = min(BANK, q.n - x)
                            for v in range(2):
                                ins = nc.tensor.matmul(ps[0:q.r, 2 * (k % 2) + x // BANK, 0:w], a_q[slot][:, v, q0:q0 + q.r],
                                                       a_k[slot][:, k0 + x:k0 + x + w], start=v == 0, stop=v == 1)
                        ins.then_inc(z_ps, 1)

                    def turn(k, it, rel, first):
                        q = seq[k]
                        pe.wait_ge(s_a, cnt("z", k + 1, it, rel))
                        for gi, grp in enumerate(key_groups(q.a0, q.n)):
                            if not (first and q.tg + gi < 2):
                                pe.wait_ge(t_lo, cnt("t", q.tg + gi - 1, it, rel))
                            for x, (blk, w) in enumerate(grp):
                                s0 = blk * P - q.a0
                                ins = nc.tensor.transpose(ps[0:w, 4 + (q.tg + gi) % 2, x * q.r:(x + 1) * q.r],
                                                          beta[k % 4][0:q.r, s0:s0 + w], ident[0:q.r, 0:q.r])
                            ins.then_inc(t_ps, 1)

                    def values(k, it, rel, first):
                        q = seq[k]
                        if not q.ends:
                            return
                        pair = pairs[q.p]
                        slot, v0 = (0, q.head * 2) if kind else (q.head, 0)
                        pe.wait_ge(t_lo, cnt("t", turned(q), it, rel))
                        if q.diag:
                            back = -1 if not first or q.ob else 0
                            pe.wait_ge(o_lo, cnt("o", q.ob + 1 + back, it, rel))
                        blocks = [b for grp in key_groups(q.a0, q.n) for b in grp]
                        width = sum(x[1] for x in pair)
                        for blk, w in blocks:
                            c0 = P * sum(x[2] <= blk * P for x in pair)
                            (own, _w), = aT_blocks(q, [(blk, w)])
                            for v, src in enumerate((aT_hi, aT_lo)):
                                ins = nc.tensor.matmul(ps[:, 6 + q.ob % 2, c0:width], a_v[slot][0:w, v0 + blk, :],
                                                       src[0:w, own, c0:width], start=q.diag and (blk, v) == (blocks[0][0], 0),
                                                       stop=q.last and (blk, v) == (blocks[-1][0], 1))
                        ins.then_inc(v_ps, 1)

                    def steps(it, ks, first=False):
                        for k in ks:
                            if k < L:
                                scores(k, it, first)
                            if at_ := behind(k, 2, L, first):
                                turn(at_[1], it, at_[0], first)
                            if at_ := behind(k, 3, L, first):
                                values(at_[1], it, at_[0], first)

                    rounds = NH // round_heads(kind)
                    steps(0, range(L), first=True)
                    if rounds > 1:
                        with pe.Fori(1, rounds) as it:
                            steps(it, range(L))
                    steps(rounds - 1, range(L, L + 3), first=rounds == 1)
                pe.wait_ge(o_lo, att_outputs(c) + 1)
                for hf in range(2):
                    g = G_OUT + hf
                    for i, (q0, r) in enumerate(tl):
                        ev = hf * nt + i
                        if ev >= 4:
                            pe.wait_ge(out_add, 8 * c + ev - 3)
                        for k in range(KD):
                            if i == 0 and k % 2 == 0:
                                pe.wait_ge(lo_done, 4 * (GROUPS * c + g) + k // 2 + 1)
                            wh, wl = slab(g, k // 2)
                            c0 = (k % 2) * BANK
                            nc.tensor.matmul(ps[0:r, 4 + ev % 4, :], mixT_hi[:, k, q0:q0 + r], wh[:, c0:c0 + BANK], start=k == 0, stop=False)
                            nc.tensor.matmul(ps[0:r, 4 + ev % 4, :], mixT_lo[:, k, q0:q0 + r], wh[:, c0:c0 + BANK], start=False, stop=False)
                            ins = nc.tensor.matmul(ps[0:r, 4 + ev % 4, :], mixT_hi[:, k, q0:q0 + r], wl[:, c0:c0 + BANK],
                                                   start=False, stop=k == KD - 1)
                        ins.then_inc(out_ps, 1)
                norm(c, 1)
                pe.wait_ge(n_lo, 2 * (norm_base(c, 1) + nt))
                with pe.Fori(0, FFE) as e:
                    f1b = 4 * FFE * c
                    f2b = 8 * FFE * c
                    for j in range(4):
                        pe.wait_ge(lo_done, 4 * (GROUPS * c + G_FF) + 8 * e + j + 1)
                        wh, wl = slab(G_FF, j)
                        for s, (s0, w) in enumerate(sp_):
                            ev = j * ns + s
                            if ev >= 4:
                                pe.wait_ge(f_rel, f1b + ev - 3 + e * 4 * ns)
                            for k in range(KD):
                                ins = mm3(ps[:, ev % 4, 0:w], (wh[:, k * P:(k + 1) * P], wl[:, k * P:(k + 1) * P]),
                                          (hT_hi[:, k, s0:s0 + w], hT_lo[:, k, s0:s0 + w]), k == 0, k == KD - 1)
                            ins.then_inc(f1_ps, 1)
                    for ev in range(2 * nt):
                        i, hf = ev // 2, ev % 2
                        q0, r = tl[i]
                        if ev >= 4:
                            pe.wait_ge(f2_add, f2b + ev - 3 + e * 2 * nt)
                        for k in range(4):
                            if ev == 0:
                                pe.wait_ge(f_lo, f1b + (k + 1) * ns + e * 4 * ns)
                                pe.wait_ge(lo_done, 4 * (GROUPS * c + G_FF + 1) + 8 * e + k + 1)
                            wh, wl = slab(G_FF + 1, k)
                            o = ps[0:r, 4 + ev % 4, :]
                            c0 = hf * BANK
                            nc.tensor.matmul(o, hid_hi[:, k, q0:q0 + r], wh[:, c0:c0 + BANK], start=k == 0, stop=False)
                            nc.tensor.matmul(o, hid_lo[:, k, q0:q0 + r], wh[:, c0:c0 + BANK], start=False, stop=False)
                            ins = nc.tensor.matmul(o, hid_hi[:, k, q0:q0 + r], wl[:, c0:c0 + BANK], start=False, stop=k == 3)
                        ins.then_inc(f2_ps, 1)


_INS = ["x_prompt", "x_sample", "cache_k", "cache_v", "state_conv", "g_mix", "w_in", "w_dw", "b_dw", "g_cn", "b_cn",
        "w_pw", "g_q", "g_k", "w_out", "g_ff", "w_ff1", "w_ff2"]
_OUTS = [(1, SEQ, D), (1, DEC, D), (1, 1, SEQ, NH, HD), (1, 1, SEQ, NH, HD), (1, 1, HIST, CC),
         (1, 1, DEC, NH, HD), (1, 1, DEC, NH, HD), (1, 1, HIST, CC)]


def kernel(**inputs):
    import numpy as np
    import concourse.bacc as bacc
    from concourse.bass_utils import run_bass_kernel_spmd

    nc = bacc.Bacc("TRN2", target_bir_lowering=False, num_devices=1)
    arrays, args = {}, []
    for name in _INS:
        a = np.ascontiguousarray(inputs[name])
        arrays[f"in_{name}"] = a
        args.append(nc.dram_tensor(f"in_{name}", a.shape, mybir.dt.from_np(a.dtype), kind="ExternalInput").ap())
    for i, shape in enumerate(_OUTS):
        args.append(nc.dram_tensor(f"out_{i}", shape, F32, kind="ExternalOutput").ap())
    build(nc, *args)
    r = run_bass_kernel_spmd(nc, [arrays], core_ids=[0])
    return tuple(r.results[0][f"out_{i}"] for i in range(len(_OUTS)))
```

```python
import concourse.bass as bass
from concourse import mybir
from collections import namedtuple
from contextlib import ExitStack

F32 = mybir.dt.float32
F32R = mybir.dt.float32r
ALU = mybir.AluOpType
ACT = mybir.ActivationFunctionType
AX = mybir.AxisListType

P = 128
D = 1024
KD = D // P
SEQ, DEC, PAST = 2048, 64, 128
NH, HD = 8, 64
AW = NH * HD
CC, CW = 512, 31
CB = CC // P
HIST = CW - 1
FF = 4096
EPS = 1e-6
BANK = 512
CHUNK = 512
NC = SEQ // CHUNK
TMAX = CHUNK + DEC
SLAB = 1024
RAW = 4
GROUPS = 24
G_AG, G_K, G_V, G_Q, G_PW, G_OUT, G_FF = 0, 2, 3, 4, 5, 6, 8
FFE = FF // P // 4
SMP = CHUNK + HIST
CVW = SMP + DEC
SIGMOIDS, SCAN, TURN, VALUES, OUTPUT = 1, 2, 4, 5, 6
NO_LIMIT, EXCLUDED = 3e38, -1e4


def tiles(c):
    t = [(P * i, P) for i in range(CHUNK // P)]
    return t + [(CHUNK, DEC)] if c == NC - 1 else t


def splits(c):
    return [(0, TMAX // 2), (TMAX // 2, TMAX // 2)] if c == NC - 1 else [(0, CHUNK)]


def conv_pieces(c):
    return [(0, 0, CHUNK)] + ([(SMP, CHUNK, DEC)] if c == NC - 1 else [])


def passes(c):
    prompt = [[(P * i, P, CHUNK * c + P * (i + 1)) for i in (2 * p, 2 * p + 1)] for p in range(2)]
    out = [(0, prompt)]
    if c == NC - 1:
        out.append((1, [[(0, DEC, PAST + DEC)]]))
    return out


Piece = namedtuple("Piece", "head p t q0 r a0 n diag last ends m tg v ob")


def key_groups(a, n):
    blocks = [((a + x) // P, min(P, n - x)) for x in range(0, n, P)]
    return [blocks[x:x + 4] for x in range(0, len(blocks), 4)]


def round_heads(kind):
    return NH if kind else 2


def att_sequence(kind, pairs):
    seq, m, tg, v = [], 0, 0, 0
    for head in range(round_heads(kind)):
        for p, pair in enumerate(pairs):
            parts = [(SLAB, 2 * SLAB), (0, SLAB)] if pair[0][2] > SLAB else [(0, SLAB)]
            for part, (a, b) in enumerate(parts):
                for t, (q0, r, keys) in enumerate(pair):
                    n = min(keys, b) - a
                    diag, last, ends = part == 0, part == len(parts) - 1, t == len(pair) - 1
                    seq.append(Piece(head, p, t, q0, r, a, n, diag, last, ends, m, tg, v, head * len(pairs) + p))
                    m += diag
                    tg += len(key_groups(a, n))
                    v += ends
    return seq


def behind(k, delay, pieces, first):
    j = k - delay
    if j < 0:
        return None if first else (-1, j + pieces)
    return (0, j) if j < pieces else None


def build(nc, x_prompt, x_sample, cache_k, cache_v, state_conv, g_mix, w_in, w_dw, b_dw, g_cn, b_cn, w_pw,
          g_q, g_k, w_out, g_ff, w_ff1, w_ff2, y_prompt, y_sample, nk_prompt, nv_prompt, ncv_prompt,
          nk_sample, nv_sample, ncv_sample):
    ctx = ExitStack()
    with ctx:
        base = (nc.sbuf_base + 31) // 32 * 32
        at = [base]

        def place(name, shape, dt=F32, offset=None):
            n = 4
            for s in shape[1:]:
                n *= s
            if offset is None:
                offset = at[0]
                at[0] += (n + 31) // 32 * 32
            return nc.alloc_sbuf_tensor_at(name, shape, dt, offset=offset)

        o_w = at[0]
        half = 2 * 4 * SLAB * 4
        at[0] += 2 * half
        w_hi = [place(f"w_hi{g}", [P, 4, SLAB], F32R, o_w + g * half) for g in range(2)]
        w_lo = [place(f"w_lo{g}", [P, 4, SLAB], F32R, o_w + g * half + half // 2) for g in range(2)]
        o_raw = at[0]
        w_raw = place("w_raw", [P, RAW, SLAB])
        resid = place("resid", [P, 5, D])
        o_h = at[0]
        hT_hi = place("hT_hi", [P, KD, TMAX], F32R)
        hT_lo = place("hT_lo", [P, KD, TMAX], F32R)
        o_mix = at[0]
        mixT_hi = place("mixT_hi", [P, KD, TMAX], F32R)
        mixT_lo = place("mixT_lo", [P, KD, TMAX], F32R)
        uT = place("uT", [P, CB, SMP + HIST + DEC])
        o_cv = at[0]
        cacc = place("cacc", [P, CB, CVW])
        cT_lo = place("cT_lo", [P, CB, CVW], F32R, o_cv)
        o_ch = at[0]
        cT_hi = place("cT_hi", [P, CB, CVW], F32R)
        o_grow = at[0]
        g_row = place("g_row", [P, D])
        vecs = place("vecs", [P, CB, CW + 3])
        gq = place("gq", [P, HD])
        gk = place("gk", [P, HD])
        ident = place("ident", [P, P])
        ones = place("ones", [P, P])
        neghalf = place("neghalf", [P, 1])
        unused = place("unused", [P, 1])
        ssum = place("ssum", [P, 5])
        rstd = place("rstd", [P, 5])
        hss = place("hss", [P, 2, NH])
        hrs = place("hrs", [P, 2, NH])
        limit = place("limit", [P, P])
        xin = place("xin", [P, 5, D], offset=o_mix + 8192)
        squares = [place("squares0", [P, D], offset=o_mix + 32768),
                   place("squares1", [P, D], offset=o_cv + 8192)]
        xn = place("xn", [P, 2, D], offset=o_cv)
        ckT = place("ckT", [P, NH, P], F32R, o_cv + 4096)
        kqT = place("kqT", [P, NH, TMAX], F32R, o_mix)
        o_t = o_mix + NH * TMAX * 4
        raw_kq = place("raw_kq", [P, 2, AW], offset=o_t)
        sqr = place("sqr", [P, AW], offset=o_t + 4096)
        kn = place("kn", [P, 2, AW], offset=o_t + 6144)
        packed = place("packed", [P, 2, NH, P], F32R, o_t + 10240)
        vout = place("vout", [P, 2, AW], offset=o_ch)
        vpack_o = o_ch + 4096
        vpack = place("vpack", [P, NH, P], F32R, vpack_o)
        sgate = place("sgate", [P, 2, BANK], offset=o_t)
        csq = place("csq", [P, CB, CVW], offset=o_ch)
        lnv = place("lnv", [P, BANK], offset=o_t)
        lnr = place("lnr", [P, BANK], offset=o_t + 2048)
        ntmp = place("ntmp", [P, BANK], offset=o_t + 4096)
        csig = place("csig", [P, 2, BANK], offset=o_t + 4096)
        cid = place("cid", [P, 2, BANK], offset=o_t + 8192)
        cvout = place("cvout", [HIST, 2, CC], offset=o_t + 12288)
        hid_hi = place("hid_hi", [P, 4, TMAX], F32R, o_cv)
        hid_lo = place("hid_lo", [P, 4, TMAX], F32R, o_cv + 4 * TMAX * 4)
        frel = place("frel", [P, 2, BANK], offset=o_mix)
        fsq = place("fsq", [P, 2, BANK], offset=o_mix + 4096)
        KB, VB, QB = SEQ * 4, (SEQ // P) * P * 4, 2 * CHUNK * 4
        a_k = [place(f"a_k{b}", [P, SEQ], F32R, o_h + b * KB) for b in range(2)]
        a_v = [place(f"a_v{b}", [P, SEQ // P, P], F32R, o_h + 2 * KB + b * VB) for b in range(2)]
        a_q = [place("a_q0", [P, 2, CHUNK], F32R, o_h + 2 * KB + 2 * VB),
               place("a_q1", [P, 2, CHUNK], F32R, o_grow)]
        beta = [place(f"beta{i}", [P, SLAB], F32, o_raw + i * SLAB * 4) for i in range(4)]
        stay = [place(f"stay{i}", [P, SLAB], F32, o_cv + i * SLAB * 4) for i in range(4)]
        aT_hi = place("aT_hi", [P, SEQ // P, 2 * P], F32R, o_w + half)
        aT_lo = place("aT_lo", [P, SEQ // P, 2 * P], F32R, o_w + half + half // 2)
        osb = place("osb", [P, 2 * P], offset=o_cv + 4 * SLAB * 4)
        of = place("of", [P, 2 * P], offset=o_cv + 4 * SLAB * 4 + 1024)
        crow = place("crow", [CW + 3, CC], offset=o_cv)
        srow = place("srow", [HIST, CC], offset=o_cv + 2048)

        ps = ctx.enter_context(nc.psum_tensor("ps", [P, 8, BANK], F32))

        k_d = nc.dram_tensor("k_scratch", [NH, P, SEQ], F32).ap()
        v_d = nc.dram_tensor("v_scratch", [NH, P, SEQ // P, P], F32).ap()
        q_d = nc.dram_tensor("q_scratch", [NH, P, SEQ + DEC], F32).ap()
        ks_d = nc.dram_tensor("ks_scratch", [NH, P, PAST + DEC], F32).ap()
        vs_d = nc.dram_tensor("vs_scratch", [NH, P, 2, P], F32).ap()

        def sem(name):
            return ctx.enter_context(nc.semaphore(name))

        raw_in = [sem(f"raw_in{j}") for j in range(RAW)]
        hi_done, lo_done = sem("hi_done"), sem("lo_done")
        consts, rows_in, vec_t, vec_ok, gains_in = (sem(n) for n in (
            "consts", "rows_in", "vec_t", "vec_ok", "gains_in"))
        ck_in, cv_in, ck_hi, ck_lo, cv_hi, cv_lo, ckT_ps, ckT_ok, cache_out = (sem(n) for n in (
            "ck_in", "cv_in", "ck_hi", "ck_lo", "cv_hi", "cv_lo", "ckT_ps", "ckT_ok", "cache_out"))
        x_in = [sem(f"x_in{i}") for i in range(5)]
        resid_in = [sem(f"resid_in{i}") for i in range(5)]
        grow_in, n_ss, n_var, n_rstd, n_xn, n_tp, n_hi, n_lo = (sem(n) for n in (
            "grow_in", "n_ss", "n_var", "n_rstd", "n_xn", "n_tp", "n_hi", "n_lo"))
        ag_ps, ag_sig, ag_u, hist_ok, taps = (sem(n) for n in ("ag_ps", "ag_sig", "ag_u", "hist_ok", "taps"))
        kvq_ps, kvq_cp, kq_sq, kq_ss, kq_var, kq_rs, kq_mul, kq_n, pk_hi, pk_lo, v_lo, kqT_ps, kqT_ok = (sem(n) for n in (
            "kvq_ps", "kvq_cp", "kq_sq", "kq_ss", "kq_var", "kq_rs", "kq_mul", "kq_n", "pk_hi", "pk_lo", "v_lo",
            "kqT_ps", "kqT_ok"))
        kn_out = [sem(f"kn_out{i}") for i in range(2)]
        vo_out = [sem(f"vo_out{i}") for i in range(2)]
        vp_out, kT_out, qT_out = sem("vp_out"), sem("kT_out"), sem("qT_out")
        lg_ok, sd_ok, id_ok, nwt = sem("lg_ok"), sem("sd_ok"), sem("id_ok"), sem("nwt")
        mean_ps, xc_ok, sq_ok, var_ps, var_ok, lnr_ok, yn_ok, sg_ok, cm_ok, c_hi, c_lo, cvo_ps, cvo_ok, cvo_out = (
            sem(n) for n in ("mean_ps", "xc_ok", "sq_ok", "var_ps", "var_ok", "lnr_ok", "yn_ok", "sg_ok", "cm_ok",
                             "c_hi", "c_lo", "cvo_ps", "cvo_ok", "cvo_out"))
        pw_ps, pw_hi, pw_lo, out_ps, out_add = (sem(n) for n in ("pw_ps", "pw_hi", "pw_lo", "out_ps", "out_add"))
        kq_in = [sem(f"kq_in{b}") for b in range(2)]
        v_in = [sem(f"v_in{b}") for b in range(2)]
        z_ps, z_msk, s_sg, s_scan, s_a, t_ps, t_hi, t_lo, v_ps, o_cp, o_sum, o_hi, o_lo = (
            sem(n) for n in ("z_ps", "z_msk", "s_sg", "s_scan", "s_a", "t_ps", "t_hi", "t_lo", "v_ps", "o_cp", "o_sum", "o_hi", "o_lo"))
        f1_ps, f_rel, f_sq, f_hi, f_lo, f2_ps, f2_add = (sem(n) for n in (
            "f1_ps", "f_rel", "f_sq", "f_hi", "f_lo", "f2_ps", "f2_add"))
        y_out = [sem(f"y_out{i}") for i in range(5)]

        def norm_base(c, which):
            return 2 * 4 * c + which * len(tiles(c))

        def att_counts(c, kind):
            before = dict(z=0, m=0, t=0, v=0, o=0)
            for cc in range(NC):
                for k, pairs in passes(cc):
                    seq = att_sequence(k, pairs)
                    n = dict(z=len(seq), m=sum(q.diag for q in seq), t=sum(len(key_groups(q.a0, q.n)) for q in seq),
                             v=sum(q.ends for q in seq), o=seq[-1].ob + 1)
                    if (cc, k) == (c, kind):
                        return before, n
                    for key in before:
                        before[key] += n[key] * NH // round_heads(k)
            return before, None

        def att_counter(c, kind):
            before, cn = att_counts(c, kind)

            def cnt(what, n, it, rel):
                return it * cn[what] + (before[what] + rel * cn[what] + n)
            return cnt

        def turned(q):
            return q.tg + len(key_groups(q.a0, q.n))

        def aT_blocks(q, grp):
            return [(b - q.a0 // P + KD * (q.v % 2), w) for b, w in grp]

        def kvq_events(c):
            nt = len(tiles(c))
            return ([("k", i, i) for i in range(nt)] + [("v", i, None) for i in range(nt)]
                    + [("q", i, nt + i) for i in range(nt)])

        TAPS = CB * CW
        EARLY = 19

        def tap_order():
            left, order = [CW] * CB, []
            while len(order) < TAPS:
                ready = min(len(order) // EARLY + 1, CB)
                for k in range(ready):
                    room = ready == CB or len(order) < EARLY * ready
                    if left[k] and room:
                        order.append((k, CW - left[k]))
                        left[k] -= 1
                if not any(left[:ready]) and ready < CB:
                    raise ValueError("too many early taps")
            return order

        taps_in_order = tap_order()

        def taps_of(c, e):
            share = [3 if sec == "v" else 1 for sec, i, m in kvq_events(c)]
            rest, total = TAPS - 3 * EARLY, sum(share)
            return range(3 * EARLY + rest * sum(share[:e]) // total, 3 * EARLY + rest * sum(share[:e + 1]) // total)

        def evacuate(copy, sub, dst, grp, t, r, bank, done):
            w0 = grp[0][1]
            b0, n = grp[0][0], len(grp)
            same = [x for x in grp if x[1] == w0]
            parts = [(b0, len(same), w0, 0)]
            if len(same) < n:
                parts.append((b0 + len(same), 1, grp[-1][1], len(same)))
            for q, (b, m, w, k0) in enumerate(parts):
                o = dst[0:w, b:b + m, t * P:t * P + r]
                i = bank[0:w, k0 * r:(k0 + m) * r].rearrange("p (a b) -> p a b", a=m)
                ins = copy(o, i) if sub is None else copy(o, i, sub[0:w, b:b + m, t * P:t * P + r].bitcast(F32), ALU.subtract)
                if q == len(parts) - 1:
                    ins.then_inc(done, 1)

        def bank(k, r, x0, x1):
            return ps[0:r, 2 * (k % 2):2 * (k % 2) + 2, :].rearrange("p a b -> p (a b)")[:, x0:x1]

        block = ctx.enter_context(nc.Block())

        def att_outputs(c):
            kind = passes(c)[-1][0]
            before, n = att_counts(c, kind)
            return before["o"] + n["o"] * NH // round_heads(kind)

        @block.sync
        def _(sp):
            def load_slab(slab, src, width=None):
                j = slab % RAW
                if not isinstance(slab, int) or slab >= RAW:
                    sp.wait_ge(lo_done, slab - RAW + 1)
                dst = w_raw[:, j, :] if width is None else w_raw[:, j, 0:width]
                if len(src.shape) == 3:
                    dst = dst.rearrange("p (a b) -> p a b", a=src.shape[1])
                sp.dma_start(dst, src).then_inc(raw_in[j], 16)

            w_in_k = w_in[0].rearrange("(k p) n -> p k n", p=P)
            w_out_k = w_out[0].rearrange("(k p) n -> p k n", p=P)
            w_pw_k = w_pw[0].rearrange("(k p) n -> p k n", p=P)
            w1_k = w_ff1[0].rearrange("(k p) n -> p k n", p=P)
            w2_k = w_ff2[0].rearrange("(k p) n -> p k n", p=P)

            def load_group(c, g):
                if c >= NC:
                    return
                for j in range(4):
                    slab = 4 * (GROUPS * c + g) + j
                    if g < G_K:
                        col = (j % 2) * CC + (2 * g + j // 2) * P
                        src = w_in_k[:, :, col:col + P]
                    elif g <= G_Q:
                        col = 2 * CC + {G_K: 1, G_V: 2, G_Q: 0}[g] * AW
                        src = w_in_k[:, 2 * j:2 * j + 2, col:col + AW]
                    elif g == G_PW:
                        src = w_pw_k[:, j, :]
                    elif g < G_FF:
                        hf = g - G_OUT
                        src = w_out_k[:, 2 * j:2 * j + 2, hf * BANK:(hf + 1) * BANK]
                    load_slab(slab, src, CC if g == G_PW else None)

            def load_ff1(c, e):
                for j in range(4):
                    col = 4 * e + j
                    sl = bass.ts(col, P)
                    n = 4 * (GROUPS * c + G_FF) + 8 * e + j
                    sp.wait_ge(lo_done, n - RAW + 1)
                    sp.dma_start(w_raw[:, j, :].rearrange("p (a b) -> p a b", a=KD),
                                 w1_k[:, :, sl]).then_inc(raw_in[j], 16)

            def load_ff2(c, e):
                for j in range(4):
                    n = 4 * (GROUPS * c + G_FF + 1) + 8 * e + j
                    sp.wait_ge(lo_done, n - RAW + 1)
                    sp.dma_start(w_raw[:, j, :], w2_k[:, 4 * e + j, :]).then_inc(raw_in[j], 16)

            def load_gain(c, which):
                g = (g_mix if which == 0 else g_ff)[0:1, :]
                if c or which:
                    sp.wait_ge(n_xn, norm_base(c, which))
                sp.dma_start(g_row[:], g.partition_broadcast(P)[:, 0, :]).then_inc(grow_in, 16)

            def load_tokens(c, dst, done):
                for i, (q0, r) in enumerate(tiles(c)):
                    src = x_prompt[0, c * CHUNK + q0:c * CHUNK + q0 + r, :] if i < 4 else x_sample[0]
                    if dst is resid and c and i < 4:
                        sp.wait_ge(y_out[i], 16 * c)
                    sp.dma_start(dst[0:r, i, :], src).then_inc(done[i], 16)

            load_tokens(0, xin, x_in)
            load_gain(0, 0)
            sp.dma_start(crow[0:CW, :], w_dw[0]).then_inc(rows_in, 16)
            sp.dma_start(crow[CW:CW + 1, :], b_dw[0:1, :]).then_inc(rows_in, 16)
            sp.dma_start(crow[CW + 1:CW + 2, :], g_cn[0:1, :]).then_inc(rows_in, 16)
            sp.dma_start(crow[CW + 2:CW + 3, :], b_cn[0:1, :]).then_inc(rows_in, 16)
            sp.dma_start(srow[:], state_conv[0, 0]).then_inc(rows_in, 16)
            sp.dma_start(gq[:], g_q[0:1, :].partition_broadcast(P)[:, 0, :]).then_inc(gains_in, 16)
            sp.dma_start(gk[:], g_k[0:1, :].partition_broadcast(P)[:, 0, :]).then_inc(gains_in, 16)
            sp.dma_start(kn[:, 0, :], cache_k[0, 0].rearrange("t h d -> t (h d)")).then_inc(ck_in, 16)
            sp.dma_start(vout[:, 0, :], cache_v[0, 0].rearrange("t h d -> t (h d)")).then_inc(cv_in, 16)
            for c in range(NC):
                tl = tiles(c)
                nt = len(tl)
                t0 = c * CHUNK
                if c == 0:
                    load_group(0, 0)
                    load_group(0, 1)
                    sp.wait_ge(ckT_ok, 2)
                    sp.dma_start(ks_d[:, :, 0:PAST].rearrange("h p k -> p h k"),
                                 ckT[:].bitcast(F32)).then_inc(cache_out, 16)
                    sp.wait_ge(cv_lo, 1)
                    sp.dma_start(vs_d[:, :, 0, :].rearrange("h p k -> p h k"), vpack[:].bitcast(F32)).then_inc(cache_out, 16)
                load_tokens(c, resid, resid_in)
                load_group(c, 2)
                load_group(c, 3)
                kq0 = 2 * 4 * c
                for s, (sec, i, m) in enumerate(kvq_events(c)):
                    q0, r = tl[i]
                    if sec == "k":
                        sp.wait_ge(kq_n, kq0 + m + 1)
                        dst = nk_prompt[0, 0, t0 + q0:t0 + q0 + r] if i < 4 else nk_sample[0, 0]
                        sp.dma_start(dst.rearrange("t h d -> t (h d)"), kn[0:r, m % 2, :]).then_inc(kn_out[m % 2], 16)
                        if i == 1:
                            load_group(c, G_Q)
                    elif sec == "v":
                        sp.wait_ge(v_lo, 4 * c + i + 1)
                        dst = nv_prompt[0, 0, t0 + q0:t0 + q0 + r] if i < 4 else nv_sample[0, 0]
                        sp.dma_start(dst.rearrange("t h d -> t (h d)"), vout[0:r, i % 2, :]).then_inc(vo_out[i % 2], 16)
                        dst = (v_d[:, :, 4 * c + i, :] if i < 4 else vs_d[:, 0:r, 1, :]).rearrange("h p k -> p h k")
                        sp.dma_start(dst, vpack[0:r].bitcast(F32)).then_inc(vp_out, 16)
                        if i == 1:
                            sp.wait_ge(kqT_ok, 2 * (kq0 + nt))
                            sp.dma_start(k_d[:, :, t0:t0 + CHUNK].rearrange("h p k -> p h k"),
                                         kqT[:, :, 0:CHUNK].bitcast(F32)).then_inc(kT_out, 16)
                            if c == NC - 1:
                                sp.dma_start(ks_d[:, :, PAST:PAST + DEC].rearrange("h p k -> p h k"),
                                             kqT[:, :, CHUNK:TMAX].bitcast(F32)).then_inc(kT_out, 16)
                        if i == 2:
                            load_group(c, G_PW)
                load_group(c, G_OUT)
                sp.wait_ge(kqT_ok, 2 * (kq0 + 2 * nt))
                T = tl[-1][0] + tl[-1][1]
                sp.dma_start(q_d[:, :, t0:t0 + T].rearrange("h p k -> p h k"),
                             kqT[:, :, 0:T].bitcast(F32)).then_inc(qT_out, 16)
                if c == NC - 1:
                    sp.wait_ge(cvo_ok, 2)
                    sp.dma_start(ncv_prompt[0, 0], cvout[:, 0, :]).then_inc(cvo_out, 16)
                    sp.dma_start(ncv_sample[0, 0], cvout[:, 1, :]).then_inc(cvo_out, 16)
                sp.wait_ge(kT_out, 16 * (c + 1 + (c == NC - 1)))
                sp.wait_ge(vp_out, 16 * (4 * c + nt))
                sp.wait_ge(qT_out, 16 * (c + 1))
                sp.wait_ge(cache_out, 32)
                sp.wait_ge(kvq_ps, 3 * (4 * c + nt))
                for kind, pairs in passes(c):
                    cnt = att_counter(c, kind)
                    before, n = att_counts(c, kind)

                    def load_keys(it, b):
                        h = 2 * it + b
                        nk = CHUNK * (c + 1)
                        sp.dma_start(a_k[b][:, 0:nk].bitcast(F32), k_d[h, :, 0:nk]).then_inc(kq_in[b], 16)
                        sp.dma_start(a_q[b][:, 0, :].bitcast(F32), q_d[h, :, t0:t0 + CHUNK]).then_inc(kq_in[b], 16)
                        for p0 in (0, HD):
                            sp.dma_start(a_q[b][p0:p0 + HD, 1, :].bitcast(F32),
                                         q_d[h, HD - p0:P - p0, t0:t0 + CHUNK]).then_inc(kq_in[b], 16)

                    def load_values(it, b):
                        h = 2 * it + b
                        nb = CB * (c + 1)
                        sp.dma_start(a_v[b][:, 0:nb, :].bitcast(F32), v_d[h, :, 0:nb, :]).then_inc(v_in[b], 16)

                    def load_running():
                        sp.dma_start(a_k[0][:, 0:NH * (PAST + DEC)].bitcast(F32).rearrange("p (h k) -> p h k", h=NH),
                                     ks_d.rearrange("h p k -> p h k")).then_inc(kq_in[0], 16)
                        qv = [a_q[0][:, v, :].bitcast(F32).rearrange("p (h k) -> p h k", h=NH) for v in range(2)]
                        sp.dma_start(qv[0], q_d[:, :, SEQ:SEQ + DEC].rearrange("h p k -> p h k")).then_inc(kq_in[0], 16)
                        for p0 in (0, HD):
                            sp.dma_start(qv[1][p0:p0 + HD],
                                         q_d[:, HD - p0:P - p0, SEQ:SEQ + DEC].rearrange("h p k -> p h k")).then_inc(kq_in[0], 16)
                        sp.wait_ge(v_ps, slot0_used["v"])
                        for b, rows in ((0, P), (1, DEC)):
                            sp.dma_start(a_v[0][0:rows, b:2 * NH:2, :].bitcast(F32),
                                         vs_d[:, 0:rows, b, :].rearrange("h p k -> p h k")).then_inc(v_in[0], 16)

                    if kind == 0:
                        sp.wait_ge(o_lo, before["o"] + 1)
                        for b in range(2):
                            load_keys(0, b)
                            load_values(0, b)
                        with sp.Fori(1, NH // 2) as it:
                            for b in range(2):
                                sp.wait_ge(z_ps, cnt("z", (b + 1) * (n["z"] // 2), it, -1))
                                load_keys(it, b)
                                sp.wait_ge(v_ps, cnt("v", (b + 1) * (n["v"] // 2), it, -1))
                                load_values(it, b)
                        slot0_used = {x: cnt(x, n[x] // 2, NH // 2 - 1, 0) for x in "zv"}
                    else:
                        sp.wait_ge(z_ps, slot0_used["z"])
                        load_running()
                sp.wait_ge(o_lo, att_outputs(c) + 1)
                load_group(c, G_OUT + 1)
                load_gain(c, 1)
                load_ff1(c, 0)
                if c + 1 < NC:
                    sp.wait_ge(out_ps, 2 * (4 * c + nt))
                    load_tokens(c + 1, xin, x_in)
                    load_gain(c + 1, 0)
                with sp.Fori(0, FFE - 1) as e:
                    load_ff2(c, e)
                    load_ff1(c, e + 1)
                load_ff2(c, FFE - 1)
                load_group(c + 1, 0)
                load_group(c + 1, 1)
                for i, (q0, r) in enumerate(tl):
                    sp.wait_ge(f2_add, 2 * (4 * c * FFE + (FFE - 1) * nt + i + 1))
                    dst = y_prompt[0, t0 + q0:t0 + q0 + r, :] if i < 4 else y_sample[0]
                    sp.dma_start(dst, resid[0:r, i, :]).then_inc(y_out[i], 16)
            for i in range(4):
                sp.wait_ge(y_out[i], 16 * NC)
            sp.wait_ge(y_out[4], 16)
            sp.wait_ge(kn_out[0], 16 * (2 * NC + 1))
            sp.wait_ge(kn_out[1], 16 * 2 * NC)
            sp.wait_ge(vo_out[0], 16 * (2 * NC + 1))
            sp.wait_ge(vo_out[1], 16 * 2 * NC)
            sp.wait_ge(cvo_out, 32)

        @block.gpsimd
        def _(pool):
            def split_lo(c, g, j, width=SLAB):
                n = 4 * (GROUPS * c + g) + j
                pool.wait_ge(hi_done, n + 1)
                nc.gpsimd.tensor_tensor(w_lo[g % 2][:, j, 0:width], w_raw[:, j, 0:width],
                                        w_hi[g % 2][:, j, 0:width].bitcast(F32), ALU.subtract).then_inc(lo_done, 1)

            def split_lo_group(c, g):
                if g == GROUPS:
                    c, g = c + 1, 0
                if c < NC:
                    for j in range(4):
                        split_lo(c, g, j, CC if g == G_PW else SLAB)

            def norm(c, which):
                nb = norm_base(c, which)
                for i, (q0, r) in enumerate(tiles(c)):
                    pool.wait_ge(n_ss, nb + i + 1)
                    if i == 0 and nb:
                        pool.wait_ge(n_xn, nb)
                    nc.gpsimd.tensor_scalar(rstd[0:r, i:i + 1], ssum[0:r, i:i + 1], 1.0 / D, EPS,
                                            ALU.mult, ALU.add).then_inc(n_var, 1)
                    pool.wait_ge(n_var, nb + i + 1)
                    nc.gpsimd.tensor_tensor(rstd[0:r, i:i + 1], rstd[0:r, i:i + 1], neghalf[0:r, :],
                                            ALU.pow).then_inc(n_rstd, 1)

            nc.gpsimd.memset(ident[:], 0.0).then_inc(consts, 1)
            nc.gpsimd.memset(ones[:], 1.0).then_inc(consts, 1)
            nc.gpsimd.memset(neghalf[:], -0.5).then_inc(consts, 1)
            pool.wait_ge(consts, 3)
            nc.gpsimd.affine_select(out=ident[:], in_=ident[:], compare_op=ALU.not_equal, fill=1.0, base=0,
                                    pattern=[[-1, P]], channel_multiplier=1).then_inc(consts, 1)
            nc.gpsimd.memset(limit[:], NO_LIMIT).then_inc(consts, 1)
            pool.wait_ge(consts, 5)
            nc.gpsimd.affine_select(out=limit[:], in_=limit[:], compare_op=ALU.is_gt, fill=EXCLUDED, base=0,
                                    pattern=[[-1, P]], channel_multiplier=1).then_inc(consts, 1)
            for c in range(NC):
                nt = len(tiles(c))
                if c == 0:
                    norm(0, 0)
                    split_lo_group(0, 0)
                split_lo_group(c, 1)
                split_lo_group(c, 2)
                split_lo_group(c, G_V)
                kq0 = 8 * c
                for s, (sec, i, m) in enumerate(kvq_events(c)):
                    if m is not None:
                        u = kq0 + m
                        rr = tiles(c)[i][1]
                        pool.wait_ge(kvq_cp, 12 * c + s + 1)
                        if u == 0:
                            pool.wait_ge(hist_ok, 2)
                        v = raw_kq[0:rr, m % 2, :].rearrange("p (h d) -> p h d", h=NH)
                        gain = gk if sec == "k" else gq
                        nc.gpsimd.tensor_tensor(v, v, gain[0:rr, :].unsqueeze(1).to_broadcast([rr, NH, HD]),
                                                ALU.mult).then_inc(kq_mul, 1)
                        pool.wait_ge(kq_ss, u + 1)
                        nc.gpsimd.tensor_scalar(hrs[0:rr, m % 2, :], hss[0:rr, m % 2, :], 1.0 / HD, EPS,
                                                ALU.mult, ALU.add).then_inc(kq_var, 1)
                        pool.wait_ge(kq_var, u + 1)
                        nc.gpsimd.tensor_tensor(hrs[0:rr, m % 2, :], hrs[0:rr, m % 2, :],
                                                neghalf[0:rr, :].to_broadcast([rr, NH]), ALU.pow).then_inc(kq_rs, 1)
                    if sec != "k" and i < 4:
                        g = {"v": G_Q, "q": G_PW}[sec]
                        split_lo(c, g, i, CC if g == G_PW else SLAB)
                split_lo_group(c, G_OUT)
                pool.wait_ge(kn_out[0], 16 * (2 * c + (nt + 1) // 2))
                pool.wait_ge(kn_out[1], 16 * (2 * c + nt // 2))
                for n, (a, q0, w) in enumerate(conv_pieces(c)):
                    lb = c + n
                    for k in range(CB):
                        pool.wait_ge(yn_ok, CB * lb + k + 1)
                        if CB * lb + k >= 2:
                            pool.wait_ge(cm_ok, CB * lb + k - 1)
                        nc.gpsimd.tensor_scalar(cid[:, k % 2, 0:w], cacc[:, k, a:a + w], vecs[:, k, CW + 1:CW + 2],
                                                vecs[:, k, CW + 2:CW + 3], ALU.mult, ALU.add).then_inc(id_ok, 1)
                for kind, pairs in passes(c):
                    cnt = att_counter(c, kind)
                    seq = att_sequence(kind, pairs)
                    L = len(seq)

                    def weights(k, it, rel):
                        q = seq[k]
                        v, n = beta[k % 4], q.n
                        pool.wait_ge(s_scan, cnt("z", k + 1, it, rel))
                        nc.gpsimd.tensor_tensor(v[0:q.r, 0:n - 1], v[0:q.r, 0:n - 1], stay[k % 4][0:q.r, 1:n],
                                                ALU.mult).then_inc(s_a, 1)

                    def steps(it, ks, first=False):
                        for k in ks:
                            if who := behind(k, SCAN, L, first):
                                weights(who[1], it, who[0])

                    rounds = NH // round_heads(kind)
                    steps(0, range(L), first=True)
                    if rounds > 1:
                        with pool.Fori(1, rounds) as it:
                            steps(it, range(L))
                    steps(rounds - 1, range(L, L + SCAN))
                split_lo_group(c, G_OUT + 1)
                split_lo_group(c, G_FF)
                norm(c, 1)
                with pool.Fori(0, FFE - 1) as e:
                    for g in (G_FF + 1, G_FF + 2):
                        for j in range(4):
                            n = 4 * (GROUPS * c + g) + 8 * e + j
                            pool.wait_ge(hi_done, n + 1)
                            nc.gpsimd.tensor_tensor(w_lo[g % 2][:, j, :], w_raw[:, j, :],
                                                    w_hi[g % 2][:, j, :].bitcast(F32), ALU.subtract).then_inc(lo_done, 1)
                if c + 1 < NC:
                    norm(c + 1, 0)
                split_lo_group(c, GROUPS - 1)
                split_lo_group(c, GROUPS)

        @block.scalar
        def _(act):
            def split_hi(c, g, j, width=SLAB, e=None):
                act.wait_ge(raw_in[j], 16 * (GROUPS * c + g + 1) + (32 * e if e is not None else 0))
                nc.scalar.copy(w_hi[g % 2][:, j, 0:width], w_raw[:, j, 0:width]).then_inc(hi_done, 1)

            def split_hi_group(c, g):
                if g == GROUPS:
                    c, g = c + 1, 0
                if c < NC:
                    for j in range(4):
                        split_hi(c, g, j, CC if g == G_PW else SLAB)

            def norm_squares(c, which, i):
                nb = norm_base(c, which)
                r = tiles(c)[i][1]
                if which == 0:
                    act.wait_ge(x_in[i], 16 * ((c if i < 4 else 0) + 1))
                else:
                    act.wait_ge(out_add, 8 * c + len(tiles(c)) + i + 1)
                if i == 0 and nb:
                    act.wait_ge(n_rstd, nb)
                if i:
                    act.wait_ge(n_ss, nb + i)
                src = (resid if which else xin)[0:r, i, :]
                nc.scalar.activation(squares[which][0:r, :], src, ACT.Square, accum_out=ssum[0:r, i:i + 1]).then_inc(n_ss, 1)

            def norm_hi(c, which, i):
                q0, r = tiles(c)[i]
                for hf in range(2):
                    ev = 2 * (norm_base(c, which) + i) + hf
                    act.wait_ge(n_tp, ev + 1)
                    nc.scalar.copy(hT_hi[:, 4 * hf:4 * hf + 4, q0:q0 + r],
                                   ps[:, (2 * i + hf) % 4, 0:4 * r].rearrange("p (a b) -> p a b", a=4)).then_inc(n_hi, 1)

            act.wait_ge(consts, 4)
            for i in range(len(tiles(0))):
                norm_squares(0, 0, i)
            act.wait_ge(vec_t, 1)
            nc.scalar.copy(vecs[:], ps[:, 4, 0:CB * (CW + 3)].rearrange("p (a b) -> p a b", a=CB)).then_inc(vec_ok, 1)
            act.wait_ge(vec_t, 2)
            nc.scalar.copy(uT[:, :, SMP:SMP + HIST], ps[:, 5, 0:CB * HIST].rearrange("p (a b) -> p a b", a=CB)).then_inc(vec_ok, 1)
            act.wait_ge(ck_in, 16)
            nc.scalar.copy(packed[:, 0, :, 0:HD], kn[:, 0, :].rearrange("p (h d) -> p h d", h=NH)).then_inc(ck_hi, 1)
            act.wait_ge(cv_in, 16)
            nc.scalar.copy(vpack[:, :, 0:HD], vout[:, 0, :].rearrange("p (h d) -> p h d", h=NH)).then_inc(cv_hi, 1)
            for q in range(2):
                act.wait_ge(ckT_ps, q + 1)
                nc.scalar.copy(ckT[:, 4 * q:4 * q + 4, :],
                               ps[:, 6 + q, :].rearrange("p (a b) -> p a b", a=4)).then_inc(ckT_ok, 1)
            for c in range(NC):
                tl = tiles(c)
                nt = len(tl)
                sp_ = splits(c)
                ns = len(sp_)
                if c == 0:
                    split_hi_group(0, 0)
                    for i in range(nt):
                        norm_hi(0, 0, i)
                for g in range(2):
                    split_hi_group(c, g + 1)
                    for pr in range(2):
                        for s, (s0, w) in enumerate(sp_):
                            ev = 8 * c + (4 * g + 2 * pr + 1) * ns + s
                            u = 4 * c + (2 * g + pr) * ns + s
                            act.wait_ge(ag_ps, ev + 1)
                            if u >= 2:
                                act.wait_ge(ag_u, u - 1)
                            if c == 0 and g == 0 and pr == 0 and s == 0:
                                act.wait_ge(vec_ok, 2)
                                act.wait_ge(vec_t, 2)
                            nc.scalar.activation(sgate[:, u % 2, 0:w], ps[:, (ev - 8 * c) % 4, 0:w],
                                                 ACT.Sigmoid).then_inc(ag_sig, 1)
                        if g == 1:
                            split_hi(c, G_V, 2 * pr)
                            split_hi(c, G_V, 2 * pr + 1)
                ev0 = 12 * c
                kq0 = 8 * c
                evs = kvq_events(c)
                act.wait_ge(ag_u, 4 * c + 4 * ns)
                act.wait_ge(cache_out, 32)
                for s in range(len(evs) + 3):
                    if s < len(evs):
                        sec, i, m = evs[s]
                        r = tl[i][1]
                        act.wait_ge(kvq_ps, ev0 + s + 1)
                        src = ps[0:r, 4 + s % 4, :]
                        if sec == "v":
                            k = i % 2
                            n = 2 * c + i // 2
                            if n:
                                act.wait_ge(vo_out[k], 16 * n)
                            if i >= 2:
                                act.wait_ge(v_lo, 4 * c + i - 1)
                            nc.scalar.copy(vout[0:r, k, :], src).then_inc(kvq_cp, 1)
                        else:
                            if m >= 2:
                                act.wait_ge(kq_n, kq0 + m - 1)
                            if kq0 + m:
                                act.wait_ge(kq_ss, kq0 + m)
                            nc.scalar.activation(sqr[0:r, :], src, ACT.Square).then_inc(kq_sq, 1)
                            nc.scalar.copy(raw_kq[0:r, m % 2, :], src).then_inc(kvq_cp, 1)
                    if 1 <= s <= len(evs):
                        sec, i, m = evs[s - 1]
                        r = tl[i][1]
                        if sec == "v":
                            act.wait_ge(kvq_cp, ev0 + s)
                            if 4 * c + i:
                                act.wait_ge(vp_out, 16 * (4 * c + i))
                            nc.scalar.copy(vpack[0:r, :, 0:HD],
                                           vout[0:r, i % 2, :].rearrange("p (h d) -> p h d", h=NH)).then_inc(cv_hi, 1)
                        else:
                            act.wait_ge(kq_n, kq0 + m + 1)
                            if m >= 2:
                                act.wait_ge(kqT_ps, 2 * (kq0 + m - 1))
                            nc.scalar.copy(packed[0:r, m % 2, :, 0:HD],
                                           kn[0:r, m % 2, :].rearrange("p (h d) -> p h d", h=NH)).then_inc(pk_hi, 1)
                    if s >= 3:
                        sec, i, m = evs[s - 3]
                        q0, r = tl[i]
                        if sec != "v":
                            if sec == "q" and i == 0:
                                act.wait_ge(kT_out, 16 * (c + 1 + (c == NC - 1)))
                            for q in range(2):
                                act.wait_ge(kqT_ps, 2 * (kq0 + m) + q + 1)
                                nc.scalar.copy(kqT[:, 4 * q:4 * q + 4, q0:q0 + r],
                                               ps[:, q, 0:4 * r].rearrange("p (a b) -> p a b", a=4)).then_inc(kqT_ok, 1)
                    if s < len(evs) and evs[s][0] != "k" and evs[s][1] < 4:
                        g = {"v": G_Q, "q": G_PW}[evs[s][0]]
                        split_hi(c, g, evs[s][1], CC if g == G_PW else SLAB)
                split_hi_group(c, G_OUT)
                if c == NC - 1:
                    for q in range(2):
                        act.wait_ge(cvo_ps, q + 1)
                        nc.scalar.copy(cvout[:, q, :], ps[0:HIST, 4 + q, :]).then_inc(cvo_ok, 1)
                for n, (a, q0, w) in enumerate(conv_pieces(c)):
                    lb = c + n
                    for k in range(CB):
                        act.wait_ge(xc_ok, CB * lb + k + 1)
                        if k == 0:
                            act.wait_ge(vp_out, 16 * (4 * c + nt))
                            act.wait_ge(vo_out[0], 16 * (2 * c + (nt + 1) // 2))
                            act.wait_ge(vo_out[1], 16 * (2 * c + 2))
                        nc.scalar.activation(csq[:, k, a:a + w], cacc[:, k, a:a + w], ACT.Square).then_inc(sq_ok, 1)
                    act.wait_ge(var_ok, lb + 1)
                    nc.scalar.activation(lnr[:, 0:w], lnv[:, 0:w], ACT.Ln).then_inc(lg_ok, 1)
                    act.wait_ge(lg_ok, lb + 1)
                    nc.scalar.activation(lnr[:, 0:w], lnr[:, 0:w], ACT.Exp, scale=-0.5).then_inc(sd_ok, 1)
                    nc.scalar.activation(unused[:], ident[:, 0:1], ACT.Sigmoid)
                    act.wait_ge(kn_out[0], 16 * (2 * c + (nt + 1) // 2))
                    act.wait_ge(kn_out[1], 16 * (2 * c + nt // 2))
                    for k in range(CB + 1):
                        if k < CB:
                            act.wait_ge(yn_ok, CB * lb + k + 1)
                            if CB * lb + k >= 2:
                                act.wait_ge(cm_ok, CB * lb + k - 1)
                            nc.scalar.activation(csig[:, k % 2, 0:w], cacc[:, k, a:a + w], ACT.Sigmoid,
                                                 bias=vecs[:, k, CW + 2:CW + 3], scale=vecs[:, k, CW + 1:CW + 2]).then_inc(sg_ok, 1)
                        if k >= 1:
                            act.wait_ge(cm_ok, CB * lb + k)
                            if k == 1:
                                act.wait_ge(var_ps, lb + 1)
                            nc.scalar.copy(cT_hi[:, k - 1, a:a + w], cacc[:, k - 1, a:a + w]).then_inc(c_hi, 1)
                act.wait_ge(qT_out, 16 * (c + 1))
                for m in range(CB):
                    for n, (a, q0, w) in enumerate(conv_pieces(c)):
                        npc = len(conv_pieces(c))
                        ev = CB * c + npc * m + n
                        act.wait_ge(pw_ps, ev + 1)
                        nc.scalar.copy(mixT_hi[:, m, q0:q0 + w], ps[:, (ev - CB * c) % 4, 0:w]).then_inc(pw_hi, 1)
                if c == NC - 1:
                    act.wait_ge(cvo_out, 32)
                for kind, pairs in passes(c):
                    cnt = att_counter(c, kind)
                    seq = att_sequence(kind, pairs)
                    L = len(seq)

                    def sigmoids(k, it, rel, first):
                        q = seq[k]
                        if q.diag:
                            act.wait_ge(z_msk, cnt("m", q.m + 1, it, rel))
                        else:
                            act.wait_ge(z_ps, cnt("z", k + 1, it, rel))
                        if old := behind(k, 4, L, first):
                            act.wait_ge(t_ps, cnt("t", turned(seq[old[1]]), it, rel + old[0]))
                        if old := behind(k, 2, L, first):
                            act.wait_ge(s_scan, cnt("z", old[1] + 1, it, rel + old[0]))
                        z = bank(k, q.r, 0, q.n)
                        nc.scalar.activation(stay[k % 4][0:q.r, 0:q.n], z, ACT.Sigmoid, scale=-1.0)
                        nc.scalar.activation(beta[k % 4][0:q.r, 0:q.n], z, ACT.Sigmoid).then_inc(s_sg, 1)

                    def turned_hi(k, it, rel, first):
                        q = seq[k]
                        for gi, grp in enumerate(key_groups(q.a0, q.n)):
                            act.wait_ge(t_ps, cnt("t", q.tg + gi + 1, it, rel))
                            if q.t == 0 and gi == 0 and not (first and q.v < 2):
                                act.wait_ge(v_ps, cnt("v", q.v - 1, it, rel))
                            evacuate(nc.scalar.copy, None, aT_hi, aT_blocks(q, grp), q.t, q.r,
                                     ps[:, 4 + (q.tg + gi) % 2, :], t_hi)

                    def output(k, it, rel):
                        q = seq[k]
                        if q.last and q.ends:
                            w = sum(x[1] for x in pairs[q.p])
                            act.wait_ge(v_ps, cnt("v", q.v + 1, it, rel))
                            act.wait_ge(o_lo, cnt("o", q.ob + 1, it, rel))
                            mine = q.head % 2 * HD
                            nc.scalar.copy(osb[mine:mine + HD, 0:w],
                                           ps[HD - mine:P - mine, 6 + q.ob % 2, 0:w]).then_inc(o_cp, 1)

                    def steps(it, ks, first=False):
                        for k in ks:
                            if who := behind(k, SIGMOIDS, L, first):
                                sigmoids(who[1], it, who[0], first)
                            if who := behind(k, TURN, L, first):
                                turned_hi(who[1], it, who[0], first)
                            if who := behind(k, OUTPUT, L, first):
                                output(who[1], it, who[0])

                    act.wait_ge(lo_done, 4 * (GROUPS * c + G_OUT + 1))
                    rounds = NH // round_heads(kind)
                    steps(0, range(L), first=True)
                    if rounds > 1:
                        with act.Fori(1, rounds) as it:
                            steps(it, range(L))
                    steps(rounds - 1, range(L, L + OUTPUT))
                split_hi_group(c, G_OUT + 1)
                act.wait_ge(out_ps, 8 * c + nt)
                split_hi_group(c, G_FF)
                for i in range(nt + 1):
                    if i < nt:
                        norm_squares(c, 1, i)
                    if i >= 1:
                        norm_hi(c, 1, i - 1)
                f1b = 4 * FFE * c
                f2b = 8 * FFE * c + 1

                def hi_of(e, k):
                    j, s = k // ns, k % ns
                    s0, w = sp_[s]
                    act.wait_ge(f_sq, f1b + k + 1 + e * 4 * ns)
                    nc.scalar.copy(hid_hi[:, j, s0:s0 + w], fsq[:, k % 2, 0:w]).then_inc(f_hi, 1)

                def ff1(e):
                    for k in range(4 * ns):
                        w = sp_[k % ns][1]
                        act.wait_ge(f1_ps, f1b + k + 1 + e * 4 * ns)
                        if k >= 2:
                            act.wait_ge(f_sq, f1b + k - 1 + e * 4 * ns)
                        nc.scalar.activation(frel[:, k % 2, 0:w], ps[:, k % 4, 0:w], ACT.Relu).then_inc(f_rel, 1)
                        if k >= 1:
                            hi_of(e, k - 1)
                    hi_of(e, 4 * ns - 1)

                with act.Fori(0, FFE - 1) as e:
                    act.wait_ge(f2_ps, f2b + e * 2 * nt)
                    for j in range(4):
                        split_hi(c, G_FF + 1, j, e=e)
                    ff1(e)
                    for j in range(4):
                        split_hi(c, G_FF + 2, j, e=e)
                following = tiles(c + 1) if c + 1 < NC else []
                for i in range(len(following)):
                    norm_squares(c + 1, 0, i)
                act.wait_ge(f2_ps, f2b + (FFE - 1) * 2 * nt)
                split_hi_group(c, GROUPS - 1)
                ff1(FFE - 1)
                for i in range(len(following)):
                    norm_hi(c + 1, 0, i)
                    if i < 4:
                        split_hi(c + 1, 0, i)

        @block.vector
        def _(dve):
            def norm_scale(c, which, i):
                nb = norm_base(c, which)
                r = tiles(c)[i][1]
                if i == 0:
                    dve.wait_ge(grow_in, 16 * (2 * c + which + 1))
                dve.wait_ge(n_rstd, nb + i + 1)
                if which and i >= 2:
                    dve.wait_ge(n_tp, 2 * (nb + i - 1))
                src, dst = (resid[0:r, i, :], xn[0:r, i % 2, :]) if which else (xin[0:r, i, :], xin[0:r, i, :])
                nc.vector.scalar_tensor_tensor(out=dst, in0=src, scalar=rstd[0:r, i:i + 1], in1=g_row[0:r, :],
                                               op0=ALU.mult, op1=ALU.mult).then_inc(n_xn, 1)

            def norm_lo(c, which, i):
                q0, r = tiles(c)[i]
                for hf in range(2):
                    dve.wait_ge(n_hi, 2 * (norm_base(c, which) + i) + hf + 1)
                    nc.vector.tensor_tensor(hT_lo[:, 4 * hf:4 * hf + 4, q0:q0 + r],
                                            ps[:, (2 * i + hf) % 4, 0:4 * r].rearrange("p (a b) -> p a b", a=4),
                                            hT_hi[:, 4 * hf:4 * hf + 4, q0:q0 + r].bitcast(F32),
                                            ALU.subtract).then_inc(n_lo, 1)

            def convolve(c, xs):
                wd = CVW if c == NC - 1 else CHUNK
                for x in xs:
                    k, tap = taps_in_order[x]
                    if tap == 0:
                        nc.vector.tensor_scalar(cacc[:, k, 0:wd], uT[:, k, 0:wd], vecs[:, k, 0:1],
                                                vecs[:, k, CW:CW + 1], ALU.mult, ALU.add).then_inc(taps, 1)
                    else:
                        dve.wait_ge(taps, TAPS * c + taps_in_order.index((k, tap - 1)) + 1)
                        nc.vector.scalar_tensor_tensor(out=cacc[:, k, 0:wd], in0=uT[:, k, tap:tap + wd],
                                                       scalar=vecs[:, k, tap:tap + 1], in1=cacc[:, k, 0:wd],
                                                       op0=ALU.mult, op1=ALU.add).then_inc(taps, 1)

            dve.wait_ge(gains_in, 32)
            nc.vector.tensor_scalar(gq[:], gq[:], HD ** -0.5, None, ALU.mult).then_inc(hist_ok, 1)
            nc.vector.memset(uT[:, 0, 0:HIST], 0.0).then_inc(o_lo, 1)
            nc.vector.memset(uT[:, 1:CB, 0:HIST], 0.0).then_inc(hist_ok, 1)
            dve.wait_ge(ck_hi, 1)
            nc.vector.tensor_tensor(packed[:, 0, :, HD:P], kn[:, 0, :].rearrange("p (h d) -> p h d", h=NH),
                                    packed[:, 0, :, 0:HD].bitcast(F32), ALU.subtract).then_inc(ck_lo, 1)
            dve.wait_ge(cv_hi, 1)
            nc.vector.tensor_tensor(vpack[:, :, HD:P], vout[:, 0, :].rearrange("p (h d) -> p h d", h=NH),
                                    vpack[:, :, 0:HD].bitcast(F32), ALU.subtract).then_inc(cv_lo, 1)
            for c in range(NC):
                tl = tiles(c)
                nt = len(tl)
                sp_ = splits(c)
                ns = len(sp_)
                if c == 0:
                    for i in range(nt):
                        norm_scale(0, 0, i)
                    for i in range(nt):
                        norm_lo(0, 0, i)
                if c:
                    dve.wait_ge(taps, TAPS * c)
                    nc.vector.tensor_copy(uT[:, :, 0:HIST], uT[:, :, CHUNK:CHUNK + HIST]).then_inc(hist_ok, 1)
                dve.wait_ge(hist_ok, 2 + c)
                for m in range(CB):
                    for s, (s0, w) in enumerate(sp_):
                        u = 4 * c + m * ns + s
                        evv = 2 * m * ns + s
                        dve.wait_ge(ag_sig, u + 1)
                        cut = max(s0, min(s0 + w, CHUNK))
                        for n, (x0, x1) in enumerate([(s0, cut), (cut, s0 + w)]):
                            if x1 > x0:
                                d0 = x0 + HIST + (HIST if x0 >= CHUNK else 0)
                                ins = nc.vector.tensor_tensor(uT[:, m, d0:d0 + x1 - x0], ps[:, evv % 4, x0 - s0:x1 - s0],
                                                              sgate[:, u % 2, x0 - s0:x1 - s0], ALU.mult)
                        ins.then_inc(ag_u, 1)
                    if m < CB - 1:
                        if m == 0:
                            dve.wait_ge(vec_ok, 2)
                            dve.wait_ge(cache_out, 32)
                        dve.wait_ge(ag_u, 4 * c + (m + 1) * ns)
                        convolve(c, range(EARLY * m, EARLY * (m + 1)))
                evs = kvq_events(c)
                kq0 = 8 * c
                dve.wait_ge(ag_u, 4 * c + 4 * ns)
                for s in range(len(evs) + 1):
                    if s < len(evs):
                        sec, i, m = evs[s]
                        r = tl[i][1]
                        if m is not None:
                            u = kq0 + m
                            b = m % 2
                            dve.wait_ge(kq_sq, u + 1)
                            nc.vector.tensor_reduce(hss[0:r, b, :], sqr[0:r, :].rearrange("p (h d) -> p h d", h=NH),
                                                    axis=AX.X, op=ALU.add).then_inc(kq_ss, 1)
                    if s >= 1:
                        psec, pi, pm = evs[s - 1]
                        pr = tl[pi][1]
                        if pm is not None:
                            dve.wait_ge(pk_hi, kq0 + pm + 1)
                            nc.vector.tensor_tensor(packed[0:pr, pm % 2, :, HD:P],
                                                    kn[0:pr, pm % 2, :].rearrange("p (h d) -> p h d", h=NH),
                                                    packed[0:pr, pm % 2, :, 0:HD].bitcast(F32), ALU.subtract).then_inc(pk_lo, 1)
                        else:
                            dve.wait_ge(cv_hi, 4 * c + pi + 2)
                            nc.vector.tensor_tensor(vpack[0:pr, :, HD:P],
                                                    vout[0:pr, pi % 2, :].rearrange("p (h d) -> p h d", h=NH),
                                                    vpack[0:pr, :, 0:HD].bitcast(F32), ALU.subtract).then_inc(v_lo, 1)
                    if s < len(evs):
                        convolve(c, taps_of(c, s))
                        if m is not None:
                            dve.wait_ge(kq_rs, u + 1)
                            dve.wait_ge(kq_mul, u + 1)
                            if u >= 2:
                                dve.wait_ge(pk_lo, u - 1)
                            uses = (2 * c + i // 2) if sec == "k" else 2 * c + (nt + 1 - b) // 2
                            if uses:
                                dve.wait_ge(kn_out[b], 16 * uses)
                            dve.wait_ge(ck_lo, 1)
                            nc.vector.tensor_tensor(kn[0:r, b, :].rearrange("p (h d) -> p h d", h=NH),
                                                    raw_kq[0:r, b, :].rearrange("p (h d) -> p h d", h=NH),
                                                    hrs[0:r, b, :].unsqueeze(2).to_broadcast([r, NH, HD]),
                                                    ALU.mult).then_inc(kq_n, 1)
                dve.wait_ge(taps, TAPS * (c + 1))
                for n, (a, q0, w) in enumerate(conv_pieces(c)):
                    lb = c + n
                    dve.wait_ge(mean_ps, lb + 1)
                    for k in range(CB):
                        nc.vector.scalar_tensor_tensor(out=cacc[:, k, a:a + w], in0=ps[:, 2, 0:w], scalar=-1.0 / CC,
                                                       in1=cacc[:, k, a:a + w], op0=ALU.mult, op1=ALU.add).then_inc(xc_ok, 1)
                    dve.wait_ge(var_ps, lb + 1)
                    if n:
                        dve.wait_ge(lnr_ok, lb)
                    nc.vector.tensor_scalar(lnv[:, 0:w], ps[:, 3, 0:w], 1.0 / CC, EPS, ALU.mult, ALU.add).then_inc(var_ok, 1)
                    dve.wait_ge(sd_ok, lb + 1)
                    if n:
                        dve.wait_ge(cm_ok, CB * lb)
                    nc.vector.scalar_tensor_tensor(out=ntmp[:, 0:w], in0=lnr[:, 0:w], scalar=-0.5, in1=lnr[:, 0:w],
                                                   op0=ALU.mult, op1=ALU.mult).then_inc(nwt, 1)
                    dve.wait_ge(nwt, 2 * lb + 1)
                    nc.vector.tensor_tensor(ntmp[:, 0:w], ntmp[:, 0:w], lnv[:, 0:w], ALU.mult).then_inc(nwt, 1)
                    dve.wait_ge(nwt, 2 * lb + 2)
                    nc.vector.scalar_tensor_tensor(out=lnr[:, 0:w], in0=ntmp[:, 0:w], scalar=1.5, in1=lnr[:, 0:w],
                                                   op0=ALU.add, op1=ALU.mult).then_inc(lnr_ok, 1)
                    dve.wait_ge(lnr_ok, lb + 1)
                    dve.wait_ge(xc_ok, CB * (lb + 1))
                    for k in range(CB):
                        nc.vector.tensor_tensor(cacc[:, k, a:a + w], cacc[:, k, a:a + w], lnr[:, 0:w],
                                                ALU.mult).then_inc(yn_ok, 1)
                    for k in range(CB + 1):
                        if k < CB:
                            dve.wait_ge(sg_ok, CB * lb + k + 1)
                            dve.wait_ge(id_ok, CB * lb + k + 1)
                            nc.vector.tensor_tensor(cacc[:, k, a:a + w], csig[:, k % 2, 0:w], cid[:, k % 2, 0:w],
                                                    ALU.mult).then_inc(cm_ok, 1)
                        if k >= 1:
                            dve.wait_ge(c_hi, CB * lb + k)
                            nc.vector.tensor_tensor(cT_lo[:, k - 1, a:a + w], cacc[:, k - 1, a:a + w],
                                                    cT_hi[:, k - 1, a:a + w].bitcast(F32), ALU.subtract).then_inc(c_lo, 1)
                npc = len(conv_pieces(c))
                for m in range(CB):
                    for n, (a, q0, w) in enumerate(conv_pieces(c)):
                        ev = CB * c + npc * m + n
                        dve.wait_ge(pw_hi, ev + 1)
                        nc.vector.tensor_tensor(mixT_lo[:, m, q0:q0 + w], ps[:, (ev - CB * c) % 4, 0:w],
                                                mixT_hi[:, m, q0:q0 + w].bitcast(F32), ALU.subtract).then_inc(pw_lo, 1)
                dve.wait_ge(consts, 6)
                if c == NC - 1:
                    dve.wait_ge(cvo_out, 32)
                for kind, pairs in passes(c):
                    cnt = att_counter(c, kind)
                    seq = att_sequence(kind, pairs)
                    L = len(seq)

                    def mask(k, it):
                        q = seq[k]
                        if q.diag:
                            dve.wait_ge(z_ps, cnt("z", k + 1, it, 0))
                            v = bank(k, q.r, q.n - q.r, q.n)
                            nc.vector.tensor_tensor(v, v, limit[0:q.r, 0:q.r], ALU.min).then_inc(z_msk, 1)

                    def products(k, it, rel):
                        q = seq[k]
                        v, r, n = stay[k % 4], q.r, q.n
                        dve.wait_ge(s_sg, cnt("z", k + 1, it, rel))
                        init = 1.0
                        if not q.diag:
                            before_ = len(pairs[q.p])
                            dve.wait_ge(s_scan, cnt("z", k - before_ + 1, it, rel))
                            init = stay[(k - before_) % 4][0:r, 0:1]
                            edge = beta[k % 4][0:r, n - 1:n]
                            nc.vector.tensor_tensor(edge, edge, init, ALU.mult)
                        nc.vector.tensor_tensor_scan(v[0:r, 0:n][:, ::-1], v[0:r, 0:n][:, ::-1],
                                                     ones[0:r, 0:1].to_broadcast([r, n]), init,
                                                     ALU.mult, ALU.mult).then_inc(s_scan, 1)

                    def turned_lo(k, it, rel):
                        q = seq[k]
                        for gi, grp in enumerate(key_groups(q.a0, q.n)):
                            dve.wait_ge(t_hi, cnt("t", q.tg + gi + 1, it, rel))
                            evacuate(nc.vector.tensor_tensor, aT_hi, aT_lo, aT_blocks(q, grp), q.t, q.r,
                                     ps[:, 4 + (q.tg + gi) % 2, :], t_lo)

                    def output(k, it, rel):
                        q = seq[k]
                        if q.last and q.ends:
                            w = sum(x[1] for x in pairs[q.p])
                            col = CHUNK if kind else pairs[q.p][0][0]
                            me = slice(q.head % 2 * HD, q.head % 2 * HD + HD)
                            blk = CB + q.head // 2 if kind else it + (CB + rel)
                            dst = mixT_hi[me, blk, col:col + w]
                            o = q.ob + 1
                            dve.wait_ge(o_cp, cnt("o", o, it, rel))
                            nc.vector.tensor_tensor(of[me, 0:w], ps[me, 6 + q.ob % 2, 0:w], osb[me, 0:w], ALU.add).then_inc(o_sum, 1)
                            dve.wait_ge(o_sum, cnt("o", o, it, rel))
                            nc.vector.tensor_copy(dst, of[me, 0:w]).then_inc(o_hi, 1)
                            dve.wait_ge(o_hi, cnt("o", o, it, rel))
                            nc.vector.tensor_tensor(mixT_lo[me, blk, col:col + w], of[me, 0:w], dst.bitcast(F32),
                                                    ALU.subtract).then_inc(o_lo, 1)

                    def steps(it, ks, first=False):
                        for k in ks:
                            if k < L:
                                mask(k, it)
                            if who := behind(k, SCAN, L, first):
                                products(who[1], it, who[0])
                            if who := behind(k, TURN, L, first):
                                turned_lo(who[1], it, who[0])
                            if who := behind(k, OUTPUT, L, first):
                                output(who[1], it, who[0])

                    rounds = NH // round_heads(kind)
                    steps(0, range(L), first=True)
                    if rounds > 1:
                        with dve.Fori(1, rounds) as it:
                            steps(it, range(L))
                    steps(rounds - 1, range(L, L + OUTPUT))
                for hf in range(2):
                    for i, (q0, r) in enumerate(tl):
                        ev = hf * nt + i
                        if hf == 0:
                            dve.wait_ge(resid_in[i], 16 * ((c if i < 4 else 0) + 1))
                        dve.wait_ge(out_ps, 8 * c + ev + 1)
                        v = resid[0:r, i, hf * BANK:(hf + 1) * BANK]
                        nc.vector.tensor_tensor(v, ps[0:r, 4 + ev % 4, :], v, ALU.add).then_inc(out_add, 1)
                        if hf:
                            if i >= 1:
                                norm_lo(c, 1, i - 1)
                            norm_scale(c, 1, i)
                norm_lo(c, 1, nt - 1)
                f1b = 4 * FFE * c
                f2b = 8 * FFE * c

                def ff1(e):
                    for k in range(4 * ns + 1):
                        if k < 4 * ns:
                            w = sp_[k % ns][1]
                            dve.wait_ge(f_rel, f1b + k + 1 + e * 4 * ns)
                            if k >= 2:
                                dve.wait_ge(f_lo, f1b + k - 1 + e * 4 * ns)
                            nc.vector.tensor_tensor(fsq[:, k % 2, 0:w], frel[:, k % 2, 0:w], frel[:, k % 2, 0:w],
                                                    ALU.mult).then_inc(f_sq, 1)
                        if k >= 1:
                            j, s = (k - 1) // ns, (k - 1) % ns
                            s0, w = sp_[s]
                            dve.wait_ge(f_hi, f1b + k + e * 4 * ns)
                            nc.vector.tensor_tensor(hid_lo[:, j, s0:s0 + w], fsq[:, (k - 1) % 2, 0:w],
                                                    hid_hi[:, j, s0:s0 + w].bitcast(F32), ALU.subtract).then_inc(f_lo, 1)

                def ff2(e, ev):
                    i, hf = ev // 2, ev % 2
                    r = tl[i][1]
                    dve.wait_ge(f2_ps, f2b + ev + 2 + e * 2 * nt)
                    v = resid[0:r, i, hf * BANK:(hf + 1) * BANK]
                    nc.vector.tensor_tensor(v, ps[0:r, 4 + ev % 4, :], v, ALU.add).then_inc(f2_add, 1)

                with dve.Fori(0, FFE - 1) as e:
                    ff1(e)
                    for ev in range(2 * nt):
                        ff2(e, ev)
                following = len(tiles(c + 1)) if c + 1 < NC else 0
                for i in range(following):
                    norm_scale(c + 1, 0, i)
                ff1(FFE - 1)
                for i in range(max(nt, following)):
                    if i < nt:
                        ff2(FFE - 1, 2 * i)
                        ff2(FFE - 1, 2 * i + 1)
                    if i < following:
                        norm_lo(c + 1, 0, i)

        @block.tensor
        def _(pe):
            def mm3(out, w, x, start, stop):
                nc.tensor.matmul(out, w[0], x[0], start=start, stop=False)
                nc.tensor.matmul(out, w[0], x[1], start=False, stop=False)
                return nc.tensor.matmul(out, w[1], x[0], start=False, stop=stop)

            def slab(g, j):
                return w_hi[g % 2][:, j, :], w_lo[g % 2][:, j, :]

            def norm_turn(c, which, i):
                nb = norm_base(c, which)
                r = tiles(c)[i][1]
                src = xn[0:r, i % 2, :] if which else xin[0:r, i, :]
                pe.wait_ge(n_xn, nb + i + 1)
                for hf in range(2):
                    ev = 2 * i + hf
                    if ev >= 4:
                        pe.wait_ge(n_lo, 2 * nb + ev - 3)
                    for k in range(4):
                        blk = 4 * hf + k
                        ins = nc.tensor.transpose(ps[:, ev % 4, k * r:(k + 1) * r], src[:, blk * P:(blk + 1) * P],
                                                  ident[0:r, 0:r])
                    ins.then_inc(n_tp, 1)

            pe.wait_ge(consts, 4)
            pe.wait_ge(rows_in, 80)
            for k in range(CB):
                n = CW + 3
                ins = nc.tensor.transpose(ps[:, 4, k * n:(k + 1) * n], crow[:, k * P:(k + 1) * P], ident[0:n, 0:n])
            ins.then_inc(vec_t, 1)
            for k in range(CB):
                ins = nc.tensor.transpose(ps[:, 5, k * HIST:(k + 1) * HIST], srow[:, k * P:(k + 1) * P], ident[0:HIST, 0:HIST])
            ins.then_inc(vec_t, 1)
            pe.wait_ge(ck_lo, 1)
            for q in range(2):
                for k in range(4):
                    ins = nc.tensor.transpose(ps[:, 6 + q, k * P:(k + 1) * P], packed[:, 0, 4 * q + k, :].bitcast(F32), ident[:])
                    if (q, k) == (0, 0):
                        ins.then_inc(f2_ps, 1)
                ins.then_inc(ckT_ps, 1)
            for c in range(NC):
                tl = tiles(c)
                nt = len(tl)
                sp_ = splits(c)
                ns = len(sp_)
                if c == 0:
                    for i in range(nt):
                        norm_turn(0, 0, i)
                pe.wait_ge(n_lo, 2 * (norm_base(c, 0) + nt))
                if c == 0:
                    pe.wait_ge(vec_ok, 2)
                    pe.wait_ge(ckT_ok, 2)
                else:
                    pe.wait_ge(f_rel, 4 * FFE * c)
                for g in range(2):
                    for j in range(4):
                        n = 4 * (GROUPS * c + g) + j
                        pe.wait_ge(lo_done, n + 1)
                        wh, wl = slab(g, j)
                        for s, (s0, w) in enumerate(sp_):
                            ev = (4 * g + j) * ns + s
                            old = ev - 4
                            if old >= 0:
                                pe.wait_ge(ag_u, 4 * c + (old // (2 * ns)) * ns + old % ns + 1)
                            for k in range(KD):
                                ins = mm3(ps[:, ev % 4, 0:w], (wh[:, k * P:(k + 1) * P], wl[:, k * P:(k + 1) * P]),
                                          (hT_hi[:, k, s0:s0 + w], hT_lo[:, k, s0:s0 + w]), k == 0, k == KD - 1)
                            ins.then_inc(ag_ps, 1)
                evs = kvq_events(c)
                kq0 = 8 * c
                for s in range(len(evs) + 2):
                    if s < len(evs):
                        sec, i, m = evs[s]
                        g = {"k": G_K, "v": G_V, "q": G_Q}[sec]
                        q0, r = tl[i]
                        if s >= 4:
                            pe.wait_ge(kvq_cp, 12 * c + s - 3)
                        for k in range(KD):
                            if i == 0 and k % 2 == 0:
                                pe.wait_ge(lo_done, 4 * (GROUPS * c + g) + k // 2 + 1)
                            wh, wl = slab(g, k // 2)
                            c0 = (k % 2) * AW
                            nc.tensor.matmul(ps[0:r, 4 + s % 4, :], hT_hi[:, k, q0:q0 + r], wh[:, c0:c0 + AW], start=k == 0, stop=False)
                            nc.tensor.matmul(ps[0:r, 4 + s % 4, :], hT_lo[:, k, q0:q0 + r], wh[:, c0:c0 + AW], start=False, stop=False)
                            ins = nc.tensor.matmul(ps[0:r, 4 + s % 4, :], hT_hi[:, k, q0:q0 + r], wl[:, c0:c0 + AW],
                                                   start=False, stop=k == KD - 1)
                        ins.then_inc(kvq_ps, 1)
                    if s >= 2:
                        sec, i, m = evs[s - 2]
                        r = tl[i][1]
                        if sec != "v":
                            pe.wait_ge(pk_lo, kq0 + m + 1)
                            for q in range(2):
                                if m:
                                    pe.wait_ge(kqT_ok, 2 * (kq0 + m) + q - 1)
                                elif q == 0:
                                    pe.wait_ge(ag_u, 4 * c + 4 * ns)
                                for k in range(4):
                                    ins = nc.tensor.transpose(ps[:, q, k * r:(k + 1) * r],
                                                              packed[0:r, m % 2, 4 * q + k, :].bitcast(F32), ident[0:r, 0:r])
                                ins.then_inc(kqT_ps, 1)
                if c == NC - 1:
                    for q, col in enumerate((CHUNK, SMP + DEC)):
                        pe.wait_ge(kvq_cp, 12 * c + len(evs))
                        for k in range(CB):
                            ins = nc.tensor.transpose(ps[0:HIST, 4 + q, k * P:(k + 1) * P], uT[:, k, col:col + HIST], ident[:])
                        ins.then_inc(cvo_ps, 1)
                for n, (a, q0, w) in enumerate(conv_pieces(c)):
                    lb = c + n
                    if n:
                        pe.wait_ge(xc_ok, CB * lb)
                    for k in range(CB):
                        pe.wait_ge(taps, TAPS * c + taps_in_order.index((k, CW - 1)) + 1)
                        ins = nc.tensor.matmul(ps[:, 2, 0:w], ones[:], cacc[:, k, a:a + w], start=k == 0, stop=k == CB - 1)
                    ins.then_inc(mean_ps, 1)
                    if n:
                        pe.wait_ge(var_ok, lb)
                    for k in range(CB):
                        pe.wait_ge(sq_ok, CB * lb + k + 1)
                        ins = nc.tensor.matmul(ps[:, 3, 0:w], ones[:], csq[:, k, a:a + w], start=k == 0, stop=k == CB - 1)
                    ins.then_inc(var_ps, 1)
                npc = len(conv_pieces(c))
                pe.wait_ge(kqT_ok, 2 * (kq0 + 2 * nt))
                for m in range(CB):
                    for n, (a, q0, w) in enumerate(conv_pieces(c)):
                        ev = npc * m + n
                        if ev >= 4:
                            pe.wait_ge(pw_lo, CB * c + ev - 3)
                        for k in range(CB):
                            if m == 0:
                                pe.wait_ge(c_lo, CB * (c + n) + k + 1)
                            if m == 0 and n == 0:
                                pe.wait_ge(lo_done, 4 * (GROUPS * c + G_PW) + k + 1)
                            wh, wl = slab(G_PW, k)
                            ins = mm3(ps[:, ev % 4, 0:w], (wh[:, m * P:(m + 1) * P], wl[:, m * P:(m + 1) * P]),
                                      (cT_hi[:, k, a:a + w], cT_lo[:, k, a:a + w]), k == 0, k == CB - 1)
                        ins.then_inc(pw_ps, 1)
                pe.wait_ge(pw_lo, CB * (c + npc))
                if c == NC - 1:
                    pe.wait_ge(cvo_ok, 2)
                for kind, pairs in passes(c):
                    cnt = att_counter(c, kind)
                    seq = att_sequence(kind, pairs)
                    L = len(seq)
                    parts = 16 * 4
                    kq_before = parts * (NH // 2) * (c + kind)
                    v_before = 16 * (NH // 2) * (c + kind)

                    def scores(k, it, first):
                        q = seq[k]
                        slot, q0, k0 = (0, q.head * DEC, q.head * (PAST + DEC)) if kind else (q.head, q.q0, q.a0)
                        if k == 0 or (not kind and seq[k - 1].head != q.head):
                            pe.wait_ge(kq_in[slot], it * parts + (kq_before + parts))
                        if old := behind(k, 2, L, first):
                            pe.wait_ge(s_sg, cnt("z", old[1] + 1, it, old[0]))
                        for x in range(0, q.n, BANK):
                            w = min(BANK, q.n - x)
                            for v in range(2):
                                ins = nc.tensor.matmul(ps[0:q.r, 2 * (k % 2) + x // BANK, 0:w], a_q[slot][:, v, q0:q0 + q.r],
                                                       a_k[slot][:, k0 + x:k0 + x + w], start=v == 0, stop=v == 1)
                        ins.then_inc(z_ps, 1)

                    def turn(k, it, rel, first):
                        q = seq[k]
                        pe.wait_ge(s_a, cnt("z", k + 1, it, rel))
                        for gi, grp in enumerate(key_groups(q.a0, q.n)):
                            if not (first and q.tg + gi < 2):
                                pe.wait_ge(t_lo, cnt("t", q.tg + gi - 1, it, rel))
                            for x, (blk, w) in enumerate(grp):
                                s0 = blk * P - q.a0
                                ins = nc.tensor.transpose(ps[0:w, 4 + (q.tg + gi) % 2, x * q.r:(x + 1) * q.r],
                                                          beta[k % 4][0:q.r, s0:s0 + w], ident[0:q.r, 0:q.r])
                            ins.then_inc(t_ps, 1)

                    def values(k, it, rel, first):
                        q = seq[k]
                        if not q.ends:
                            return
                        pair = pairs[q.p]
                        slot, v0 = (0, q.head * 2) if kind else (q.head, 0)
                        if q.v % ((seq[-1].v + 1) // (1 if kind else 2)) == 0:
                            pe.wait_ge(v_in[slot], it * 16 + (rel * 16 + v_before + (16 * 2 if kind else 16)))
                        pe.wait_ge(t_lo, cnt("t", turned(q), it, rel))
                        if q.diag:
                            back = -1 if not first or q.ob else 0
                            pe.wait_ge(o_lo, cnt("o", q.ob + 1 + back, it, rel))
                        blocks = [b for grp in key_groups(q.a0, q.n) for b in grp]
                        width = sum(x[1] for x in pair)
                        for blk, w in blocks:
                            c0 = P * sum(x[2] <= blk * P for x in pair)
                            (own, _w), = aT_blocks(q, [(blk, w)])
                            for v, src in enumerate((aT_hi, aT_lo)):
                                ins = nc.tensor.matmul(ps[:, 6 + q.ob % 2, c0:width], a_v[slot][0:w, v0 + blk, :],
                                                       src[0:w, own, c0:width], start=q.diag and (blk, v) == (blocks[0][0], 0),
                                                       stop=q.last and (blk, v) == (blocks[-1][0], 1))
                        ins.then_inc(v_ps, 1)

                    def steps(it, ks, first=False):
                        for k in ks:
                            if k < L:
                                scores(k, it, first)
                            if who := behind(k, TURN, L, first):
                                turn(who[1], it, who[0], first)
                            if who := behind(k, VALUES, L, first):
                                values(who[1], it, who[0], first)

                    rounds = NH // round_heads(kind)
                    steps(0, range(L), first=True)
                    if rounds > 1:
                        with pe.Fori(1, rounds) as it:
                            steps(it, range(L))
                    steps(rounds - 1, range(L, L + VALUES), first=rounds == 1)
                pe.wait_ge(o_lo, att_outputs(c) + 1)
                for hf in range(2):
                    g = G_OUT + hf
                    for i, (q0, r) in enumerate(tl):
                        ev = hf * nt + i
                        if ev >= 4:
                            pe.wait_ge(out_add, 8 * c + ev - 3)
                        for k in range(KD):
                            if i == 0 and k % 2 == 0:
                                pe.wait_ge(lo_done, 4 * (GROUPS * c + g) + k // 2 + 1)
                            wh, wl = slab(g, k // 2)
                            c0 = (k % 2) * BANK
                            nc.tensor.matmul(ps[0:r, 4 + ev % 4, :], mixT_hi[:, k, q0:q0 + r], wh[:, c0:c0 + BANK], start=k == 0, stop=False)
                            nc.tensor.matmul(ps[0:r, 4 + ev % 4, :], mixT_lo[:, k, q0:q0 + r], wh[:, c0:c0 + BANK], start=False, stop=False)
                            ins = nc.tensor.matmul(ps[0:r, 4 + ev % 4, :], mixT_hi[:, k, q0:q0 + r], wl[:, c0:c0 + BANK],
                                                   start=False, stop=k == KD - 1)
                        ins.then_inc(out_ps, 1)
                        if hf and i:
                            norm_turn(c, 1, i - 1)
                norm_turn(c, 1, nt - 1)
                pe.wait_ge(n_lo, 2 * (norm_base(c, 1) + nt))
                f1b = 4 * FFE * c
                f2b = 8 * FFE * c

                def ff1(e):
                    for j in range(4):
                        pe.wait_ge(lo_done, 4 * (GROUPS * c + G_FF) + 8 * e + j + 1)
                        wh, wl = slab(G_FF, j)
                        for s, (s0, w) in enumerate(sp_):
                            ev = j * ns + s
                            if ev >= 4:
                                pe.wait_ge(f_rel, f1b + ev - 3 + e * 4 * ns)
                            for k in range(KD):
                                ins = mm3(ps[:, ev % 4, 0:w], (wh[:, k * P:(k + 1) * P], wl[:, k * P:(k + 1) * P]),
                                          (hT_hi[:, k, s0:s0 + w], hT_lo[:, k, s0:s0 + w]), k == 0, k == KD - 1)
                            ins.then_inc(f1_ps, 1)

                def ff2(e, ev):
                    i, hf = ev // 2, ev % 2
                    q0, r = tl[i]
                    if ev >= 4:
                        pe.wait_ge(f2_add, f2b + ev - 3 + e * 2 * nt)
                    for k in range(4):
                        if ev == 0:
                            pe.wait_ge(f_lo, f1b + (k + 1) * ns + e * 4 * ns)
                            pe.wait_ge(lo_done, 4 * (GROUPS * c + G_FF + 1) + 8 * e + k + 1)
                        wh, wl = slab(G_FF + 1, k)
                        o = ps[0:r, 4 + ev % 4, :]
                        c0 = hf * BANK
                        nc.tensor.matmul(o, hid_hi[:, k, q0:q0 + r], wh[:, c0:c0 + BANK], start=k == 0, stop=False)
                        nc.tensor.matmul(o, hid_lo[:, k, q0:q0 + r], wh[:, c0:c0 + BANK], start=False, stop=False)
                        ins = nc.tensor.matmul(o, hid_hi[:, k, q0:q0 + r], wl[:, c0:c0 + BANK], start=False, stop=k == 3)
                    ins.then_inc(f2_ps, 1)

                with pe.Fori(0, FFE - 1) as e:
                    ff1(e)
                    for ev in range(2 * nt):
                        ff2(e, ev)
                ff1(FFE - 1)
                following = len(tiles(c + 1)) if c + 1 < NC else 0
                for i in range(max(nt, following)):
                    if i < nt:
                        ff2(FFE - 1, 2 * i)
                        ff2(FFE - 1, 2 * i + 1)
                    if i < following:
                        if i == 0:
                            pe.wait_ge(f_rel, 4 * FFE * (c + 1))
                        norm_turn(c + 1, 0, i)


_INS = ["x_prompt", "x_sample", "cache_k", "cache_v", "state_conv", "g_mix", "w_in", "w_dw", "b_dw", "g_cn", "b_cn",
        "w_pw", "g_q", "g_k", "w_out", "g_ff", "w_ff1", "w_ff2"]
_OUTS = [(1, SEQ, D), (1, DEC, D), (1, 1, SEQ, NH, HD), (1, 1, SEQ, NH, HD), (1, 1, HIST, CC),
         (1, 1, DEC, NH, HD), (1, 1, DEC, NH, HD), (1, 1, HIST, CC)]


def kernel(**inputs):
    import numpy as np
    import concourse.bacc as bacc
    from concourse.bass_utils import run_bass_kernel_spmd

    nc = bacc.Bacc("TRN2", target_bir_lowering=False, num_devices=1)
    arrays, args = {}, []
    for name in _INS:
        a = np.ascontiguousarray(inputs[name])
        arrays[f"in_{name}"] = a
        args.append(nc.dram_tensor(f"in_{name}", a.shape, mybir.dt.from_np(a.dtype), kind="ExternalInput").ap())
    for i, shape in enumerate(_OUTS):
        args.append(nc.dram_tensor(f"out_{i}", shape, F32, kind="ExternalOutput").ap())
    build(nc, *args)
    r = run_bass_kernel_spmd(nc, [arrays], core_ids=[0])
    return tuple(r.results[0][f"out_{i}"] for i in range(len(_OUTS)))
```
